# Optimizing a Trainium2 kernel written in Bass

```python
import jax, jax.numpy as jnp
from jax import lax
import numpy as np

D_MODEL = 1024
BATCH = 1
SEQ = 256
DEPTH = 2

GRID_W = 64
CTX_LEN = 256
NORM_EPS = 1e-6

MLA_HEADS = 8
Q_LORA = 384
KV_LORA = 256
QK_NOPE = 64
QK_ROPE = 32
V_HEAD = 64
ROPE_THETA = 10000.0
MLA_SCALE = (QK_NOPE + QK_ROPE) ** -0.5
Q_BLOCK = 128
MLA_WIDTH = MLA_HEADS * V_HEAD
MLA_SPLITS = (Q_LORA, KV_LORA, QK_ROPE)
MLA_IN = Q_LORA + KV_LORA + QK_ROPE

POOL_WINDOWS = (2, 4, 8, 16)
POOL_GROUPS = 4
POOL_CH = 64
POOL_WIDTH = POOL_GROUPS * POOL_CH

RWKV_HEADS = 4
RWKV_HEAD = 64
RWKV_WIDTH = RWKV_HEADS * RWKV_HEAD
DECAY_LORA = 32
ICLR_LORA = 32
GATE_LORA = 64
RWKV_GN_EPS = 64e-5
RWKV_SPLITS = (RWKV_WIDTH, RWKV_WIDTH, RWKV_WIDTH, DECAY_LORA, DECAY_LORA, ICLR_LORA, ICLR_LORA, GATE_LORA)
RWKV_IN = 3 * RWKV_WIDTH + 2 * DECAY_LORA + 2 * ICLR_LORA + GATE_LORA

MIX_WIDTH = MLA_WIDTH + POOL_WIDTH + RWKV_WIDTH
IN_WIDTH = MLA_IN + POOL_WIDTH + RWKV_IN

N_EXPERTS = 64
TOP_K = 6
EXPERT_FF = 256
SHARED_FF = 256
N_GROUPS = 8
TOPK_GROUPS = 4
ROUTED_SCALE = 2.5
MOE_BLOCK = 128

kernel_name = 'hybrid_mla_pool_rwkv7_moe_dit'

def _split(z, sizes):
    out, o = [], 0
    for s in sizes:
        out.append(z[..., o:o + s])
        o += s
    return out

def rmsnorm(x, g):
    xf = x.astype(jnp.float32)
    y = xf * lax.rsqrt(jnp.mean(xf * xf, -1, keepdims=True) + NORM_EPS)
    return (y * g.astype(jnp.float32)).astype(x.dtype)

def modulate(h, shift, scale):
    return h * (1 + scale) + shift

def axial_rope_tables(n_tokens):
    rows = n_tokens // GRID_W
    row = jnp.repeat(jnp.arange(rows, dtype=jnp.float32), GRID_W)
    col = jnp.tile(jnp.arange(GRID_W, dtype=jnp.float32), rows)
    n_freq = QK_ROPE // 4
    inv = ROPE_THETA ** (-jnp.arange(n_freq, dtype=jnp.float32) / n_freq)
    ang = jnp.concatenate([row[:, None] * inv, col[:, None] * inv], -1)
    return jnp.cos(ang), jnp.sin(ang)

def apply_rope(x, cos, sin):
    half = x.shape[-1] // 2
    x1, x2 = x[..., :half], x[..., half:]
    return jnp.concatenate([x1 * cos - x2 * sin, x2 * cos + x1 * sin], -1).astype(x.dtype)

def mla_keys(z, p, cos, sin, rotate):
    B, L, _ = z.shape
    _, kv_a, k_pe = _split(z, MLA_SPLITS)
    kv = (rmsnorm(kv_a, p['mla_kv_norm']) @ p['mla_w_kv_b']).reshape(B, L, MLA_HEADS, QK_NOPE + V_HEAD)
    if rotate:
        k_pe = apply_rope(k_pe, cos[None], sin[None])
    return kv[..., :QK_NOPE], k_pe, kv[..., QK_NOPE:]

def mla_queries(z, p, cos, sin, rotate):
    B, L, _ = z.shape
    q = (rmsnorm(z[..., :Q_LORA], p['mla_q_norm']) @ p['mla_w_q_b']).reshape(B, L, MLA_HEADS, QK_NOPE + QK_ROPE)
    q_pe = q[..., QK_NOPE:]
    if rotate:
        q_pe = apply_rope(q_pe, cos[None, :, None, :], sin[None, :, None, :])
    return q[..., :QK_NOPE], q_pe

def mla_attend(q_nope, q_pe, k_nope, k_pe, v):
    s = jnp.einsum('bqhd,bkhd->bhqk', q_nope, k_nope) + jnp.einsum('bqhr,bkr->bhqk', q_pe, k_pe)
    pr = jax.nn.softmax(s.astype(jnp.float32) * MLA_SCALE, axis=-1).astype(v.dtype)
    return jnp.einsum('bhqk,bkhd->bqhd', pr, v)

def mla_mixer(z_lat, z_ctx, p, cos, sin, need_ctx):
    B, L, _ = z_lat.shape
    kn, kp, v = mla_keys(z_lat, p, cos, sin, True)
    ckn, ckp, cv = mla_keys(z_ctx, p, None, None, False)
    keys_nope = jnp.concatenate([kn, ckn], 1)
    keys_pe = jnp.concatenate([kp, ckp], 1)
    vals = jnp.concatenate([v, cv], 1)
    qn, qp = mla_queries(z_lat, p, cos, sin, True)
    n_blk = L // Q_BLOCK
    to_blocks = lambda t: jnp.moveaxis(t.reshape(B, n_blk, Q_BLOCK, *t.shape[2:]), 1, 0)
    out = lax.map(lambda qb: mla_attend(qb[0], qb[1], keys_nope, keys_pe, vals), (to_blocks(qn), to_blocks(qp)))
    y_lat = jnp.moveaxis(out, 0, 1).reshape(B, L, MLA_WIDTH)
    y_ctx = None
    if need_ctx:
        cqn, cqp = mla_queries(z_ctx, p, None, None, False)
        y_ctx = mla_attend(cqn, cqp, ckn, ckp, cv).reshape(B, z_ctx.shape[1], MLA_WIDTH)
    return y_lat, y_ctx

def pool_mixer(z, pool_w, pool_scale):
    B, L, _ = z.shape
    zf = z.astype(jnp.float32)
    csum = jnp.concatenate([jnp.zeros((B, 1, POOL_WIDTH), jnp.float32), jnp.cumsum(zf, axis=1)], axis=1)
    csum = csum.reshape(B, L + 1, POOL_GROUPS, POOL_CH)
    t = jnp.arange(L)[:, None]
    half = jnp.array(POOL_WINDOWS, jnp.int32)[None, :] // 2
    lo = jnp.clip(t - half, 0, L)
    hi = jnp.clip(t + half, 0, L)
    grp = jnp.arange(POOL_GROUPS)[None, :]
    total = csum[:, hi, grp] - csum[:, lo, grp]
    count = (hi - lo).astype(jnp.float32)[None, :, :, None]
    diff = total / count - zf.reshape(B, L, POOL_GROUPS, POOL_CH)
    y = jnp.einsum('blgc,gcd->blgd', diff.astype(z.dtype), pool_w)
    return y.reshape(B, L, POOL_WIDTH) * pool_scale

def token_shift(z, mu):
    zp = jnp.pad(z, ((0, 0), (1, 1), (0, 0)))
    return z + mu * (0.5 * (zp[:, :-2] + zp[:, 2:]) - z)

def rwkv_prepare(z, p):
    B, L, _ = z.shape
    z = token_shift(z, p['rwkv_mu'])
    r, k, v, w_f, w_b, a_f, a_b, g_in = _split(z, RWKV_SPLITS)
    g = jax.nn.sigmoid(g_in) @ p['rwkv_g2']
    heads = lambda t: t.astype(jnp.float32).reshape(B, L, RWKV_HEADS, RWKV_HEAD)
    kk = heads(k * p['rwkv_k_k'])
    kk = kk / jnp.maximum(jnp.sqrt(jnp.sum(kk * kk, -1, keepdims=True)), 1e-12)
    dirs = []
    for d, (w_lo, a_lo) in enumerate(((w_f, a_f), (w_b, a_b))):
        log_w = -jax.nn.softplus(-(p['rwkv_w0'][d] + jnp.tanh(w_lo) @ p['rwkv_w2'][d])) - 0.5
        decay = jnp.exp(-jnp.exp(log_w.astype(jnp.float32)))
        a = jax.nn.sigmoid(p['rwkv_a0'][d] + a_lo @ p['rwkv_a2'][d])
        k_d = k * (1 + (a - 1) * p['rwkv_k_a'])
        dirs.append((heads(decay), kk * heads(a), heads(k_d)))
    return heads(r), kk, heads(v), g, dirs

def wkv_scan(state0, r, kk, v, decay, b, k, reverse):
    def step(S, inp):
        r_t, kk_t, v_t, w_t, b_t, k_t = inp
        sa = jnp.einsum('bhvk,bhk->bhv', S, kk_t)
        S = S * w_t[:, :, None, :] - sa[..., None] * b_t[:, :, None, :] + v_t[..., None] * k_t[:, :, None, :]
        return S, jnp.einsum('bhvk,bhk->bhv', S, r_t)
    xs = tuple(jnp.moveaxis(t, 1, 0) for t in (r, kk, v, decay, b, k))
    S, ys = lax.scan(step, state0, xs, reverse=reverse)
    return S, jnp.moveaxis(ys, 0, 1)

def rwkv_readout(y, prep, p):
    r, _, v, g, dirs = prep
    B, L = y.shape[:2]
    mean = jnp.mean(y, -1, keepdims=True)
    var = jnp.mean(jnp.square(y - mean), -1, keepdims=True)
    ln_w = p['rwkv_ln_w'].astype(jnp.float32).reshape(RWKV_HEADS, RWKV_HEAD)
    ln_b = p['rwkv_ln_b'].astype(jnp.float32).reshape(RWKV_HEADS, RWKV_HEAD)
    r_k = p['rwkv_r_k'].astype(jnp.float32)
    yn = (y - mean) * lax.rsqrt(var + RWKV_GN_EPS) * ln_w + ln_b
    bonus = sum(jnp.sum(r * k_d * r_k, -1, keepdims=True) for _, _, k_d in dirs) * v
    return (yn + bonus).reshape(B, L, RWKV_WIDTH).astype(g.dtype) * g

def rwkv_mixer(z_lat, z_ctx, p, need_ctx):
    lat = rwkv_prepare(z_lat, p)
    cx = rwkv_prepare(z_ctx, p)
    s0 = jnp.zeros((z_ctx.shape[0], RWKV_HEADS, RWKV_HEAD, RWKV_HEAD), jnp.float32)
    y_lat, y_ctx = 0.0, 0.0
    for d in range(2):
        reverse = d == 1
        s_ctx, yc = wkv_scan(s0, cx[0], cx[1], cx[2], *cx[4][d], reverse)
        _, yl = wkv_scan(s_ctx, lat[0], lat[1], lat[2], *lat[4][d], reverse)
        y_lat = y_lat + yl
        y_ctx = y_ctx + yc
    out_ctx = rwkv_readout(y_ctx, cx, p) if need_ctx else None
    return rwkv_readout(y_lat, lat, p), out_ctx

def swiglu(h, w_gate, w_up, w_down):
    return (jax.nn.silu(h @ w_gate) * (h @ w_up)) @ w_down

def moe_ffn(h, p):
    T, D = h.shape
    scores = jax.nn.sigmoid((h @ p['router_w']).astype(jnp.float32))
    sel = scores + p['router_bias'].astype(jnp.float32)
    per_group = N_EXPERTS // N_GROUPS
    group_score = lax.top_k(sel.reshape(T, N_GROUPS, per_group), 2)[0].sum(-1)
    _, group_idx = lax.top_k(group_score, TOPK_GROUPS)
    group_mask = jax.nn.one_hot(group_idx, N_GROUPS, dtype=jnp.float32).sum(1)
    expert_mask = jnp.repeat(group_mask, per_group, axis=1) > 0
    _, expert_idx = lax.top_k(jnp.where(expert_mask, sel, -jnp.inf), TOP_K)
    gate = jnp.take_along_axis(scores, expert_idx, axis=1)
    gate = gate / jnp.sum(gate, -1, keepdims=True) * ROUTED_SCALE

    n_assign = T * TOP_K
    n_slots = -(-(n_assign + N_EXPERTS * (MOE_BLOCK - 1)) // MOE_BLOCK) * MOE_BLOCK
    n_blocks = n_slots // MOE_BLOCK
    flat_e = expert_idx.reshape(-1)
    flat_tok = jnp.repeat(jnp.arange(T, dtype=jnp.int32), TOP_K)
    flat_gate = gate.reshape(-1)
    order = jnp.argsort(flat_e)
    sorted_e = flat_e[order]
    counts = jnp.bincount(flat_e, length=N_EXPERTS)
    starts = jnp.cumsum(counts) - counts
    padded = (counts + MOE_BLOCK - 1) // MOE_BLOCK * MOE_BLOCK
    padded_ends = jnp.cumsum(padded)
    padded_starts = padded_ends - padded
    dest = padded_starts[sorted_e] + jnp.arange(n_assign, dtype=jnp.int32) - starts[sorted_e]
    slot_tok = jnp.full((n_slots,), T, jnp.int32).at[dest].set(flat_tok[order])
    slot_gate = jnp.zeros((n_slots,), jnp.float32).at[dest].set(flat_gate[order])
    block_expert = jnp.minimum(jnp.searchsorted(padded_ends, jnp.arange(n_blocks, dtype=jnp.int32) * MOE_BLOCK, side='right'), N_EXPERTS - 1)
    h_pad = jnp.concatenate([h, jnp.zeros((1, D), h.dtype)], 0)

    def expert_block(acc, blk):
        tok, g, e = blk
        yb = swiglu(h_pad[tok], p['exp_w_gate'][e], p['exp_w_up'][e], p['exp_w_down'][e])
        return acc.at[tok].add(yb.astype(jnp.float32) * g[:, None]), None

    acc, _ = lax.scan(expert_block, jnp.zeros((T + 1, D), jnp.float32),
                      (slot_tok.reshape(n_blocks, MOE_BLOCK), slot_gate.reshape(n_blocks, MOE_BLOCK), block_expert))
    shared = swiglu(h, p['sh_w_gate'], p['sh_w_up'], p['sh_w_down'])
    return (acc[:T] + shared.astype(jnp.float32)).astype(h.dtype)

def trunk_layer(x, ctx, mod, mod_ctx, p, cos, sin, is_last):
    B, L, D = x.shape
    need_ctx = not is_last
    sh1, sc1, gt1, sh2, sc2, gt2 = jnp.split(mod[:, None, :], 6, axis=-1)
    csh1, csc1, cgt1, csh2, csc2, cgt2 = jnp.split(mod_ctx[None, None, :], 6, axis=-1)

    z_lat = modulate(rmsnorm(x, p['pre_mix_g']), sh1, sc1) @ p['w_in']
    z_ctx = modulate(rmsnorm(ctx, p['pre_mix_g']), csh1, csc1) @ p['w_in']
    m_lat, pl_lat, r_lat = _split(z_lat, (MLA_IN, POOL_WIDTH, RWKV_IN))
    m_ctx, pl_ctx, r_ctx = _split(z_ctx, (MLA_IN, POOL_WIDTH, RWKV_IN))
    a_lat, a_ctx = mla_mixer(m_lat, m_ctx, p, cos, sin, need_ctx)
    w_lat, w_ctx = rwkv_mixer(r_lat, r_ctx, p, need_ctx)
    y = jnp.concatenate([a_lat, pool_mixer(pl_lat, p['pool_w'], p['pool_scale']), w_lat], -1) @ p['w_out']
    x = x + gt1 * rmsnorm(y, p['post_mix_g'])

    if is_last:
        h = modulate(rmsnorm(x, p['pre_ffn_g']), sh2, sc2)
        f = moe_ffn(h.reshape(B * L, D), p).reshape(B, L, D)
        return x + gt2 * rmsnorm(f, p['post_ffn_g']), None

    yc = jnp.concatenate([a_ctx, pool_mixer(pl_ctx, p['pool_w'], p['pool_scale']), w_ctx], -1) @ p['w_out']
    ctx = ctx + cgt1 * rmsnorm(yc, p['post_mix_g'])

    h = modulate(rmsnorm(x, p['pre_ffn_g']), sh2, sc2)
    hc = modulate(rmsnorm(ctx, p['pre_ffn_g']), csh2, csc2)
    f = moe_ffn(jnp.concatenate([h.reshape(B * L, D), hc.reshape(-1, D)], 0), p)
    x = x + gt2 * rmsnorm(f[:B * L].reshape(B, L, D), p['post_ffn_g'])
    ctx = ctx + cgt2 * rmsnorm(f[B * L:].reshape(ctx.shape), p['post_ffn_g'])
    return x, ctx

def setup_inputs(seed: int = 0) -> dict:
    key = jax.random.key(seed)
    ks = iter(jax.random.split(key, 48))
    nrm = lambda shape, scale: jax.random.normal(next(ks), shape, jnp.float32) * scale
    D = D_MODEL
    return {
        'x': nrm((BATCH, SEQ, D), 1.0),
        'c': nrm((BATCH, D), 1.0),
        'ctx': nrm((BATCH, CTX_LEN, D), 1.0),
        'c_ctx': nrm((D,), 1.0),
        'ada_w': nrm((DEPTH, D, 6 * D), 0.5 * D ** -0.5),
        'ada_b': nrm((DEPTH, 6 * D), 0.02),
        'pre_mix_g': 1.0 + nrm((DEPTH, D), 0.05),
        'post_mix_g': 1.0 + nrm((DEPTH, D), 0.05),
        'pre_ffn_g': 1.0 + nrm((DEPTH, D), 0.05),
        'post_ffn_g': 1.0 + nrm((DEPTH, D), 0.05),
        'w_in': nrm((DEPTH, D, IN_WIDTH), D ** -0.5),
        'w_out': nrm((DEPTH, MIX_WIDTH, D), MIX_WIDTH ** -0.5),
        'mla_q_norm': 1.0 + nrm((DEPTH, Q_LORA), 0.05),
        'mla_w_q_b': nrm((DEPTH, Q_LORA, MLA_HEADS * (QK_NOPE + QK_ROPE)), Q_LORA ** -0.5),
        'mla_kv_norm': 1.0 + nrm((DEPTH, KV_LORA), 0.05),
        'mla_w_kv_b': nrm((DEPTH, KV_LORA, MLA_HEADS * (QK_NOPE + V_HEAD)), KV_LORA ** -0.5),
        'pool_w': nrm((DEPTH, POOL_GROUPS, POOL_CH, POOL_CH), POOL_CH ** -0.5),
        'pool_scale': 1.0 + nrm((DEPTH, POOL_WIDTH), 0.1),
        'rwkv_mu': jax.random.uniform(next(ks), (DEPTH, RWKV_IN), jnp.float32),
        'rwkv_w0': -2.0 + nrm((DEPTH, 2, RWKV_WIDTH), 1.0),
        'rwkv_w2': nrm((DEPTH, 2, DECAY_LORA, RWKV_WIDTH), 0.5 * DECAY_LORA ** -0.5),
        'rwkv_a0': nrm((DEPTH, 2, RWKV_WIDTH), 0.5),
        'rwkv_a2': nrm((DEPTH, 2, ICLR_LORA, RWKV_WIDTH), ICLR_LORA ** -0.5),
        'rwkv_g2': nrm((DEPTH, GATE_LORA, RWKV_WIDTH), GATE_LORA ** -0.5),
        'rwkv_k_k': 0.85 + nrm((DEPTH, RWKV_WIDTH), 0.05),
        'rwkv_k_a': 1.0 + nrm((DEPTH, RWKV_WIDTH), 0.05),
        'rwkv_r_k': nrm((DEPTH, RWKV_HEADS, RWKV_HEAD), 0.1),
        'rwkv_ln_w': 1.0 + nrm((DEPTH, RWKV_WIDTH), 0.05),
        'rwkv_ln_b': nrm((DEPTH, RWKV_WIDTH), 0.02),
        'router_w': nrm((DEPTH, D, N_EXPERTS), D ** -0.5),
        'router_bias': nrm((DEPTH, N_EXPERTS), 0.01),
        'exp_w_gate': nrm((DEPTH, N_EXPERTS, D, EXPERT_FF), D ** -0.5),
        'exp_w_up': nrm((DEPTH, N_EXPERTS, D, EXPERT_FF), D ** -0.5),
        'exp_w_down': nrm((DEPTH, N_EXPERTS, EXPERT_FF, D), EXPERT_FF ** -0.5),
        'sh_w_gate': nrm((DEPTH, D, SHARED_FF), D ** -0.5),
        'sh_w_up': nrm((DEPTH, D, SHARED_FF), D ** -0.5),
        'sh_w_down': nrm((DEPTH, SHARED_FF, D), SHARED_FF ** -0.5),
    }

def reference(x, c, ctx, c_ctx, ada_w, ada_b, pre_mix_g, post_mix_g, pre_ffn_g, post_ffn_g, w_in, w_out,
              mla_q_norm, mla_w_q_b, mla_kv_norm, mla_w_kv_b, pool_w, pool_scale,
              rwkv_mu, rwkv_w0, rwkv_w2, rwkv_a0, rwkv_a2, rwkv_g2, rwkv_k_k, rwkv_k_a, rwkv_r_k, rwkv_ln_w, rwkv_ln_b,
              router_w, router_bias, exp_w_gate, exp_w_up, exp_w_down, sh_w_gate, sh_w_up, sh_w_down):
    cos, sin = axial_rope_tables(x.shape[1])
    silu_c = jax.nn.silu(c)
    silu_cc = jax.nn.silu(c_ctx)
    for i in range(DEPTH):
        p = {
            'pre_mix_g': pre_mix_g[i], 'post_mix_g': post_mix_g[i], 'pre_ffn_g': pre_ffn_g[i], 'post_ffn_g': post_ffn_g[i],
            'w_in': w_in[i], 'w_out': w_out[i],
            'mla_q_norm': mla_q_norm[i], 'mla_w_q_b': mla_w_q_b[i], 'mla_kv_norm': mla_kv_norm[i], 'mla_w_kv_b': mla_w_kv_b[i],
            'pool_w': pool_w[i], 'pool_scale': pool_scale[i],
            'rwkv_mu': rwkv_mu[i], 'rwkv_w0': rwkv_w0[i], 'rwkv_w2': rwkv_w2[i], 'rwkv_a0': rwkv_a0[i], 'rwkv_a2': rwkv_a2[i],
            'rwkv_g2': rwkv_g2[i], 'rwkv_k_k': rwkv_k_k[i], 'rwkv_k_a': rwkv_k_a[i], 'rwkv_r_k': rwkv_r_k[i],
            'rwkv_ln_w': rwkv_ln_w[i], 'rwkv_ln_b': rwkv_ln_b[i],
            'router_w': router_w[i], 'router_bias': router_bias[i],
            'exp_w_gate': exp_w_gate[i], 'exp_w_up': exp_w_up[i], 'exp_w_down': exp_w_down[i],
            'sh_w_gate': sh_w_gate[i], 'sh_w_up': sh_w_up[i], 'sh_w_down': sh_w_down[i],
        }
        mod = silu_c @ ada_w[i] + ada_b[i]
        mod_ctx = silu_cc @ ada_w[i] + ada_b[i]
        x, ctx = trunk_layer(x, ctx, mod, mod_ctx, p, cos, sin, i == DEPTH - 1)
    return x


_drawn_inputs = setup_inputs


def setup_inputs(seed=0):
    import zlib

    import numpy as np

    out = dict(_drawn_inputs(seed))
    spreads = {}
    factors = {'mla_q_norm': 3.404, 'rwkv_ln_b': 3.157}
    for name, (base, spread) in spreads.items():
        noise = np.random.default_rng([zlib.crc32(name.encode()), seed]).standard_normal(out[name].shape)
        drawn = base * np.exp(spread * noise) if base else spread * noise
        out[name] = __import__('jax').numpy.asarray(drawn.astype(out[name].dtype))
    for name, factor in factors.items():
        out[name] = (out[name] * factor).astype(out[name].dtype)
    return out
```

```python
from contextlib import ExitStack

import numpy as np
import concourse.bass as bass
from concourse import mybir

ALU = mybir.AluOpType
ACT = mybir.ActivationFunctionType
AX = mybir.AxisListType
F32 = mybir.dt.float32
BF16 = mybir.dt.bfloat16
I32 = mybir.dt.int32
U32 = mybir.dt.uint32

P = 128
D = 1024
KD = D // P
SEQ, CTX = 256, 256
NT = (SEQ + CTX) // P
NL = SEQ // P
DEPTH = 2
GRID_W = 64
EPS = 1e-6
H, NOPE, ROPE, VH = 8, 64, 32, 64
QK = NOPE + ROPE
QL, KVL = 384, 256
MLA_IN = QL + KVL + ROPE
MLA_SCALE = QK ** -0.5
WINDOWS = (2, 4, 8, 16)
PG, PC = 4, 64
PW = PG * PC
RH, RD = 4, 64
RW = RH * RD
LORA, GLORA = 32, 64
RIN = 3 * RW + 4 * LORA + GLORA
INW = MLA_IN + PW + RIN
GN_EPS = 64e-5
C = 64
NPAIR = RH // 2
E, TOPK, FF, NG, TG = 64, 6, 256, 8, 4
EG = E // NG
ROUTED = 2.5
CAP = 128
OUT_OF_RANGE = 65536.0
DECAY = -float(np.exp(-0.5))


def lay_constants():
    t = np.arange(P)
    same = (t[:, None] // C) == (t[None, :] // C)
    parts = {}
    parts["ident"] = np.eye(P)
    strict = (t[:, None] < t[None, :]) & same
    incl = (t[:, None] <= t[None, :]) & same
    parts["mask_st"] = np.concatenate([strict, incl, strict.T, incl.T], 1)
    parts["cum"] = np.concatenate([incl, incl.T], 1)
    lv = []
    for d in range(2):
        for s in [1, 2, 4, 8, 16, 32]:
            blk = (t[:, None] // (2 * s)) == (t[None, :] // (2 * s))
            m = blk & ((t[:, None] // s) % 2 == 1) & ((t[None, :] // s) % 2 == 0)
            lv.append(-(m if d == 0 else m.T).astype(np.float64))
    parts["levels"] = np.concatenate(lv, 1)
    parts["chunk_of"] = np.stack([t < C, t >= C], 1)
    tt = np.arange(SEQ)
    sh = 0.5 * (np.abs(tt[:, None] - tt[None, :]) == 1) - np.eye(SEQ)
    parts["shift"] = np.concatenate([sh[0:P], sh[P:SEQ]], 1)
    row, col = tt // GRID_W, tt % GRID_W
    inv = np.float32(10000.0) ** (-np.arange(ROPE // 4, dtype=np.float32) / np.float32(ROPE // 4))
    ang = np.concatenate([row[:, None].astype(np.float32) * inv, col[:, None].astype(np.float32) * inv], 1)
    for nm, f in (("cos", np.cos), ("sin", np.sin)):
        v = f(ang.astype(np.float32))
        parts[nm] = np.concatenate([v[0:P], v[P:SEQ]], 1)
    parts["iota"] = np.broadcast_to(np.arange(P)[None, :], (P, P))
    parts["before"] = t[:, None] < t[None, :]
    parts["tok"] = t[:, None]
    parts["eye2"] = np.tile(np.eye(C), (2, 1))
    parts["ones"] = np.ones((P, P))
    at, cols, n = {}, [], 0
    for k, v in parts.items():
        v = np.asarray(v, np.float32)
        at[k] = (n, n + v.shape[1])
        n += v.shape[1]
        cols.append(v)
    pool = []
    for w in WINDOWS:
        lo, hi = np.clip(tt - w // 2, 0, SEQ), np.clip(tt + w // 2, 0, SEQ)
        m = ((tt[None, :] >= lo[:, None]) & (tt[None, :] < hi[:, None])) / (hi - lo)[:, None] - np.eye(SEQ)
        pool.append(m.T)
    pool = np.stack(pool, 0).reshape(PG, 2, P, SEQ).transpose(2, 1, 0, 3).reshape(P, 2 * PG * SEQ)
    return np.ascontiguousarray(np.concatenate(cols, 1)), at, np.ascontiguousarray(pool, np.float32)


class Seen:

    def __init__(self):
        self.n = {}

    def __call__(self, sem, by=1):
        self.n[id(sem)] = self.n.get(id(sem), 0) + by
        return self.n[id(sem)]


class Region:

    def __init__(self, arena, start, end):
        self.arena, self.at, self.end = arena, start, end

    def take(self, n, dt=F32):
        a = self.arena[:, self.at:self.at + n]
        self.at += n
        assert self.at <= self.end, (self.at, self.end)
        return a if dt == F32 else a.bitcast(dt)


def trunk_kernel(nc, A, out):
    const_cols, at, _ = lay_constants()
    NCONST = const_cols.shape[1]
    ctx = ExitStack()
    with ctx:
        def sem(name):
            return ctx.enter_context(nc.semaphore(name))

        mod_dram = nc.dram_tensor("mod_rows", [DEPTH, 2, 6 * D], F32).ap()
        h_dram = nc.dram_tensor("h_rows", [NT * P, D], F32).ap()
        y_dram = nc.dram_tensor("y_rows", [NT * P * TOPK, D], F32).ap()

        AR = 52600
        arena = ctx.enter_context(nc.sbuf_tensor("arena", [P, AR], F32))
        pb = ctx.enter_context(nc.psum_tensor("pb", [P, 8, 512], F32))

        fixed = Region(arena, 0, AR)
        x = fixed.take(NT * D).rearrange("p (i d) -> p i d", i=NT)
        cst = fixed.take(NCONST)
        small = fixed.take(2048)
        ones_bf = fixed.take(64, BF16)
        before_bf = fixed.take(64, BF16)
        R0 = fixed.at

        def c_(name):
            return cst[:, at[name][0]:at[name][1]]

        ident = c_("ident")
        masks = c_("mask_st").rearrange("p (d m t) -> p d m t", d=2, m=2)
        cum = c_("cum").rearrange("p (d t) -> p d t", d=2)
        levels = c_("levels").rearrange("p (d l t) -> p d l t", d=2, l=6)
        shift = c_("shift").rearrange("p (k t) -> p k t", k=2)
        cos = c_("cos").rearrange("p (i f) -> p i f", i=NL)
        sin = c_("sin").rearrange("p (i f) -> p i f", i=NL)

        sreg = Region(small, 0, 2048)
        cs = sreg.take(2 * KD).rearrange("p (k s) -> p k s", s=2)
        craw = sreg.take(2 * KD).rearrange("p (s k) -> p s k", s=2)
        ssq = sreg.take(16)
        root = sreg.take(8)
        minus_half = sreg.take(8)
        qcol = sreg.take(QL // P)
        kvcol = sreg.take(KVL // P)

        phase_end = sem("phase_end")
        phases = {}

        def end_phase(eng, name):
            phases[name] = phases.get(name, 0) + 1
            eng.drain().then_inc(phase_end, 1)
            eng.wait_ge(phase_end, 5 * phases[name])

        start_in = sem("start_in")
        ada_in = [sem(f"ada_in{j}") for j in range(4)]
        ada_rows_in = sem("ada_rows_in")
        silu_c = sem("silu_c")
        ada_sum = sem("ada_sum")
        ada_row = sem("ada_row")
        mod_rows = sem("mod_rows_ready")
        mod_out = sem("mod_out")
        bc_in = sem("bc_in")
        h_ready = sem("h_ready")
        hT_sum = sem("hT_sum")
        hT_ready = sem("hT_ready")
        w_in_in = sem("w_in_in")
        z_sum = sem("z_sum")
        z_ready = sem("z_ready")
        mla_in = sem("mla_in")
        zn_ready = sem("zn_ready")
        znT_sum = sem("znT_sum")
        znT_ready = sem("znT_ready")
        qkv_sum = sem("qkv_sum")
        qkv_raw = sem("qkv_raw")
        qk_ready = sem("qk_ready")
        qkT_sum = sem("qkT_sum")
        qkT_ready = sem("qkT_ready")
        score_sum = sem("score_sum")
        max_ready = sem("max_ready")
        probs_ready = sem("probs_ready")
        probsT_sum = sem("probsT_sum")
        probsT_ready = sem("probsT_ready")
        att_sum = sem("att_sum")
        att_ready = sem("att_ready")
        pool_in = sem("pool_in")
        diff_sum = sem("diff_sum")
        diff_ready = sem("diff_ready")
        pool_sum = sem("pool_sum")
        pool_ready = sem("pool_ready")
        w_out_in = sem("w_out_in")
        mixT_sum = sem("mixT_sum")
        mixT_ready = sem("mixT_ready")
        y_sum = sem("y_sum")
        y_sq = sem("y_sq")
        y_used = sem("y_used")

        root_in = sem("root_in")
        root_out = sem("root_out")
        dve_step = sem("dve_step")
        act_step = sem("act_step")
        pool_step = sem("pool_step")
        steps = {}

        def link(eng, ins, s):
            steps[id(s)] = steps.get(id(s), 0) + 1
            ins.then_inc(s, 1)
            eng.wait_ge(s, steps[id(s)])

        r = Region(arena, R0, AR)
        ada_ring = r.take(4 * KD * 512).rearrange("p (j k n) -> p j k n", j=4, k=KD)
        modrow = r.take(6 * D)
        brow = r.take(6 * D)
        grow = r.take(4 * D)
        r = Region(arena, R0, AR)
        hT = r.take(KD * NT * P).rearrange("p (k t) -> p k t", k=KD)
        mix = r.take(NT * D).rearrange("p (i d) -> p i d", i=NT)
        zr = r.take(NT * RIN).rearrange("p (i n) -> p i n", i=NT)
        R_RWKV = r.at
        za = r.take(NT * (INW - RIN)).rearrange("p (i n) -> p i n", i=NT)
        R1 = r.at
        htmp = r.take(D)
        hbuf = r.take(2 * D).rearrange("p (j d) -> p j d", j=2)
        bc = r.take(4 * D).rearrange("p (j d) -> p j d", j=4)
        w_in = r.take(KD * INW).rearrange("p (k n) -> p k n", k=KD)
        ZA = INW - RIN
        ZC = INW // 4
        r = Region(arena, R1, AR)
        w_q = r.take(3 * H * QK).rearrange("p (k n) -> p k n", k=3)
        w_kv = r.take(2 * H * (NOPE + VH)).rearrange("p (k n) -> p k n", k=2)
        qT = r.take(H * NT * P).rearrange("p (h t) -> p h t", h=H)
        kT = r.take(H * NT * P).rearrange("p (h t) -> p h t", h=H)
        vv = r.take(NT * H * VH).rearrange("p (i n) -> p i n", i=NT)
        zn = r.take(2 * (QL + KVL)).rearrange("p (j n) -> p j n", j=2)
        znT = r.take(2 * (QL + KVL)).rearrange("p (j k t) -> p j k t", j=2, k=5)
        qraw = r.take(H * QK).rearrange("p (h n) -> p h n", h=H)
        qrot = r.take(H * QK).rearrange("p (h n) -> p h n", h=H)
        kk_ = r.take(H * QK).rearrange("p (h n) -> p h n", h=H)
        rtmp = r.take(2 * H * ROPE // 2).rearrange("p (j h n) -> p j h n", j=2, h=H)
        probs = r.take(2 * 512).rearrange("p (j t) -> p j t", j=2)
        probsT = r.take(2 * 512).rearrange("p (j k t) -> p j k t", j=2, k=4)
        mrow = r.take(2)
        rsum = r.take(NT * H).rearrange("p (i h) -> p i h", i=NT)
        rinv = r.take(NT * H).rearrange("p (i h) -> p i h", i=NT)
        r = Region(arena, R1, AR)
        poolm = r.take(2 * PG * SEQ).rearrange("p (k g t) -> p k g t", k=2, g=PG)
        pool_w = r.take(PG * PC).rearrange("p (g n) -> p g n", g=PG)
        pool_s = r.take(PW)
        diffT = r.take(2 * SEQ).rearrange("p (j t) -> p j t", j=2)
        r = Region(arena, R1, AR)
        w_out = r.take(KD * D).rearrange("p (k n) -> p k n", k=KD)
        mixT = r.take(2 * KD * P).rearrange("p (j k t) -> p j k t", j=2, k=KD)
        gbc = r.take(2 * D).rearrange("p (s d) -> p s d", s=2)
        ytmp = r.take(D)

        r = Region(arena, R_RWKV, AR)
        rb = {}
        UD = 2 * NPAIR
        NC = NT * 2
        hr = Region(arena, R0, R0 + KD * NT * P)
        rb["TT"] = hr.take(2 * NPAIR * NC * C).rearrange("p (d q c k) -> p d q c k", d=2, q=NPAIR, c=NC)
        rb["W"] = hr.take(2 * NPAIR * NC * C).rearrange("p (d q c k) -> p d q c k", d=2, q=NPAIR, c=NC)
        rb["Z"] = r.take(2 * NPAIR * NC * C).rearrange("p (d q c k) -> p d q c k", d=2, q=NPAIR, c=NC)
        rb["RQT"] = r.take(2 * NPAIR * NT * P).rearrange("p (d q t) -> p d q t", d=2, q=NPAIR)
        rb["AC"] = r.take(2 * NPAIR * NC).rearrange("p (d q c) -> p d q c", d=2, q=NPAIR)
        rb["YV"] = r.take(NT * RW).rearrange("p (i n) -> p i n", i=NT)
        rb["g"] = r.take(NT * RW).rearrange("p (i n) -> p i n", i=NT)
        rb["bonus"] = r.take(NT * RW).rearrange("p (i n) -> p i n", i=NT)
        rb["loraW"] = r.take(4 * RW)
        rb["g2"] = r.take(RW)
        rb["mu"] = r.take(RIN)
        rb["wbias"] = r.take(4 * RW)
        for nm in ("k_k", "k_a", "r_k", "ln_w", "ln_b"):
            rb[nm] = r.take(RW)
        rb["zs"] = r.take(RIN)
        rb["lo"] = r.take(4 * LORA + GLORA)
        rb["loT"] = r.take(2 * P).rearrange("p (j t) -> p j t", j=2)
        rb["xwa"] = r.take(4 * RW).rearrange("p (a d n) -> p a d n", a=2, d=2)
        rb["kk"] = r.take(RW)
        rb["s1"] = r.take(2 * RW).rearrange("p (d n) -> p d n", d=2)
        rb["s2"] = r.take(2 * RW).rearrange("p (d n) -> p d n", d=2)
        rb["arr"] = r.take(4 * 2 * RW).rearrange("p (a d n) -> p a d n", a=4, d=2)
        rb["arrT"] = r.take(4 * 2 * RW).rearrange("p (d q a t) -> p d q a t", d=2, q=NPAIR, a=4)
        rb["LG"] = r.take(2 * RH * 2 * P).rearrange("p (d h m t) -> p d h m t", d=2, h=RH, m=2)
        rb["MG"] = r.take(2 * RH * 2 * P).rearrange("p (d h m t) -> p d h m t", d=2, h=RH, m=2)
        rb["X"] = r.take(2 * RH * P).rearrange("p (d h t) -> p d h t", d=2, h=RH)
        rb["XT"] = r.take(2 * RH * P).rearrange("p (d h t) -> p d h t", d=2, h=RH)
        rb["T1"] = r.take(2 * RH * P).rearrange("p (d h t) -> p d h t", d=2, h=RH)
        rb["KMV"] = r.take(2 * RH * 2 * RD).rearrange("p (d h m n) -> p d h m n", d=2, h=RH, m=2)
        rb["nX"] = r.take(2 * 2 * RW).rearrange("p (d m h n) -> p d m h n", d=2, m=2, h=RH)
        rb["st"] = r.take(32)
        rwkv_top = r.at

        rs = {n: sem("r_" + n) for n in (
            "in", "zero", "shift_sum", "zs_ready", "lo_act", "lo_ready", "loT_sum", "loT_ready", "lora_sum", "xwa_ready",
            "th_ready", "lw_ready", "cum_sum", "eL_ready", "Lx_ready", "eLx_ready", "arr_ready", "arrT_sum",
            "arrT_ready", "mats_sum", "mats_ready", "mv_sum", "kmv_ready", "t1_sum", "t1_ready", "x_sum",
            "x_ready", "nx_sum", "nx_ready", "fin_sum", "fin_ready", "chain_sum", "chain_ready", "inter_sum",
            "inter_used")}
        ORDER = [list(range(2 * NL, NC)) + list(range(2 * NL)), list(range(NC - 1, 2 * NL - 1, -1)) + list(range(2 * NL - 1, -1, -1))]
        r = Region(arena, R0 + 2 * KD * NT * P, AR)
        acc = mix
        ring = r.take(4 * 6 * D).rearrange("p (j n) -> p j n", j=4)
        ring_gu = ring[:, :, 0:4 * D].rearrange("p j (m k n) -> p j m k n", m=2, k=KD)
        ring_dn = ring[:, :, 4 * D:6 * D].rearrange("p j (k n) -> p j k n", k=2)
        r2 = Region(arena, R0 + 2 * KD * NT * P, r.at)
        mtmp = r2.take(D)
        mh = r2.take(2 * D).rearrange("p (j d) -> p j d", j=2)
        mbc = r2.take(4 * D).rearrange("p (j d) -> p j d", j=4)
        rw = r2.take(KD * E).rearrange("p (k e) -> p k e", k=KD)
        sh_gu = r2.take(4 * D).rearrange("p (m k n) -> p m k n", m=2, k=KD)
        sh_dn = r2.take(2 * D).rearrange("p (k n) -> p k n", k=2)
        sh_sg = r2.take(FF)
        sh_act = r2.take(FF)
        sh_aT = r2.take(2 * P).rearrange("p (k t) -> p k t", k=2)
        rbias = r2.take(E)
        sc_ = r2.take(E)
        ex = r2.take(E)
        sel = r2.take(E)
        incl = r2.take(E)
        zero64 = r2.take(E)
        g8 = r2.take(NG * 8).rearrange("p (g n) -> p g n", g=NG)
        small8 = r2.take(64).rearrange("p (a n) -> p a n", n=8)
        idx8 = r2.take(8, U32)
        eq = r2.take(8 * E)
        r3 = Region(arena, R0 + 2 * KD * NT * P, r.at)
        onehot = r3.take(NT * E * CAP // 2, BF16).rearrange("p (i e s) -> p i e s", i=NT, e=E)
        tabf = r3.take(4 * E).rearrange("p (a e) -> p a e", a=4)
        posb = r3.take(NT * E).rearrange("p (i e) -> p i e", i=NT)
        r4 = Region(arena, R0 + 2 * KD * NT * P, r.at)
        ybuf = r4.take(2 * TOPK * D).rearrange("p (j k d) -> p j k d", j=2, k=TOPK)
        fbc = r4.take(2 * D).rearrange("p (s d) -> p s d", s=2)
        ftmp = r4.take(D)
        gx = r.take(2 * D).rearrange("p (j d) -> p j d", j=2)
        gT = r.take(2 * D).rearrange("p (j k t) -> p j k t", j=2, k=KD)
        yx = r.take(2 * D).rearrange("p (j d) -> p j d", j=2)
        sg = r.take(2 * FF).rearrange("p (j n) -> p j n", j=2)
        actx = r.take(2 * FF).rearrange("p (j n) -> p j n", j=2)
        aT = r.take(2 * 2 * P).rearrange("p (j k t) -> p j k t", j=2, k=2)
        mask = r.take(NT * E).rearrange("p (i e) -> p i e", i=NT)
        gates = r.take(E)
        posm = r.take(NT * E).rearrange("p (i e) -> p i e", i=NT)
        gk = r.take(NT * 8).rearrange("p (i k) -> p i k", i=NT)
        mask_bf = r.take(NT * E // 2, BF16).rearrange("p (i e) -> p i e", i=NT)
        meta = r.take(NT * E * 4 // 2, BF16).rearrange("p (i e c) -> p i e c", i=NT, e=E)
        gi = r.take(E, U32)
        si = r.take(E, U32)
        idx_now = r.take(8, U32)
        cntf = r.take(1)
        cnti = r.take(1, I32)
        ms = {n: sem("m_" + n) for n in ("in", "h_out", "logit_sum", "shgu_sum", "ex_ready", "shg_ready", "act_ready", "aT_sum",
                                         "aT_ready", "dn_sum", "sh_ready", "mask_ready", "pos_sum", "count_ready",
                                         "onehot_ready", "tab_sum", "tab_ready", "y_in", "y_used", "x_ready", "out_done")}

        class Pass:

            def __init__(self, tag):
                self.gT_sum = sem(f"{tag}_gT_sum")
                self.gT_ready = sem(f"{tag}_gT_ready")
                self.gu_sum = sem(f"{tag}_gu_sum")
                self.sg_ready = sem(f"{tag}_sg_ready")
                self.act_ready = sem(f"{tag}_act_ready")
                self.aT_sum = sem(f"{tag}_aT_sum")
                self.aT_ready = sem(f"{tag}_aT_ready")
                self.dn_sum = sem(f"{tag}_dn_sum")
                self.y_ready = sem(f"{tag}_y_ready")
                self.gather_idx = sem(f"{tag}_gather_idx")
                self.scatter_idx = sem(f"{tag}_scatter_idx")
                self.w_in = [sem(f"{tag}_w_in{j}") for j in range(4)]
                self.g_in = [sem(f"{tag}_g_in{j}") for j in range(2)]
                self.y_out = [sem(f"{tag}_y_out{j}") for j in range(2)]

        main = Pass("main")
        x_chain = [sem(f"extra{l}_chain") for l in range(DEPTH)]
        x_in = [sem(f"extra{l}_in") for l in range(DEPTH)]
        x_rows = [sem(f"extra{l}_rows") for l in range(DEPTH)]
        x_out = [sem(f"extra{l}_out") for l in range(DEPTH)]
        x_step = [sem(f"extra{l}_step") for l in range(DEPTH)]
        X_TAB = 3
        (X_IDX, X_TURN, X_TURNED, X_GU, X_SILU, X_ACT, X_AT, X_ATC, X_DN, X_Y, X_SIDX, X_OUT) = range(1, 13)

        wait_held = sem("wait_held")

        def x_at(b, e, s=0):
            return (b - 1) * (X_TAB + E * X_OUT) + X_TAB + e * X_OUT + s

        def walk(eng, body):
            n = E // 4
            body(0, True, False)
            with eng.Fori(1, n - 1) as it:
                body(it, False, False)
            body(n - 1, False, True)

        block = ctx.enter_context(nc.Block())

        def tiles_of(l):
            return range(NT if l < DEPTH - 1 else NL)

        def head_rows(h):
            return (h % 2) * RD, (h % 2) * RD + RD

        @block.sync
        def _(sp):
            seen = Seen()
            sp.dma_start(cst, A["shape_consts"]).then_inc(start_in, 16)
            sp.dma_start(craw[:, 0, :], A["c"].rearrange("a (p k) -> p (a k)", p=P)).then_inc(start_in, 16)
            sp.dma_start(craw[:, 1, :], A["c_ctx"].rearrange("(p k) -> p k", p=P)).then_inc(start_in, 16)
            sp.dma_start(x[:, 0:NL, :], A["x"].rearrange("a (i p) d -> p (a i) d", p=P)).then_inc(start_in, 16)
            sp.dma_start(x[:, NL:NT, :], A["ctx"].rearrange("a (i p) d -> p (a i) d", p=P)).then_inc(start_in, 16)

            for l in range(DEPTH):
                if l > 0:
                    sp.wait_ge(mod_rows, l)
                for s in range(2):
                    sp.dma_start(brow[s:s + 1, :], A["ada_b"][l:l + 1, :]).then_inc(ada_rows_in, 16)
                    for g, nm in enumerate(("pre_mix_g", "post_mix_g", "pre_ffn_g", "post_ffn_g")):
                        sp.dma_start(grow[s:s + 1, g * D:(g + 1) * D], A[nm][l:l + 1, :]).then_inc(ada_rows_in, 16)
                for c in range(12):
                    n = 12 * l + c
                    if n >= 4:
                        sp.wait_ge(ada_sum, n - 3)
                    sp.dma_start(ada_ring[:, n % 4], A["ada_w"][l].rearrange("(p k) n -> p k n", p=P)[:, :, c * 512:(c + 1) * 512]
                                 ).then_inc(ada_in[n % 4], 16)
                sp.wait_ge(mod_rows, l + 1)
                sp.dma_start(mod_dram[l], modrow[0:2, :]).then_inc(mod_out, 16)
            sp.wait_ge(mod_out, 16 * DEPTH)
            end_phase(sp, "sp")

            def row(l, s, j):
                return mod_dram[l][s:s + 1, j * D:(j + 1) * D].broadcast_to([P, D])

            for l in range(DEPTH):
                for s in range(2):
                    sp.dma_start(bc[:, 2 * s, :], row(l, s, 1)).then_inc(bc_in, 16)
                    sp.dma_start(bc[:, 2 * s + 1, :], row(l, s, 0)).then_inc(bc_in, 16)
                for k in range(4):
                    sp.dma_start(w_in[:, 2 * k:2 * k + 2, :], A["w_in"][l].rearrange("(p k) n -> p k n", p=P)[:, 2 * k:2 * k + 2, :]
                                 ).then_inc(w_in_in, 16)
                end_phase(sp, "sp")
                sp.dma_start(w_q, A["mla_w_q_b"][l].rearrange("(k p) n -> p k n", p=P)).then_inc(mla_in, 16)
                sp.dma_start(w_kv, A["mla_w_kv_b"][l].rearrange("(k p) n -> p k n", p=P)).then_inc(mla_in, 16)
                sp.dma_start(qcol, A["mla_q_norm"][l].rearrange("(k p) -> p k", p=P), allow_slow_non_contiguous=True).then_inc(mla_in, 16)
                sp.dma_start(kvcol, A["mla_kv_norm"][l].rearrange("(k p) -> p k", p=P), allow_slow_non_contiguous=True).then_inc(mla_in, 16)
                end_phase(sp, "sp")
                sp.dma_start(poolm, A["pool_matrix"].rearrange("p (k g t) -> p k g t", k=2, g=PG)).then_inc(pool_in, 16)
                sp.dma_start(pool_w[0:PC], A["pool_w"][l].rearrange("g c n -> c g n")).then_inc(pool_in, 16)
                sp.dma_start(pool_s, A["pool_scale"][l:l + 1, :].broadcast_to([P, PW])).then_inc(pool_in, 16)
                end_phase(sp, "sp")
                for nm, src, n in (("mu", A["rwkv_mu"][l:l + 1, :], RIN), ("k_k", A["rwkv_k_k"][l:l + 1, :], RW),
                                   ("k_a", A["rwkv_k_a"][l:l + 1, :], RW), ("r_k", A["rwkv_r_k"][l:l + 1].rearrange("a h n -> a (h n)"), RW),
                                   ("ln_w", A["rwkv_ln_w"][l:l + 1, :], RW), ("ln_b", A["rwkv_ln_b"][l:l + 1, :], RW)):
                    sp.dma_start(rb[nm], src.broadcast_to([P, n])).then_inc(rs["in"], 16)
                for a, nm in enumerate(("rwkv_w0", "rwkv_a0")):
                    sp.dma_start(rb["wbias"][:, a * 2 * RW:(a + 1) * 2 * RW], A[nm][l:l + 1].rearrange("a d n -> a (d n)").broadcast_to([P, 2 * RW])
                                 ).then_inc(rs["in"], 16)
                sp.dma_start(rb["g2"][0:GLORA], A["rwkv_g2"][l]).then_inc(rs["in"], 16)
                sp.wait_ge(rs["zero"], l + 1)
                for a, nm in enumerate(("rwkv_w2", "rwkv_a2")):
                    for d in range(2):
                        j = 2 * a + d
                        sp.dma_start(rb["loraW"][j * LORA:(j + 1) * LORA, j * RW:(j + 1) * RW], A[nm][l, d]).then_inc(rs["in"], 16)
                end_phase(sp, "sp")
                for k in range(4):
                    sp.dma_start(w_out[:, 2 * k:2 * k + 2, :], A["w_out"][l].rearrange("(k p) n -> p k n", p=P)[:, 2 * k:2 * k + 2, :]
                                 ).then_inc(w_out_in, 16)
                for s in range(2):
                    sp.dma_start(gbc[:, s, :], row(l, s, 2)).then_inc(w_out_in, 16)
                end_phase(sp, "sp")
                for s in range(2 if l < DEPTH - 1 else 1):
                    sp.dma_start(mbc[:, 2 * s, :], row(l, s, 4)).then_inc(ms["in"], 16)
                    sp.dma_start(mbc[:, 2 * s + 1, :], row(l, s, 3)).then_inc(ms["in"], 16)
                sp.dma_start(rw, A["router_w"][l].rearrange("(p k) e -> p k e", p=P)).then_inc(ms["in"], 16)
                sp.dma_start(rbias, A["router_bias"][l:l + 1, :].broadcast_to([P, E])).then_inc(ms["in"], 16)
                for m, nm in enumerate(("sh_w_gate", "sh_w_up")):
                    sp.dma_start(sh_gu[:, m], A[nm][l].rearrange("(p k) n -> p k n", p=P)).then_inc(ms["in"], 16)
                sp.dma_start(sh_dn, A["sh_w_down"][l].rearrange("(p k) n -> p k n", p=P)).then_inc(ms["in"], 16)
                for i in tiles_of(l):
                    sp.wait_ge(h_ready, NT * (l + 1) + sum(len(tiles_of(a)) for a in range(l)) + i + 1)
                    sp.dma_start(h_dram[i * P:(i + 1) * P, :], mh[:, i % 2, :]).then_inc(ms["h_out"], 16)
                    sp.wait_ge(ms["h_out"], seen(ms["h_out"], 16))
                end_phase(sp, "sp")
                end_phase(sp, "sp")

                def load_walk(S, base):
                    def body(it, first, last):
                        for j in range(4):
                            e = it * 4 + j
                            if not first:
                                sp.wait_ge(S.dn_sum, base + e - 3)
                            for m, nm in enumerate(("exp_w_gate", "exp_w_up")):
                                sp.dma_start(ring_gu[:, j, m], A[nm][l, bass.ds(e, 1)].rearrange("a (p k) n -> p (a k) n", p=P)).then_inc(S.w_in[j], 16)
                            sp.dma_start(ring_dn[:, j], A["exp_w_down"][l, bass.ds(e, 1)].rearrange("a (p k) n -> p (a k) n", p=P)).then_inc(S.w_in[j], 16)
                    walk(sp, body)

                load_walk(main, E * l)
                end_phase(sp, "sp")
                sp.wait_ge(ms["count_ready"], l + 1)
                most = sp.value_load(cnti[0:1, 0:1], min_val=0, max_val=NT * P)
                with sp.If(most > CAP):
                    for b in range(1, len(tiles_of(l))):
                        with sp.Fori(0, E) as e:
                            sp.wait_ge(x_chain[l], x_at(b, e))
                            for m, nm in enumerate(("exp_w_gate", "exp_w_up")):
                                sp.dma_start(ring_gu[:, 0, m], A[nm][l, bass.ds(e, 1)].rearrange("a (p k) n -> p (a k) n", p=P)).then_inc(x_in[l], 16)
                            sp.dma_start(ring_dn[:, 0], A["exp_w_down"][l, bass.ds(e, 1)].rearrange("a (p k) n -> p (a k) n", p=P)).then_inc(x_in[l], 16)
                end_phase(sp, "sp")
                for s in range(len(tiles_of(l)) // 2):
                    sp.dma_start(fbc[:, s, :], row(l, s, 5)).then_inc(ms["y_in"], 16)
                sp.wait_ge(ms["y_in"], seen(ms["y_in"], 16 * (len(tiles_of(l)) // 2)))
                for i in tiles_of(l):
                    if i >= 2:
                        sp.wait_ge(ms["y_used"], seen(ms["y_used"]))
                    sp.dma_start(ybuf[:, i % 2], y_dram[i * P * TOPK:(i + 1) * P * TOPK, :].rearrange("(p k) d -> p k d", k=TOPK)).then_inc(ms["y_in"], 16)
                    sp.wait_ge(ms["y_in"], seen(ms["y_in"], 16))
                seen(ms["y_used"], 2)
                end_phase(sp, "sp")
                if l == DEPTH - 1:
                    sp.dma_start(out[0].rearrange("(i p) d -> p i d", p=P), x[:, 0:NL, :]).then_inc(ms["out_done"], 16)
                    sp.wait_ge(ms["out_done"], 16)

        @block.tensor
        def _(pe):
            seen = Seen()
            mm = nc.tensor.matmul
            tr = nc.tensor.transpose
            pe.wait_ge(start_in, 80)
            pe.wait_ge(silu_c, 1)
            for n in range(12 * DEPTH):
                pe.wait_ge(ada_in[n % 4], 16 * (n // 4 + 1))
                if n >= 2:
                    pe.wait_ge(ada_row, n - 1)
                for k in range(KD):
                    last = mm(pb[0:2, n % 2, :], cs[:, k, :], ada_ring[:, n % 4, k, :], start=(k == 0), stop=(k == KD - 1))
                last.then_inc(ada_sum, 1)
            end_phase(pe, "pe")

            def turn_tile(src, first_bank):
                for k in range(KD):
                    last = tr(pb[:, first_bank + k // 4, (k % 4) * P:(k % 4 + 1) * P], src[:, k * P:(k + 1) * P], ident)
                return last

            for l in range(DEPTH):
                def h_turn(i):
                    pe.wait_ge(h_ready, seen(h_ready))
                    if i >= 2:
                        pe.wait_ge(hT_ready, seen(hT_ready))
                    turn_tile(hbuf[:, i % 2, :], 2 * (i % 2)).then_inc(hT_sum, 1)

                for i in range(NT):
                    h_turn(i)
                pe.wait_ge(hT_ready, seen(hT_ready, 2))
                pe.wait_ge(w_in_in, seen(w_in_in, 64))
                n = 0
                for i in range(NT):
                    for c in range(4):
                        if n >= 4:
                            pe.wait_ge(z_ready, seen(z_ready))
                        w0, wn = (c * ZA // 2, ZA // 2) if c < 2 else (ZA + (c - 2) * RIN // 2, RIN // 2)
                        for k in range(KD):
                            last = mm(pb[:, 4 + n % 4, 0:wn], hT[:, k, i * P:(i + 1) * P], w_in[:, k, w0:w0 + wn],
                                      start=(k == 0), stop=(k == KD - 1))
                        last.then_inc(z_sum, 1)
                        n += 1
                seen(z_ready, 4)
                end_phase(pe, "pe")

                pe.wait_ge(mla_in, seen(mla_in, 64))
                for i in range(NT):
                    pe.wait_ge(zn_ready, seen(zn_ready))
                    for k in range(5):
                        last = tr(pb[:, k // 4, (k % 4) * P:(k % 4 + 1) * P], zn[:, i % 2, k * P:(k + 1) * P], ident)
                    last.then_inc(znT_sum, 1)
                    pe.wait_ge(znT_ready, seen(znT_ready))
                    for c in range(2):
                        for k in range(3):
                            mm(pb[:, 2 + c, 0:384], znT[:, i % 2, k, :], w_q[:, k, c * 384:(c + 1) * 384], start=(k == 0), stop=(k == 2))
                    for c in range(2):
                        for k in range(2):
                            last = mm(pb[:, 4 + c, :], znT[:, i % 2, 3 + k, :], w_kv[:, k, c * 512:(c + 1) * 512], start=(k == 0), stop=(k == 1))
                    last.then_inc(qkv_sum, 1)
                    pe.wait_ge(qk_ready, seen(qk_ready))
                    for src in (qraw, kk_):
                        for h in range(H):
                            last = tr(pb[0:QK, 6 + h // 4, (h % 4) * P:(h % 4 + 1) * P], src[:, h, :], ident)
                        last.then_inc(qkT_sum, 1)
                        pe.wait_ge(qkT_ready, seen(qkT_ready))

                units = [(i, h) for i in tiles_of(l) for h in range(H)]
                keys = lambda i: (0, NT) if i < NL else (NL, NT)

                def score(u):
                    i, h = units[u]
                    a, b = keys(i)
                    mm(pb[:, u % 2, 0:(b - a) * P], qT[0:QK, h, i * P:(i + 1) * P], kT[0:QK, h, a * P:b * P],
                       start=True, stop=True).then_inc(score_sum, 1)

                score(0)
                for u, (i, h) in enumerate(units):
                    a, b = keys(i)
                    pe.wait_ge(probs_ready, seen(probs_ready))
                    if u + 1 < len(units):
                        score(u + 1)
                    if u >= 2:
                        pe.wait_ge(probsT_ready, seen(probsT_ready) - 1)
                        seen(probsT_ready, -1)
                    for k in range(b - a):
                        last = tr(pb[:, 2 + u % 2, k * P:(k + 1) * P], probs[:, u % 2, k * P:(k + 1) * P], ident)
                    last.then_inc(probsT_sum, 1)
                    pe.wait_ge(probsT_ready, seen(probsT_ready))
                    if h == 0 and i >= 2:
                        pe.wait_ge(att_ready, seen(att_ready))
                    for k in range(a, b):
                        last = mm(pb[:, 4 + i % 2, h * VH:(h + 1) * VH], probsT[:, u % 2, k - a, :], vv[:, k, h * VH:(h + 1) * VH],
                                  start=(k == a), stop=(k == b - 1))
                    last.then_inc(att_sum, 1)
                pe.wait_ge(att_ready, seen(att_ready, 2))
                end_phase(pe, "pe")

                pe.wait_ge(pool_in, seen(pool_in, 48))
                groups = [(s, g) for s in range(len(tiles_of(l)) // 2) for g in range(PG)]
                for u, (s, g) in enumerate(groups):
                    for k in range(2):
                        last = mm(pb[0:PC, u % 2, 0:SEQ], za[:, 2 * s + k, MLA_IN + g * PC:MLA_IN + (g + 1) * PC], poolm[:, k, g, :],
                                  start=(k == 0), stop=(k == 1))
                    last.then_inc(diff_sum, 1)
                    pe.wait_ge(diff_ready, seen(diff_ready))
                    for t in range(2):
                        last = mm(pb[:, 2 + 2 * s + t, g * PC:(g + 1) * PC], diffT[0:PC, u % 2, t * P:(t + 1) * P], pool_w[0:PC, g, :],
                                  start=True, stop=True)
                    last.then_inc(pool_sum, 1)
                end_phase(pe, "pe")

                R = rs
                pe.wait_ge(R["in"], seen(R["in"], 16 * 13))
                order_i = list(range(NT))
                for i in order_i:
                    s = i // 2
                    for c in range(2):
                        for k in range(2):
                            last = mm(pb[:, c, 0:RIN // 2], shift[:, k, (i % 2) * P:(i % 2 + 1) * P],
                                      zr[:, 2 * s + k, c * RIN // 2:(c + 1) * RIN // 2], start=(k == 0), stop=(k == 1))
                    last.then_inc(R["shift_sum"], 1)
                    pe.wait_ge(R["lo_ready"], seen(R["lo_ready"]))
                    tr(pb[:, 2, 0:P], rb["lo"][:, 0:P], ident)
                    tr(pb[0:GLORA, 2, P:2 * P], rb["lo"][:, P:P + GLORA], ident).then_inc(R["loT_sum"], 1)
                    pe.wait_ge(R["loT_ready"], seen(R["loT_ready"]))
                    for c in range(2):
                        mm(pb[:, 3 + c, :], rb["loT"][:, 0, :], rb["loraW"][:, c * 512:(c + 1) * 512], start=True, stop=True)
                    mm(pb[:, 5, 0:RW], rb["loT"][0:GLORA, 1, :], rb["g2"][0:GLORA], start=True, stop=True).then_inc(R["lora_sum"], 1)
                    pe.wait_ge(R["lw_ready"], seen(R["lw_ready"]))
                    for d in range(2):
                        mm(pb[:, 6, d * RW:(d + 1) * RW], cum[:, d, :], rb["xwa"][:, 0, d, :], start=True, stop=True)
                    for d in range(2):
                        for q in range(NPAIR):
                            last = mm(pb[:, 7, (2 * d + q) * 2:(2 * d + q) * 2 + 2], rb["xwa"][:, 0, d, q * P:(q + 1) * P], c_("chunk_of"),
                                      start=True, stop=True)
                    last.then_inc(R["cum_sum"], 1)
                    pe.wait_ge(R["arr_ready"], seen(R["arr_ready"]))
                    for d in range(2):
                        for q in range(NPAIR):
                            for a in range(4):
                                last = tr(pb[:, 2 * d + q, a * P:(a + 1) * P], rb["arr"][:, a, d, q * P:(q + 1) * P], ident)
                    last.then_inc(R["arrT_sum"], 1)
                    pe.wait_ge(R["arrT_ready"], seen(R["arrT_ready"]))
                    v_ = lambda h: rb["zs"][:, 2 * RW + h * RD:2 * RW + (h + 1) * RD]
                    for d in range(2):
                        if d == 1:
                            pe.wait_ge(R["mats_ready"], seen(R["mats_ready"]))
                        for h in range(RH):
                            a, b = head_rows(h)
                            q = h // 2
                            T = rb["arrT"][a:b, d, q]
                            mm(pb[:, 4 + h % 2, q * P:(q + 1) * P], T[:, 0, :], T[:, 2, :], start=True, stop=True)
                            kr = T[:, 0:2, :].rearrange("p a t -> p (a t)")
                            mm(pb[:, h % 2, q * 256:(q + 1) * 256], T[:, 2, :], kr, start=True, stop=True)
                            last = mm(pb[:, 2 + h % 2, q * 256:(q + 1) * 256], T[:, 3, :], kr, start=True, stop=True)
                        last.then_inc(R["mats_sum"], 1)
                    pe.wait_ge(R["mats_ready"], seen(R["mats_ready"]))
                    for d in range(2):
                        for h in range(RH):
                            last = mm(pb[:, 6 + d, h * RD:(h + 1) * RD], rb["MG"][:, d, h, 0, :], v_(h), start=True, stop=True)
                        last.then_inc(R["mv_sum"], 1)
                    for lv in range(1, 6):
                        for d in range(2):
                            if lv > 1:
                                pe.wait_ge(R["x_ready"], seen(R["x_ready"]))
                            for h in range(RH):
                                last = mm(pb[:, 4 + d, h * P:(h + 1) * P], rb["LG"][:, d, h, 0, :], rb["X"][:, d, h, :], start=True, stop=True)
                            last.then_inc(R["t1_sum"], 1)
                        for d in range(2):
                            pe.wait_ge(R["t1_ready"], seen(R["t1_ready"]))
                            for h in range(RH):
                                if lv < 5:
                                    mm(pb[:, d, h * P:(h + 1) * P], rb["XT"][:, d, h, :], rb["T1"][:, d, h, :], start=True, stop=True)
                                last = mm(pb[:, 2 + d, h * P:(h + 1) * P], rb["T1"][:, d, h, :], rb["XT"][:, d, h, :], start=True, stop=True)
                            last.then_inc(R["x_sum"], 1)
                    for d in range(2):
                        pe.wait_ge(R["x_ready"], seen(R["x_ready"]))
                        pe.wait_ge(R["kmv_ready"], seen(R["kmv_ready"]))
                        for h in range(RH):
                            last = mm(pb[:, 4 + d, h * P:(h + 1) * P], rb["XT"][:, d, h, :], rb["KMV"][:, d, h].rearrange("p m n -> p (m n)"),
                                      start=True, stop=True)
                        last.then_inc(R["nx_sum"], 1)
                    pe.wait_ge(R["nx_ready"], seen(R["nx_ready"], 2))
                    for h in range(RH):
                        for d in range(2):
                            mm(pb[:, 0, h * RD:(h + 1) * RD], rb["MG"][:, d, h, 1, :], v_(h), start=(d == 0), stop=False)
                            mm(pb[:, 0, h * RD:(h + 1) * RD], rb["LG"][:, d, h, 1, :], rb["nX"][:, d, 1, h, :], start=False, stop=(d == 1))
                    for d in range(2):
                        for h in range(RH):
                            a, b = head_rows(h)
                            dq = 2 * d + h // 2
                            mm(pb[a:b, 1, dq * P:(dq + 1) * P], rb["nX"][:, d, 0, h, :], rb["LG"][:, d, h, 1, :], start=True, stop=True)
                            for c in range(2):
                                ca, cb = c * C, (c + 1) * C
                                o = dq * C
                                beta = rb["arr"][ca:cb, 2, d, h * RD:(h + 1) * RD]
                                khat = rb["arr"][ca:cb, 3, d, h * RD:(h + 1) * RD]
                                mm(pb[a:b, 2 + 2 * c, o:o + C], rb["nX"][ca:cb, d, 0, h, :], beta, start=True, stop=True)
                                mm(pb[a:b, 3 + 2 * c, o:o + C], khat, rb["zs"][ca:cb, 2 * RW + h * RD:2 * RW + (h + 1) * RD], start=True, stop=False)
                                last = mm(pb[a:b, 3 + 2 * c, o:o + C], beta, rb["nX"][ca:cb, d, 1, h, :], start=False, stop=True)
                    last.then_inc(R["fin_sum"], 1)
                    pe.wait_ge(R["fin_ready"], seen(R["fin_ready"]))
                for n in range(1, NC - 1):
                    for d in range(2):
                        pe.wait_ge(R["chain_ready"], seen(R["chain_ready"]))
                        cp = ORDER[d][n]
                        for h in range(RH):
                            a, b = head_rows(h)
                            last = mm(pb[a:b, d, (h // 2) * RD:(h // 2 + 1) * RD], rb["TT"][a:b, d, h // 2, cp, :], rb["Z"][a:b, d, h // 2, cp, :],
                                      start=True, stop=True)
                        last.then_inc(R["chain_sum"], 1)
                pe.wait_ge(R["chain_ready"], seen(R["chain_ready"], 2))
                for i in tiles_of(l):
                    if i >= 2:
                        pe.wait_ge(R["inter_used"], seen(R["inter_used"]))
                    for h in range(RH):
                        a, b = head_rows(h)
                        for j in range(2):
                            c = 2 * i + j
                            ds = [d for d in range(2) if c != ORDER[d][0]]
                            for d in ds:
                                last = mm(pb[j * C:(j + 1) * C, 4 + 2 * (i % 2) + h % 2, (h // 2) * RD:(h // 2 + 1) * RD], rb["RQT"][a:b, d, h // 2, c * C:(c + 1) * C],
                                          rb["Z"][a:b, d, h // 2, c, :], start=(d == ds[0]), stop=(d == ds[-1]))
                    last.then_inc(R["inter_sum"], 1)
                pe.wait_ge(R["inter_used"], seen(R["inter_used"], 2))
                end_phase(pe, "pe")

                pe.wait_ge(w_out_in, seen(w_out_in, 96))
                for i in tiles_of(l):
                    turn_tile(mix[:, i, :], 0).then_inc(mixT_sum, 1)
                    pe.wait_ge(mixT_ready, seen(mixT_ready))
                    if i >= 2:
                        pe.wait_ge(y_used, seen(y_used))
                    for c in range(2):
                        for k in range(KD):
                            last = mm(pb[:, 4 + 2 * (i % 2) + c, :], mixT[:, i % 2, k, :], w_out[:, k, c * 512:(c + 1) * 512],
                                      start=(k == 0), stop=(k == KD - 1))
                    last.then_inc(y_sum, 1)
                pe.wait_ge(y_used, seen(y_used, 2))
                end_phase(pe, "pe")
                pe.wait_ge(ms["in"], seen(ms["in"], 16 * (5 + 2 * (len(tiles_of(l)) // 2))))
                for i in tiles_of(l):
                    pe.wait_ge(h_ready, seen(h_ready))
                    turn_tile(mh[:, i % 2, :], 2 * (i % 2)).then_inc(hT_sum, 1)
                    pe.wait_ge(hT_ready, seen(hT_ready))
                    own = slice(i * P, (i + 1) * P)
                    for k in range(KD):
                        last = mm(pb[:, 4, 0:E], hT[:, k, own], rw[:, k, :], start=(k == 0), stop=(k == KD - 1))
                    last.then_inc(ms["logit_sum"], 1)
                    for m in range(2):
                        for k in range(KD):
                            last = mm(pb[:, 5, m * FF:(m + 1) * FF], hT[:, k, own], sh_gu[:, m, k, :], start=(k == 0), stop=(k == KD - 1))
                    last.then_inc(ms["shgu_sum"], 1)
                    pe.wait_ge(ms["act_ready"], seen(ms["act_ready"]))
                    for k in range(2):
                        last = tr(pb[:, 4, k * P:(k + 1) * P], sh_act[:, k * P:(k + 1) * P], ident)
                    last.then_inc(ms["aT_sum"], 1)
                    pe.wait_ge(ms["aT_ready"], seen(ms["aT_ready"]))
                    for c in range(2):
                        for k in range(2):
                            last = mm(pb[:, 6 + c, :], sh_aT[:, k, :], sh_dn[:, k, c * 512:(c + 1) * 512], start=(k == 0), stop=(k == 1))
                    last.then_inc(ms["dn_sum"], 1)
                    pe.wait_ge(ms["sh_ready"], seen(ms["sh_ready"]))
                pe.wait_ge(ms["mask_ready"], seen(ms["mask_ready"], len(tiles_of(l))))
                nt = len(tiles_of(l))
                for i in range(nt):
                    for j in range(i + 1):
                        mm(pb[:, 0, i * E:(i + 1) * E], before_bf if j == i else ones_bf, mask_bf[:, j, :], start=(j == 0), stop=(j == i))
                for j in range(nt):
                    last = mm(pb[:, 0, nt * E:(nt + 1) * E], ones_bf, mask_bf[:, j, :], start=(j == 0), stop=(j == nt - 1))
                last.then_inc(ms["pos_sum"], 1)
                end_phase(pe, "pe")

                def tables(done):
                    for e in range(E):
                        for i in range(nt):
                            last = mm(pb[:, 0, 4 * e:4 * e + 4], onehot[:, i, e, :], meta[:, i, e, :], start=(i == 0), stop=(i == nt - 1))
                    last.then_inc(done, 1)

                pe.wait_ge(ms["onehot_ready"], seen(ms["onehot_ready"]))
                tables(ms["tab_sum"])
                end_phase(pe, "pe")

                def ffn_walk(S, base):
                    def turn(m, j):
                        pe.wait_ge(S.g_in[j % 2], m)
                        turn_tile(gx[:, j % 2, :], 0).then_inc(S.gT_sum, 1)

                    def gathered(it, j):
                        return 16 * (base // 2 + 2 * it + j // 2 + 1)

                    def body(it, first, last_):
                        for j in range(4):
                            n = it * 4 + j + base
                            if first and j == 0:
                                turn(gathered(0, 0), 0)
                            pe.wait_ge(S.w_in[j], 48 * (it + 1 + base // 4))
                            pe.wait_ge(S.gT_ready, n + 1)
                            if not (first and j < 2):
                                pe.wait_ge(S.act_ready, n - 1)
                            for m in range(2):
                                for k in range(KD):
                                    last = mm(pb[:, 2 + j % 2, m * FF:(m + 1) * FF], gT[:, j % 2, k, :], ring_gu[:, j, m, k, :],
                                              start=(k == 0), stop=(k == KD - 1))
                            last.then_inc(S.gu_sum, 1)
                            if not (last_ and j == 3):
                                turn(gathered(it, j + 1) if j < 3 else gathered(it + 1, 0), j + 1)
                            pe.wait_ge(S.act_ready, n + 1)
                            for k in range(2):
                                last = tr(pb[:, 4, k * P:(k + 1) * P], actx[:, j % 2, k * P:(k + 1) * P], ident)
                            last.then_inc(S.aT_sum, 1)
                            pe.wait_ge(S.aT_ready, n + 1)
                            if not (first and j == 0):
                                pe.wait_ge(S.y_ready, n)
                            for c in range(2):
                                for k in range(2):
                                    last = mm(pb[:, 5 + c, :], aT[:, j % 2, k, :], ring_dn[:, j, k, c * 512:(c + 1) * 512], start=(k == 0), stop=(k == 1))
                            last.then_inc(S.dn_sum, 1)
                    walk(pe, body)

                ffn_walk(main, E * l)
                end_phase(pe, "pe")
                pe.wait_ge(ms["count_ready"], l + 1)
                most = pe.value_load(cnti[0:1, 0:1], min_val=0, max_val=NT * P)
                with pe.If(most > CAP):
                    for b in range(1, nt):
                        pe.wait_ge(x_chain[l], x_at(b, 0) - 2)
                        tables(x_chain[l])
                        with pe.Fori(0, E) as e:
                            pe.wait_ge(x_in[l], 48 * ((b - 1) * E + e + 1))
                            pe.wait_ge(x_rows[l], 16 * ((b - 1) * E + e + 1))
                            turn_tile(gx[:, 0, :], 0).then_inc(x_chain[l], 1)
                            pe.wait_ge(x_chain[l], x_at(b, e, X_TURNED))
                            for m in range(2):
                                for k in range(KD):
                                    last = mm(pb[:, 2, m * FF:(m + 1) * FF], gT[:, 0, k, :], ring_gu[:, 0, m, k, :], start=(k == 0), stop=(k == KD - 1))
                            last.then_inc(x_chain[l], 1)
                            pe.wait_ge(x_chain[l], x_at(b, e, X_ACT))
                            for k in range(2):
                                last = tr(pb[:, 4, k * P:(k + 1) * P], actx[:, 0, k * P:(k + 1) * P], ident)
                            last.then_inc(x_chain[l], 1)
                            pe.wait_ge(x_chain[l], x_at(b, e, X_ATC))
                            for c in range(2):
                                for k in range(2):
                                    last = mm(pb[:, 5 + c, :], aT[:, 0, k, :], ring_dn[:, 0, k, c * 512:(c + 1) * 512], start=(k == 0), stop=(k == 1))
                            last.then_inc(x_chain[l], 1)
                end_phase(pe, "pe")
                end_phase(pe, "pe")

        @block.scalar
        def _(act):
            seen = Seen()
            ac = nc.scalar.activation
            act.wait_ge(start_in, 80)
            ac(cs.rearrange("p k s -> p s k"), craw, ACT.Silu).then_inc(silu_c, 1)
            end_phase(act, "act")
            for l in range(DEPTH):
                for i in range(NT):
                    act.wait_ge(hT_sum, seen(hT_sum))
                    ac(hT[:, :, i * P:(i + 1) * P], pb[:, 2 * (i % 2):2 * (i % 2) + 2, :].rearrange("p b (k t) -> p (b k) t", k=4), ACT.Copy
                       ).then_inc(hT_ready, 1)
                for i in range(NT):
                    for c in range(4):
                        act.wait_ge(z_sum, seen(z_sum))
                        wn = ZA // 2 if c < 2 else RIN // 2
                        dst = za[:, i, c * wn:(c + 1) * wn] if c < 2 else zr[:, i, (c - 2) * wn:(c - 1) * wn]
                        ac(dst, pb[:, 4 + (4 * i + c) % 4, 0:wn], ACT.Copy).then_inc(z_ready, 1)
                end_phase(act, "act")
                act.wait_ge(mla_in, seen(mla_in, 64))
                for i in range(NT):
                    act.wait_ge(znT_sum, seen(znT_sum))
                    for k in range(5):
                        col = qcol[:, k:k + 1] if k < 3 else kvcol[:, k - 3:k - 2]
                        last = ac(znT[:, i % 2, k, :], pb[:, k // 4, (k % 4) * P:(k % 4 + 1) * P], ACT.Copy, scale=col)
                    last.then_inc(znT_ready, 1)
                    act.wait_ge(qkv_sum, seen(qkv_sum))
                    for c in range(2):
                        ac(qraw[:, 4 * c:4 * c + 4, :], pb[:, 2 + c, 0:384].rearrange("p (h n) -> p h n", h=4), ACT.Copy)
                        kv = pb[:, 4 + c, :].rearrange("p (h n) -> p h n", h=4)
                        ac(kk_[:, 4 * c:4 * c + 4, 0:NOPE], kv[:, :, 0:NOPE], ACT.Copy)
                        last = ac(vv[:, i, 4 * c * VH:4 * (c + 1) * VH].rearrange("p (h n) -> p h n", h=4), kv[:, :, NOPE:NOPE + VH], ACT.Copy)
                    last.then_inc(qkv_raw, 1)
                    for dst in (qT, kT):
                        act.wait_ge(qkT_sum, seen(qkT_sum))
                        ac(dst[0:QK, :, i * P:(i + 1) * P], pb[0:QK, 6:8, :].rearrange("p b (h t) -> p (b h) t", h=4), ACT.Copy
                           ).then_inc(qkT_ready, 1)
                units = [(i, h) for i in tiles_of(l) for h in range(H)]
                for u, (i, h) in enumerate(units):
                    nk = (NT if i < NL else NT - NL) * P
                    act.wait_ge(max_ready, seen(max_ready))
                    if u >= 2:
                        act.wait_ge(probsT_sum, seen(probsT_sum))
                    ac(probs[:, u % 2, 0:nk], pb[:, u % 2, 0:nk], ACT.Exp, bias=mrow[:, u % 2:u % 2 + 1], scale=MLA_SCALE,
                       accum_out=rsum[:, i, h:h + 1]).then_inc(probs_ready, 1)
                seen(probsT_sum, 2)
                end_phase(act, "act")
                for u in range(len(tiles_of(l)) // 2 * PG):
                    act.wait_ge(diff_sum, seen(diff_sum))
                    if u >= 2:
                        act.wait_ge(pool_sum, seen(pool_sum))
                    ac(diffT[0:PC, u % 2, :], pb[0:PC, u % 2, 0:SEQ], ACT.Copy).then_inc(diff_ready, 1)
                seen(pool_sum, 2)
                end_phase(act, "act")
                R = rs
                for i in range(NT):
                    act.wait_ge(R["zs_ready"], seen(R["zs_ready"]))
                    ac(rb["lo"][:, 0:2 * LORA], rb["zs"][:, 3 * RW:3 * RW + 2 * LORA], ACT.Tanh)
                    ac(rb["lo"][:, 2 * LORA:4 * LORA], rb["zs"][:, 3 * RW + 2 * LORA:3 * RW + 4 * LORA], ACT.Copy)
                    ac(rb["lo"][:, 4 * LORA:], rb["zs"][:, 3 * RW + 4 * LORA:RIN], ACT.Tanh, scale=0.5).then_inc(R["lo_act"], 1)
                    act.wait_ge(R["loT_sum"], seen(R["loT_sum"]))
                    ac(rb["loT"][:, 0, :], pb[:, 2, 0:P], ACT.Copy)
                    ac(rb["loT"][0:GLORA, 1, :], pb[0:GLORA, 2, P:2 * P], ACT.Copy).then_inc(R["loT_ready"], 1)
                    act.wait_ge(R["xwa_ready"], seen(R["xwa_ready"]))
                    ac(rb["xwa"], rb["xwa"], ACT.Tanh, scale=0.5).then_inc(R["th_ready"], 1)
                    act.wait_ge(R["cum_sum"], seen(R["cum_sum"]))
                    ac(rb["arr"][:, 1].rearrange("p d n -> p (d n)"), pb[:, 6, :], ACT.Exp)
                    ac(rb["s1"].rearrange("p d n -> p (d n)"), pb[:, 6, :], ACT.Exp, scale=-1.0)
                    ac(rb["AC"].rearrange("p d q c -> p (d q) c")[:, :, 2 * i:2 * i + 2], pb[:, 7, 0:8].rearrange("p (a c) -> p a c", c=2), ACT.Exp
                       ).then_inc(R["eL_ready"], 1)
                    act.wait_ge(R["Lx_ready"], seen(R["Lx_ready"]))
                    ac(rb["arr"][:, 0], rb["s2"], ACT.Exp).then_inc(R["eLx_ready"], 1)
                    act.wait_ge(R["arrT_sum"], seen(R["arrT_sum"]))
                    for dq in range(4):
                        last = ac(rb["arrT"][:, dq // 2, dq % 2].rearrange("p a t -> p (a t)"), pb[:, dq, :], ACT.Copy)
                    last.then_inc(R["arrT_ready"], 1)
                end_phase(act, "act")
                for i in tiles_of(l):
                    act.wait_ge(mixT_sum, seen(mixT_sum))
                    ac(mixT[:, i % 2], pb[:, 0:2, :].rearrange("p b (k t) -> p (b k) t", k=4), ACT.Copy).then_inc(mixT_ready, 1)
                    act.wait_ge(y_sum, seen(y_sum))
                    if i >= 1:
                        act.wait_ge(y_used, seen(y_used))
                    ac(ytmp, pb[:, 4 + 2 * (i % 2):6 + 2 * (i % 2), :].rearrange("p b n -> p (b n)"), ACT.Square,
                       accum_out=ssq[:, i:i + 1]).then_inc(y_sq, 1)
                seen(y_used, 1)
                end_phase(act, "act")
                for i in tiles_of(l):
                    act.wait_ge(hT_sum, seen(hT_sum))
                    ac(hT[:, :, i * P:(i + 1) * P], pb[:, 2 * (i % 2):2 * (i % 2) + 2, :].rearrange("p b (k t) -> p (b k) t", k=4), ACT.Copy
                       ).then_inc(hT_ready, 1)
                    act.wait_ge(ms["logit_sum"], seen(ms["logit_sum"]))
                    if i >= 1:
                        act.wait_ge(ms["mask_ready"], seen(ms["mask_ready"]))
                    ac(ex, pb[:, 4, 0:E], ACT.Exp, scale=-1.0).then_inc(ms["ex_ready"], 1)
                    act.wait_ge(ms["shgu_sum"], seen(ms["shgu_sum"]))
                    ac(sh_sg, pb[:, 5, 0:FF], ACT.Silu).then_inc(ms["shg_ready"], 1)
                    act.wait_ge(ms["aT_sum"], seen(ms["aT_sum"]))
                    ac(sh_aT.rearrange("p k t -> p (k t)"), pb[:, 4, 0:2 * P], ACT.Copy).then_inc(ms["aT_ready"], 1)
                    act.wait_ge(ms["dn_sum"], seen(ms["dn_sum"]))
                    ac(acc[:, i, :], pb[:, 6:8, :].rearrange("p b n -> p (b n)"), ACT.Copy).then_inc(ms["sh_ready"], 1)
                seen(ms["mask_ready"])
                end_phase(act, "act")
                end_phase(act, "act")

                def act_walk(S, base):
                    def turned(n, j):
                        act.wait_ge(S.gT_sum, n + 1)
                        ac(gT[:, j % 2].rearrange("p k t -> p (k t)"), pb[:, 0:2, :].rearrange("p b n -> p (b n)"), ACT.Copy).then_inc(S.gT_ready, 1)

                    def body(it, first, last_):
                        for j in range(4):
                            n = it * 4 + j + base
                            if first and j == 0:
                                turned(n, 0)
                            act.wait_ge(S.gu_sum, n + 1)
                            if not (first and j < 2):
                                act.wait_ge(S.act_ready, n - 1)
                            ac(sg[:, j % 2], pb[:, 2 + j % 2, 0:FF], ACT.Silu).then_inc(S.sg_ready, 1)
                            if not (last_ and j == 3):
                                turned(n + 1, j + 1)
                    walk(act, body)

                act_walk(main, E * l)
                end_phase(act, "act")
                act.wait_ge(ms["count_ready"], l + 1)
                most = act.value_load(cnti[0:1, 0:1], min_val=0, max_val=NT * P)
                with act.If(most > CAP):
                    for b in range(1, len(tiles_of(l))):
                        with act.Fori(0, E) as e:
                            act.wait_ge(x_chain[l], x_at(b, e, X_TURN))
                            ac(gT[:, 0].rearrange("p k t -> p (k t)"), pb[:, 0:2, :].rearrange("p b n -> p (b n)"), ACT.Copy).then_inc(x_chain[l], 1)
                            act.wait_ge(x_chain[l], x_at(b, e, X_GU))
                            ac(sg[:, 0], pb[:, 2, 0:FF], ACT.Silu).then_inc(x_chain[l], 1)
                end_phase(act, "act")
                end_phase(act, "act")

        @block.vector
        def _(dve):
            seen, sent = Seen(), Seen()
            V = nc.vector

            def step(ins):
                link(dve, ins, dve_step)

            def power(last):
                last.then_inc(root_in, 1)
                dve.wait_ge(root_out, seen(root_out))

            def inv_root(src, n, eps):
                dst = root[:, 0:src.shape[1]]
                power(V.tensor_scalar(dst, src, 1.0 / n, eps, ALU.mult, ALU.add))
                return dst

            def norm_tile(i, gain, shift_row, dst, tmp):
                step(V.tensor_tensor_reduce(tmp, x[:, i, :], x[:, i, :], 1.0, 0.0, ALU.mult, ALU.add, ssq[:, i:i + 1]))
                rstd = inv_root(ssq[:, i:i + 1], D, EPS)
                step(V.scalar_tensor_tensor(tmp, x[:, i, :], rstd, gain, ALU.mult, ALU.mult))
                return V.tensor_tensor(dst.rearrange("p (k q) -> p q k", k=KD), tmp.rearrange("p (q k) -> p q k", k=KD),
                                       shift_row.rearrange("p (q k) -> p q k", k=KD), ALU.add)

            def residual(i, y, gain, tmp):
                rstd = inv_root(ssq[:, i:i + 1], D, EPS)
                step(V.scalar_tensor_tensor(tmp, y, rstd, gain, ALU.mult, ALU.mult))
                return V.tensor_tensor(x[:, i, :], x[:, i, :], tmp, ALU.add)

            dve.wait_ge(start_in, 80)
            V.memset(minus_half, -0.5)
            step(V.memset(root, 1.0))
            V.tensor_copy(ones_bf, c_("ones"))
            V.tensor_copy(before_bf, c_("before"))
            for l in range(DEPTH):
                dve.wait_ge(ada_rows_in, 160 * (l + 1))
                if l > 0:
                    dve.wait_ge(mod_out, 16 * l)
                for c in range(12):
                    dve.wait_ge(ada_sum, 12 * l + c + 1)
                    last = V.tensor_tensor(modrow[0:2, c * 512:(c + 1) * 512], pb[0:2, (12 * l + c) % 2, :], brow[0:2, c * 512:(c + 1) * 512], ALU.add)
                    last.then_inc(ada_row, 1)
                dve.wait_ge(ada_row, 12 * (l + 1))
                def mr(j):
                    return modrow[0:2, j * D:(j + 1) * D]
                V.scalar_tensor_tensor(mr(1), mr(1), 1.0, grow[0:2, 0:D], ALU.add, ALU.mult)
                V.tensor_tensor(mr(2), mr(2), grow[0:2, D:2 * D], ALU.mult)
                V.scalar_tensor_tensor(mr(4), mr(4), 1.0, grow[0:2, 2 * D:3 * D], ALU.add, ALU.mult)
                V.tensor_tensor(mr(5), mr(5), grow[0:2, 3 * D:4 * D], ALU.mult).then_inc(mod_rows, 1)
                dve.wait_ge(mod_rows, sent(mod_rows))
            end_phase(dve, "dve")

            for l in range(DEPTH):
                dve.wait_ge(bc_in, seen(bc_in, 64))
                for i in range(NT):
                    if i >= 2:
                        dve.wait_ge(hT_sum, seen(hT_sum))
                    s = i // NL
                    norm_tile(i, bc[:, 2 * s, :], bc[:, 2 * s + 1, :], hbuf[:, i % 2, :], htmp).then_inc(h_ready, 1)
                    dve.wait_ge(h_ready, sent(h_ready))
                seen(hT_sum, 2)
                end_phase(dve, "dve")
                def rope(pe_, co, si, t):
                    n = ROPE // 2
                    V.tensor_tensor(t[:, 0], pe_[:, :, 0:n], si, ALU.mult)
                    step(V.tensor_tensor(t[:, 1], pe_[:, :, n:2 * n], si, ALU.mult))
                    V.tensor_tensor(pe_[:, :, 0:n], pe_[:, :, 0:n], co, ALU.mult)
                    step(V.tensor_tensor(pe_[:, :, n:2 * n], pe_[:, :, n:2 * n], co, ALU.mult))
                    V.tensor_tensor(pe_[:, :, 0:n], pe_[:, :, 0:n], t[:, 1], ALU.subtract)
                    return V.tensor_tensor(pe_[:, :, n:2 * n], pe_[:, :, n:2 * n], t[:, 0], ALU.add)

                for i in range(NT):
                    zt, zz = za[:, i, :], zn[:, i % 2, :]
                    V.tensor_tensor_reduce(zz[:, 0:QL], zt[:, 0:QL], zt[:, 0:QL], 1.0, 0.0, ALU.mult, ALU.add, ssq[:, 0:1])
                    step(V.tensor_tensor_reduce(zz[:, QL:QL + KVL], zt[:, QL:QL + KVL], zt[:, QL:QL + KVL], 1.0, 0.0, ALU.mult, ALU.add, ssq[:, 1:2]))
                    V.tensor_scalar(root[:, 0:1], ssq[:, 0:1], 1.0 / QL, EPS, ALU.mult, ALU.add)
                    power(V.tensor_scalar(root[:, 1:2], ssq[:, 1:2], 1.0 / KVL, EPS, ALU.mult, ALU.add))
                    V.tensor_scalar(zz[:, 0:QL], zt[:, 0:QL], root[:, 0:1], None, ALU.mult)
                    V.tensor_scalar(zz[:, QL:QL + KVL], zt[:, QL:QL + KVL], root[:, 1:2], None, ALU.mult).then_inc(zn_ready, 1)
                    dve.wait_ge(zn_ready, sent(zn_ready))
                    k_pe = zt[:, QL + KVL:MLA_IN].rearrange("p (a n) -> p a n", a=1)
                    if i < NL:
                        step(rope(k_pe, cos[:, i:i + 1, :], sin[:, i:i + 1, :], rtmp[:, :, 0:1, :]))
                    dve.wait_ge(qkv_raw, seen(qkv_raw))
                    last = V.tensor_copy(kk_[:, :, NOPE:QK], k_pe.broadcast_to([P, H, ROPE]))
                    if i < NL:
                        last = rope(qraw[:, :, NOPE:QK], cos[:, i:i + 1, :].broadcast_to([P, H, ROPE // 2]),
                                    sin[:, i:i + 1, :].broadcast_to([P, H, ROPE // 2]), rtmp)
                    last.then_inc(qk_ready, 1)
                    dve.wait_ge(qk_ready, sent(qk_ready))
                units = [(i, h) for i in tiles_of(l) for h in range(H)]

                def finish(u):
                    i, h = units[u]
                    nk = (NT if i < NL else NT - NL) * P
                    dve.wait_ge(probsT_sum, seen(probsT_sum))
                    if u >= 2:
                        dve.wait_ge(att_sum, seen(att_sum))
                    V.tensor_copy(probsT[:, u % 2].rearrange("p k t -> p (k t)")[:, 0:nk], pb[:, 2 + u % 2, 0:nk]).then_inc(probsT_ready, 1)
                    dve.wait_ge(probsT_ready, sent(probsT_ready))
                    if h == H - 1:
                        step(V.reciprocal(rinv[:, i, :], rsum[:, i, :]))
                        dve.wait_ge(att_sum, seen(att_sum, 2))
                        V.tensor_tensor(mix[:, i, 0:H * VH].rearrange("p (h n) -> p h n", h=H), pb[:, 4 + i % 2, :].rearrange("p (h n) -> p h n", h=H),
                                        rinv[:, i, :].rearrange("p (h a) -> p h a", a=1).broadcast_to([P, H, VH]), ALU.mult).then_inc(att_ready, 1)
                        dve.wait_ge(att_ready, sent(att_ready))
                        seen(att_sum, -2)

                for u, (i, h) in enumerate(units):
                    nk = (NT if i < NL else NT - NL) * P
                    dve.wait_ge(score_sum, seen(score_sum))
                    if u >= 2:
                        dve.wait_ge(probs_ready, seen(probs_ready))
                    step(V.tensor_reduce(mrow[:, u % 2:u % 2 + 1], pb[:, u % 2, 0:nk], AX.X, ALU.max))
                    V.tensor_scalar(mrow[:, u % 2:u % 2 + 1], mrow[:, u % 2:u % 2 + 1], -MLA_SCALE, None, ALU.mult).then_inc(max_ready, 1)
                    dve.wait_ge(max_ready, sent(max_ready))
                    if u >= 1:
                        finish(u - 1)
                finish(len(units) - 1)
                seen(probs_ready, 2)
                seen(att_sum, 2)
                end_phase(dve, "dve")
                dve.wait_ge(pool_in, seen(pool_in, 48))
                for s in range(len(tiles_of(l)) // 2):
                    dve.wait_ge(pool_sum, seen(pool_sum, PG))
                    for t in range(2):
                        V.tensor_tensor(mix[:, 2 * s + t, H * VH:H * VH + PW], pb[:, 2 + 2 * s + t, 0:PW], pool_s, ALU.mult)
                end_phase(dve, "dve")
                R = rs
                dve.wait_ge(R["in"], seen(R["in"], 16 * 13))
                heads = lambda ap: ap.rearrange("p (h n) -> p h n", h=RH)
                over_heads = lambda ap: ap.rearrange("p (h a) -> p h a", a=1).broadcast_to([P, RH, RD])
                over_dirs = lambda ap: ap.rearrange("p (a n) -> p a n", a=1).broadcast_to([P, 2, RW])
                for i in range(NT):
                    zs, arr, xwa, st, kk = rb["zs"], rb["arr"], rb["xwa"], rb["st"], rb["kk"]
                    tmp = rb["T1"][:, 0, 0:2, :].rearrange("p h t -> p (h t)")
                    tmp2 = rb["T1"][:, 0, 2:4, :].rearrange("p h t -> p (h t)")
                    r_, k_, v_ = zs[:, 0:RW], zs[:, RW:2 * RW], zs[:, 2 * RW:3 * RW]
                    dve.wait_ge(R["shift_sum"], seen(R["shift_sum"]))
                    half = RIN // 2
                    V.tensor_tensor(zs[:, 0:half], pb[:, 0, 0:half], rb["mu"][:, 0:half], ALU.mult)
                    step(V.tensor_tensor(zs[:, half:RIN], pb[:, 1, 0:half], rb["mu"][:, half:RIN], ALU.mult))
                    V.tensor_tensor(zs, zs, zr[:, i, :], ALU.add).then_inc(R["zs_ready"], 1)
                    dve.wait_ge(R["zs_ready"], sent(R["zs_ready"]))
                    dve.wait_ge(R["lo_act"], seen(R["lo_act"]))
                    V.tensor_scalar(rb["lo"][:, 4 * LORA:], rb["lo"][:, 4 * LORA:], 0.5, 0.5, ALU.mult, ALU.add).then_inc(R["lo_ready"], 1)
                    dve.wait_ge(R["lo_ready"], sent(R["lo_ready"]))
                    dve.wait_ge(R["lora_sum"], seen(R["lora_sum"]))
                    V.tensor_tensor(xwa.rearrange("p a d n -> p (a d n)"), pb[:, 3:5, :].rearrange("p b n -> p (b n)"), rb["wbias"], ALU.add
                                    ).then_inc(R["xwa_ready"], 1)
                    dve.wait_ge(R["xwa_ready"], sent(R["xwa_ready"]))
                    V.tensor_copy(rb["g"][:, i, :], pb[:, 5, 0:RW])
                    step(V.tensor_tensor(kk, k_, rb["k_k"], ALU.mult))
                    step(V.tensor_tensor(tmp, kk, kk, ALU.mult))
                    step(V.tensor_reduce(st[:, 0:RH], heads(tmp), AX.X, ALU.add))
                    power(V.tensor_scalar(root[:, 0:RH], st[:, 0:RH], 1e-24, None, ALU.max))
                    V.tensor_tensor(heads(kk), heads(kk), over_heads(root[:, 0:RH]), ALU.mult)
                    dve.wait_ge(R["th_ready"], seen(R["th_ready"]))
                    V.tensor_scalar(xwa[:, 1], xwa[:, 1], 1.0, 0.5, ALU.add, ALU.mult)
                    last = V.tensor_scalar(xwa[:, 0], xwa[:, 0], 1.0, 0.5 * DECAY, ALU.add, ALU.mult)
                    last.then_inc(R["lw_ready"], 1)
                    dve.wait_ge(R["lw_ready"], sent(R["lw_ready"]))
                    V.tensor_tensor(arr[:, 2], xwa[:, 1], over_dirs(kk), ALU.mult)
                    step(V.scalar_tensor_tensor(arr[:, 3], xwa[:, 1], -1.0, over_dirs(rb["k_a"]), ALU.add, ALU.mult))
                    V.tensor_tensor(tmp, r_, rb["r_k"], ALU.mult)
                    step(V.scalar_tensor_tensor(arr[:, 3], arr[:, 3], 1.0, over_dirs(k_), ALU.add, ALU.mult))
                    step(V.tensor_tensor(tmp2, arr[:, 3, 0, :], arr[:, 3, 1, :], ALU.add))
                    step(V.tensor_tensor(tmp, tmp, tmp2, ALU.mult))
                    step(V.tensor_reduce(st[:, RH:2 * RH], heads(tmp), AX.X, ALU.add))
                    V.tensor_tensor(heads(rb["bonus"][:, i, :]), heads(v_), over_heads(st[:, RH:2 * RH]), ALU.mult)
                    dve.wait_ge(R["cum_sum"], seen(R["cum_sum"]))
                    dve.wait_ge(R["eL_ready"], seen(R["eL_ready"]))
                    V.tensor_tensor(rb["s2"], pb[:, 6, :].rearrange("p (d n) -> p d n", d=2), xwa[:, 0], ALU.subtract).then_inc(R["Lx_ready"], 1)
                    dve.wait_ge(R["Lx_ready"], sent(R["Lx_ready"]))
                    V.tensor_tensor(arr[:, 1], arr[:, 1], over_dirs(r_), ALU.mult)
                    V.tensor_tensor(arr[:, 2], arr[:, 2], rb["s1"], ALU.mult)
                    V.tensor_tensor(arr[:, 3], arr[:, 3], rb["s1"], ALU.mult)
                    dve.wait_ge(R["eLx_ready"], seen(R["eLx_ready"]))
                    V.tensor_tensor(arr[:, 0], arr[:, 0], over_dirs(kk), ALU.mult).then_inc(R["arr_ready"], 1)
                    dve.wait_ge(R["arr_ready"], sent(R["arr_ready"]))
                    for d in range(2):
                        dve.wait_ge(R["mats_sum"], seen(R["mats_sum"]))
                        lv0 = lambda dd: levels[:, dd, 0:1, :].broadcast_to([P, NPAIR, P])
                        m2 = masks[:, d].rearrange("p m t -> p (m t)").rearrange("p (a n) -> p a n", a=1).broadcast_to([P, NPAIR, 2 * P])
                        for r in range(2):
                            mine = lambda nm: rb[nm][:, d].rearrange("p (q r) t -> p r q t", r=2)[:, r]
                            mine2 = lambda nm: rb[nm][:, d].rearrange("p (q r) m t -> p r q (m t)", r=2)[:, r]
                            lg = pb[:, r, :].rearrange("p (q n) -> p q n", q=2)
                            mg = pb[:, 2 + r, :].rearrange("p (q n) -> p q n", q=2)
                            V.tensor_tensor(mine("X"), pb[:, 4 + r, 0:2 * P].rearrange("p (q t) -> p q t", q=2), lv0(d), ALU.mult)
                            V.tensor_tensor(mine("XT"), lg[:, :, 0:P], lv0(1 - d), ALU.mult)
                            V.tensor_tensor(mine2("LG"), lg, m2, ALU.mult)
                            last = V.tensor_tensor(mine2("MG"), mg, m2, ALU.mult)
                        step(last)
                        eye = ident.rearrange("p (a t) -> p a t", a=1).broadcast_to([P, RH, P])
                        V.tensor_tensor(rb["X"][:, d], rb["X"][:, d], eye, ALU.add)
                        last = V.tensor_tensor(rb["XT"][:, d], rb["XT"][:, d], eye, ALU.add)
                        last.then_inc(R["mats_ready"], 1)
                        dve.wait_ge(R["mats_ready"], sent(R["mats_ready"]))
                    for d in range(2):
                        dve.wait_ge(R["mv_sum"], seen(R["mv_sum"]))
                        V.tensor_copy(rb["KMV"][:, d, :, 0, :], heads(arr[:, 0, d, :]))
                        V.tensor_copy(rb["KMV"][:, d, :, 1, :], heads(pb[:, 6 + d, 0:RW])).then_inc(R["kmv_ready"], 1)
                        dve.wait_ge(R["kmv_ready"], sent(R["kmv_ready"]))
                    for lv in range(1, 6):
                        for d in range(2):
                            dve.wait_ge(R["t1_sum"], seen(R["t1_sum"]))
                            V.tensor_tensor(rb["T1"][:, d], pb[:, 4 + d, :].rearrange("p (h t) -> p h t", h=RH),
                                            levels[:, d, lv:lv + 1, :].broadcast_to([P, RH, P]), ALU.mult).then_inc(R["t1_ready"], 1)
                            dve.wait_ge(R["t1_ready"], sent(R["t1_ready"]))
                        for d in range(2):
                            dve.wait_ge(R["x_sum"], seen(R["x_sum"]))
                            if lv < 5:
                                V.tensor_tensor(rb["X"][:, d], pb[:, d, :].rearrange("p (h t) -> p h t", h=RH), rb["X"][:, d], ALU.add)
                            V.tensor_tensor(rb["XT"][:, d], pb[:, 2 + d, :].rearrange("p (h t) -> p h t", h=RH), rb["XT"][:, d], ALU.add
                                            ).then_inc(R["x_ready"], 1)
                            dve.wait_ge(R["x_ready"], sent(R["x_ready"]))
                    for d in range(2):
                        dve.wait_ge(R["nx_sum"], seen(R["nx_sum"]))
                        V.tensor_scalar(rb["nX"][:, d].rearrange("p m h n -> p h m n"), pb[:, 4 + d, :].rearrange("p (h m n) -> p h m n", h=RH, m=2),
                                        -1.0, None, ALU.mult).then_inc(R["nx_ready"], 1)
                        dve.wait_ge(R["nx_ready"], sent(R["nx_ready"]))
                    dve.wait_ge(R["fin_sum"], seen(R["fin_sum"]))
                    V.tensor_copy(rb["YV"][:, i, :], pb[:, 0, 0:RW])
                    V.tensor_tensor(rb["RQT"].rearrange("p d q t -> p (d q) t")[:, :, i * P:(i + 1) * P], pb[:, 1, :].rearrange("p (a t) -> p a t", a=4),
                                    rb["arrT"].rearrange("p d q a t -> p (d q) a t")[:, :, 1, :], ALU.add)
                    eye2 = c_("eye2").rearrange("p (a k) -> p a k", a=1)
                    for c in range(2):
                        cc = 2 * i + c
                        V.tensor_tensor(rb["TT"].rearrange("p d q c k -> p (d q) c k")[:, :, cc, :], pb[:, 2 + 2 * c, 0:4 * C].rearrange("p (a k) -> p a k", a=4),
                                        eye2.broadcast_to([P, 4, C]), ALU.add)
                        last = V.tensor_tensor(rb["W"].rearrange("p d q c k -> p (d q) c k")[:, :, cc, :], pb[:, 3 + 2 * c, 0:4 * C].rearrange("p (a k) -> p a k", a=4),
                                               rb["AC"].rearrange("p d q c -> p (d q) c")[:, :, cc:cc + 1].broadcast_to([P, 4, C]), ALU.mult)
                    last.then_inc(R["fin_ready"], 1)
                    dve.wait_ge(R["fin_ready"], sent(R["fin_ready"]))
                for d in range(2):
                    c0, c1 = ORDER[d][0], ORDER[d][1]
                    V.tensor_copy(rb["Z"][:, d, :, c1, :], rb["W"][:, d, :, c0, :]).then_inc(R["chain_ready"], 1)
                    dve.wait_ge(R["chain_ready"], sent(R["chain_ready"]))
                for n in range(1, NC - 1):
                    for d in range(2):
                        dve.wait_ge(R["chain_sum"], seen(R["chain_sum"]))
                        cp, cn = ORDER[d][n], ORDER[d][n + 1]
                        for q in range(NPAIR):
                            last = V.scalar_tensor_tensor(rb["Z"][:, d, q, cn, :], pb[:, d, q * RD:(q + 1) * RD], rb["AC"][:, d, q, cp:cp + 1],
                                                          rb["W"][:, d, q, cp, :], ALU.mult, ALU.add)
                        last.then_inc(R["chain_ready"], 1)
                        dve.wait_ge(R["chain_ready"], sent(R["chain_ready"]))
                Y = rb["s1"].rearrange("p d n -> p (d n)")[:, 0:RW]
                SQ = rb["s2"].rearrange("p d n -> p (d n)")[:, 0:RW]
                st = rb["st"]
                for i in tiles_of(l):
                    dve.wait_ge(R["inter_sum"], seen(R["inter_sum"]))
                    for r in range(2):
                        by_pair = lambda ap: ap.rearrange("p (q r n) -> p r q n", r=2, n=RD)[:, r]
                        last = V.tensor_tensor(by_pair(Y), pb[:, 4 + 2 * (i % 2) + r, 0:NPAIR * RD].rearrange("p (q n) -> p q n", n=RD),
                                               by_pair(rb["YV"][:, i, :]), ALU.add)
                    last.then_inc(R["inter_used"], 1)
                    dve.wait_ge(R["inter_used"], sent(R["inter_used"]))
                    step(V.tensor_reduce(st[:, 0:RH], heads(Y), AX.X, ALU.add))
                    step(V.tensor_scalar(st[:, 0:RH], st[:, 0:RH], -1.0 / RD, None, ALU.mult))
                    step(V.tensor_tensor(heads(Y), heads(Y), over_heads(st[:, 0:RH]), ALU.add))
                    step(V.tensor_tensor(SQ, Y, Y, ALU.mult))
                    step(V.tensor_reduce(st[:, RH:2 * RH], heads(SQ), AX.X, ALU.add))
                    step(V.tensor_tensor(heads(Y), heads(Y), over_heads(inv_root(st[:, RH:2 * RH], RD, GN_EPS)), ALU.mult))
                    step(V.tensor_tensor(Y, Y, rb["ln_w"], ALU.mult))
                    step(V.tensor_tensor(Y, Y, rb["ln_b"], ALU.add))
                    step(V.tensor_tensor(Y, Y, rb["bonus"][:, i, :], ALU.add))
                    step(V.tensor_tensor(mix[:, i, H * VH + PW:D], Y, rb["g"][:, i, :], ALU.mult))
                end_phase(dve, "dve")
                dve.wait_ge(w_out_in, seen(w_out_in, 96))
                for i in tiles_of(l):
                    dve.wait_ge(y_sq, seen(y_sq))
                    residual(i, pb[:, 4 + 2 * (i % 2):6 + 2 * (i % 2), :].rearrange("p b n -> p (b n)"), gbc[:, i // NL, :], ytmp).then_inc(y_used, 1)
                    dve.wait_ge(y_used, sent(y_used))
                end_phase(dve, "dve")
                nt = len(tiles_of(l))
                dve.wait_ge(ms["in"], seen(ms["in"], 16 * (5 + 2 * (nt // 2))))
                step(V.memset(zero64, 0.0))
                iota = c_("iota")
                for i in range(nt):
                    if i >= 2:
                        dve.wait_ge(ms["h_out"], 16 * (sum(len(tiles_of(a)) for a in range(l)) + i - 1))
                        dve.wait_ge(hT_sum, seen(hT_sum))
                    s = i // NL
                    norm_tile(i, mbc[:, 2 * s, :], mbc[:, 2 * s + 1, :], mh[:, i % 2, :], mtmp).then_inc(h_ready, 1)
                    dve.wait_ge(h_ready, sent(h_ready))
                    dve.wait_ge(ms["ex_ready"], seen(ms["ex_ready"]))
                    step(V.tensor_scalar(sc_, ex, 1.0, None, ALU.add))
                    step(V.reciprocal(sc_, sc_))
                    step(V.tensor_tensor(sel, sc_, rbias, ALU.add))
                    for g in range(NG):
                        last = V.max(g8[:, g, :], sel[:, g * EG:(g + 1) * EG])
                    step(last)
                    step(V.tensor_tensor(small8[:, 0, :], g8[:, :, 0], g8[:, :, 1], ALU.add))
                    step(V.max(small8[:, 1, :], small8[:, 0, :]))
                    step(V.max_index(idx8, small8[:, 1, :], small8[:, 0, :]))
                    step(V.tensor_copy(small8[:, 2, :], idx8))

                    def chosen(dst, n, count):
                        q = eq[:, 0:n * count].rearrange("p (n k) -> p n k", n=n)
                        step(V.tensor_tensor(q, iota[:, 0:n].rearrange("p (n a) -> p n a", a=1).broadcast_to([P, n, count]),
                                             small8[:, 2:3, 0:count].broadcast_to([P, n, count]), ALU.is_equal))
                        step(V.tensor_reduce(dst, q, AX.X, ALU.add))

                    chosen(small8[:, 3, :], NG, TG)
                    step(V.tensor_scalar(small8[:, 3, :], small8[:, 3, :], -1.0, 1e30, ALU.add, ALU.mult))
                    step(V.tensor_tensor(sel.rearrange("p (g n) -> p g n", g=NG), sel.rearrange("p (g n) -> p g n", g=NG),
                                         small8[:, 3, :].rearrange("p (g a) -> p g a", a=1).broadcast_to([P, NG, EG]), ALU.add))
                    step(V.max(small8[:, 1, :], sel))
                    step(V.max_index(idx8, small8[:, 1, :], sel))
                    step(V.tensor_copy(small8[:, 2, :], idx8))
                    chosen(mask[:, i, :], E, TOPK)
                    step(V.tensor_tensor(gates, sc_, mask[:, i, :], ALU.mult))
                    step(V.tensor_reduce(small8[:, 4, 0:1], gates, AX.X, ALU.add))
                    step(V.reciprocal(small8[:, 4, 0:1], small8[:, 4, 0:1]))
                    step(V.tensor_scalar(gates, gates, small8[:, 4, 0:1], ROUTED, ALU.mult, ALU.mult))
                    step(V.tensor_tensor_scan(incl, mask[:, i, :], zero64, 0.0, ALU.add, ALU.add))
                    step(V.tensor_tensor(incl, incl, mask[:, i, :], ALU.mult))
                    q = eq[:, 0:TOPK * E].rearrange("p (k n) -> p k n", k=TOPK)
                    step(V.tensor_tensor(q, incl.rearrange("p (a n) -> p a n", a=1).broadcast_to([P, TOPK, E]),
                                         iota[:, 1:TOPK + 1].rearrange("p (k a) -> p k a", a=1).broadcast_to([P, TOPK, E]), ALU.is_equal))
                    step(V.tensor_tensor(q, q, gates.rearrange("p (a n) -> p a n", a=1).broadcast_to([P, TOPK, E]), ALU.mult))
                    step(V.tensor_reduce(gk[:, i, 0:TOPK], q, AX.X, ALU.add))
                    V.tensor_copy(meta[:, i, :, 0], c_("tok").broadcast_to([P, E]))
                    V.memset(meta[:, i, :, 1], float(i))
                    V.tensor_scalar(meta[:, i, :, 2], incl, -1.0, None, ALU.add)
                    V.memset(meta[:, i, :, 3], 1.0)
                    step(V.tensor_copy(mask_bf[:, i, :], mask[:, i, :]))
                    dve.wait_ge(ms["shg_ready"], seen(ms["shg_ready"]))
                    V.tensor_tensor(sh_act.rearrange("p (k q) -> p q k", k=2), sh_sg.rearrange("p (q k) -> p q k", k=2),
                                    pb[:, 5, FF:2 * FF].rearrange("p (q k) -> p q k", k=2), ALU.mult).then_inc(ms["act_ready"], 1)
                    dve.wait_ge(ms["act_ready"], sent(ms["act_ready"]))
                    V.tensor_copy(small8[:, 5, 0:1], small8[:, 4, 0:1]).then_inc(ms["mask_ready"], 1)
                    dve.wait_ge(ms["mask_ready"], sent(ms["mask_ready"]))
                seen(hT_sum, 2)
                dve.wait_ge(ms["pos_sum"], seen(ms["pos_sum"]))
                step(V.scalar_tensor_tensor(posm[:, 0:nt, :], pb[:, 0, 0:nt * E].rearrange("p (i e) -> p i e", i=nt), 1.0, mask[:, 0:nt, :], ALU.add, ALU.mult))
                step(V.tensor_scalar(posm[:, 0:nt, :], posm[:, 0:nt, :], -1.0, None, ALU.add))
                step(V.tensor_reduce(cntf, pb[:, 0, nt * E:(nt + 1) * E], AX.X, ALU.max))
                V.tensor_copy(cnti, cntf).then_inc(ms["count_ready"], 1)
                end_phase(dve, "dve")

                def slots(b, ready, step):
                    step(V.tensor_scalar(posb[:, 0:nt, :], posm[:, 0:nt, :], -float(b * CAP), None, ALU.add))
                    for i in range(nt):
                        last = V.tensor_tensor(onehot[:, i], iota[:, 0:CAP].rearrange("p (a s) -> p a s", a=1).broadcast_to([P, E, CAP]),
                                               posb[:, i, :].rearrange("p (e a) -> p e a", a=1).broadcast_to([P, E, CAP]), ALU.is_equal)
                    last.then_inc(ready, 1)

                def index_tables(step):
                    t = pb[:, 0, 0:4 * E].rearrange("p (e c) -> p e c", c=4)
                    V.tensor_scalar(tabf[:, 0, :], t[:, :, 1], float(P), None, ALU.mult)
                    step(V.tensor_scalar(tabf[:, 1, :], t[:, :, 3], -OUT_OF_RANGE, OUT_OF_RANGE, ALU.mult, ALU.add))
                    step(V.tensor_tensor(tabf[:, 0, :], t[:, :, 0], tabf[:, 0, :], ALU.add))
                    step(V.scalar_tensor_tensor(tabf[:, 2, :], tabf[:, 0, :], float(TOPK), tabf[:, 1, :], ALU.mult, ALU.add))
                    step(V.tensor_tensor(tabf[:, 2, :], t[:, :, 2], tabf[:, 2, :], ALU.add))
                    step(V.tensor_tensor(tabf[:, 0, :], tabf[:, 0, :], tabf[:, 1, :], ALU.add))
                    V.tensor_copy(gi, tabf[:, 0, :])
                    return V.tensor_copy(si, tabf[:, 2, :])

                slots(0, ms["onehot_ready"], step)
                dve.wait_ge(ms["tab_sum"], seen(ms["tab_sum"]))
                V.memset(gx, 0.0)
                step(index_tables(step))
                end_phase(dve, "dve")

                def dve_walk(S, base):
                    def body(it, first, last_):
                        for j in range(4):
                            n = it * 4 + j + base
                            dve.wait_ge(S.sg_ready, n + 1)
                            if not (first and j < 2):
                                dve.wait_ge(S.aT_sum, n - 1)
                            V.tensor_tensor(actx[:, j % 2].rearrange("p (k q) -> p q k", k=2), sg[:, j % 2].rearrange("p (q k) -> p q k", k=2),
                                            pb[:, 2 + j % 2, FF:2 * FF].rearrange("p (q k) -> p q k", k=2), ALU.mult).then_inc(S.act_ready, 1)
                            dve.wait_ge(S.aT_sum, n + 1)
                            if not (first and j < 2):
                                dve.wait_ge(S.dn_sum, n - 1)
                            V.tensor_copy(aT[:, j % 2].rearrange("p k t -> p (k t)"), pb[:, 4, 0:2 * P]).then_inc(S.aT_ready, 1)
                            dve.wait_ge(S.dn_sum, n + 1)
                            if not (first and j < 2):
                                dve.wait_ge(S.y_out[j % 2], 16 * (base // 2 + 2 * it + j // 2))
                            V.tensor_copy(yx[:, j % 2], pb[:, 5:7, :].rearrange("p b n -> p (b n)")).then_inc(S.y_ready, 1)
                    walk(dve, body)

                dve_walk(main, E * l)
                end_phase(dve, "dve")
                dve.wait_ge(ms["count_ready"], l + 1)
                most = dve.value_load(cnti[0:1, 0:1], min_val=0, max_val=NT * P)
                with dve.If(most > CAP):
                    xstep = lambda ins: link(dve, ins, x_step[l])
                    for b in range(1, nt):
                        if b > 1:
                            dve.wait_ge(x_chain[l], x_at(b, 0) - X_TAB)
                        slots(b, x_chain[l], xstep)
                        dve.wait_ge(x_chain[l], x_at(b, 0) - 1)
                        xstep(index_tables(xstep))
                        dve.engine_nop().then_inc(x_chain[l], 1)
                        with dve.Fori(0, E) as e:
                            dve.wait_ge(x_chain[l], x_at(b, e, X_SILU))
                            V.tensor_tensor(actx[:, 0].rearrange("p (k q) -> p q k", k=2), sg[:, 0].rearrange("p (q k) -> p q k", k=2),
                                            pb[:, 2, FF:2 * FF].rearrange("p (q k) -> p q k", k=2), ALU.mult).then_inc(x_chain[l], 1)
                            dve.wait_ge(x_chain[l], x_at(b, e, X_AT))
                            V.tensor_copy(aT[:, 0].rearrange("p k t -> p (k t)"), pb[:, 4, 0:2 * P]).then_inc(x_chain[l], 1)
                            dve.wait_ge(x_chain[l], x_at(b, e, X_DN))
                            V.tensor_copy(yx[:, 0], pb[:, 5:7, :].rearrange("p b n -> p (b n)")).then_inc(x_chain[l], 1)
                end_phase(dve, "dve")
                dve.wait_ge(ms["y_in"], seen(ms["y_in"], 16 * (nt // 2)))
                for i in range(nt):
                    dve.wait_ge(ms["y_in"], seen(ms["y_in"], 16))
                    for k in range(TOPK):
                        last = V.scalar_tensor_tensor(acc[:, i, :], ybuf[:, i % 2, k, :], gk[:, i, k:k + 1], acc[:, i, :], ALU.mult, ALU.add)
                        if k < TOPK - 1:
                            step(last)
                    last.then_inc(ms["y_used"], 1)
                    dve.wait_ge(ms["y_used"], sent(ms["y_used"]))
                    step(V.tensor_tensor_reduce(ftmp, acc[:, i, :], acc[:, i, :], 1.0, 0.0, ALU.mult, ALU.add, ssq[:, i:i + 1]))
                    step(residual(i, acc[:, i, :], fbc[:, i // NL, :], ftmp))
                end_phase(dve, "dve")

        @block.gpsimd
        def _(pool):
            seen = Seen()

            def roots(n):
                for _ in range(n):
                    pool.wait_ge(root_in, seen(root_in))
                    nc.gpsimd.tensor_tensor(root, root, minus_half, ALU.pow).then_inc(root_out, 1)

            end_phase(pool, "pool")
            for l in range(DEPTH):
                for k in range(1, 6):
                    if k == 4:
                        nc.gpsimd.memset(rb["loraW"], 0.0).then_inc(rs["zero"], 1)
                    nt = len(tiles_of(l))
                    roots({1: NT, 2: NT, 3: 0, 4: NT + nt, 5: nt}[k])
                    end_phase(pool, "pool")
                roots(len(tiles_of(l)))
                end_phase(pool, "pool")
                end_phase(pool, "pool")

                def row_walk(S, base):
                    def gather(e, n, j):
                        nc.gpsimd.tensor_copy(idx_now[:, 2 * j:2 * j + 1], gi[:, bass.ds(e, 1)]).then_inc(S.gather_idx, 1)
                        pool.wait_ge(S.gather_idx, n + 1)
                        pool.sem_inc(wait_held, 1)
                        nc.gpsimd.indirect_dma_start(gx[:, j, :], None, h_dram, bass.IndirectOffsetOnAxis(ap=idx_now[:, 2 * j:2 * j + 1], axis=0),
                                                     bounds_check=NT * P - 1, oob_is_err=False).then_inc(S.g_in[j], 16)

                    def body(it, first, last_):
                        if first:
                            for a in range(2):
                                gather(a, base + a, a)
                        for j in range(4):
                            e = it * 4 + j
                            n = e + base
                            if not (last_ and j >= 2):
                                pool.wait_ge(S.gT_sum, n + 1)
                                gather(e + 2, n + 2, j % 2)
                            pool.wait_ge(S.y_ready, n + 1)
                            sl = idx_now[:, 2 * (j % 2) + 1:2 * (j % 2) + 2]
                            if not (first and j < 2):
                                pool.wait_ge(S.y_out[j % 2], 16 * (base // 2 + 2 * it + j // 2))
                            nc.gpsimd.tensor_copy(sl, si[:, bass.ds(e, 1)]).then_inc(S.scatter_idx, 1)
                            pool.wait_ge(S.scatter_idx, n + 1)
                            pool.sem_inc(wait_held, 1)
                            nc.gpsimd.indirect_dma_start(y_dram, bass.IndirectOffsetOnAxis(ap=sl, axis=0), yx[:, j % 2, :], None,
                                                         bounds_check=NT * P * TOPK - 1, oob_is_err=False).then_inc(S.y_out[j % 2], 16)
                    walk(pool, body)
                    for j in range(2):
                        pool.wait_ge(S.y_out[j], 16 * (base // 2 + E // 2))

                row_walk(main, E * l)
                end_phase(pool, "pool")
                pool.wait_ge(ms["count_ready"], l + 1)
                most = pool.value_load(cnti[0:1, 0:1], min_val=0, max_val=NT * P)
                with pool.If(most > CAP):
                    for b in range(1, len(tiles_of(l))):
                        with pool.Fori(0, E) as e:
                            pool.wait_ge(x_chain[l], x_at(b, e))
                            nc.gpsimd.tensor_copy(idx_now[:, 0:1], gi[:, bass.ds(e, 1)]).then_inc(x_chain[l], 1)
                            pool.wait_ge(x_chain[l], x_at(b, e, X_IDX))
                            pool.sem_inc(wait_held, 1)
                            nc.gpsimd.indirect_dma_start(gx[:, 0, :], None, h_dram, bass.IndirectOffsetOnAxis(ap=idx_now[:, 0:1], axis=0),
                                                         bounds_check=NT * P - 1, oob_is_err=False).then_inc(x_rows[l], 16)
                            pool.wait_ge(x_chain[l], x_at(b, e, X_Y))
                            nc.gpsimd.tensor_copy(idx_now[:, 1:2], si[:, bass.ds(e, 1)]).then_inc(x_chain[l], 1)
                            pool.wait_ge(x_chain[l], x_at(b, e, X_SIDX))
                            pool.sem_inc(wait_held, 1)
                            nc.gpsimd.indirect_dma_start(y_dram, bass.IndirectOffsetOnAxis(ap=idx_now[:, 1:2], axis=0), yx[:, 0, :], None,
                                                         bounds_check=NT * P * TOPK - 1, oob_is_err=False).then_inc(x_out[l], 16)
                            pool.wait_ge(x_out[l], 16 * ((b - 1) * E + e + 1))
                            pool.sem_inc(x_chain[l], 1)
                end_phase(pool, "pool")
                roots(len(tiles_of(l)))
                end_phase(pool, "pool")



_INS = ['x', 'c', 'ctx', 'c_ctx', 'ada_w', 'ada_b', 'pre_mix_g', 'post_mix_g', 'pre_ffn_g', 'post_ffn_g', 'w_in', 'w_out',
        'mla_q_norm', 'mla_w_q_b', 'mla_kv_norm', 'mla_w_kv_b', 'pool_w', 'pool_scale', 'rwkv_mu', 'rwkv_w0', 'rwkv_w2',
        'rwkv_a0', 'rwkv_a2', 'rwkv_g2', 'rwkv_k_k', 'rwkv_k_a', 'rwkv_r_k', 'rwkv_ln_w', 'rwkv_ln_b', 'router_w',
        'router_bias', 'exp_w_gate', 'exp_w_up', 'exp_w_down', 'sh_w_gate', 'sh_w_up', 'sh_w_down']


def kernel(**inputs):
    import numpy as _np
    import concourse.bacc as _bacc
    from concourse import mybir as _mybir
    from concourse.bass_utils import run_bass_kernel_spmd as _run

    nc = _bacc.Bacc("TRN2", target_bir_lowering=False, num_devices=1)
    arrays, args = {}, {}
    const, _, pool = lay_constants()
    for name, a in [(n, inputs[n]) for n in _INS] + [("shape_consts", const), ("pool_matrix", pool)]:
        a = _np.ascontiguousarray(a)
        arrays[f"in_{name}_dram"] = a
        args[name] = nc.dram_tensor(f"in_{name}_dram", a.shape, _mybir.dt.from_np(a.dtype), kind="ExternalInput").ap()
    out = nc.dram_tensor("out_0_dram", (1, SEQ, D), _mybir.dt.float32, kind="ExternalOutput").ap()
    trunk_kernel(nc, args, out)
    r = _run(nc, [arrays], core_ids=[0])
    return r.results[0]["out_0_dram"]
```

```python
from contextlib import ExitStack

import numpy as np
import concourse.bass as bass
from concourse import mybir

ALU = mybir.AluOpType
ACT = mybir.ActivationFunctionType
AX = mybir.AxisListType
F32 = mybir.dt.float32
BF16 = mybir.dt.bfloat16
I32 = mybir.dt.int32
U32 = mybir.dt.uint32

P = 128
D = 1024
KD = D // P
SEQ, CTX = 256, 256
NT = (SEQ + CTX) // P
NL = SEQ // P
DEPTH = 2
GRID_W = 64
EPS = 1e-6
H, NOPE, ROPE, VH = 8, 64, 32, 64
QK = NOPE + ROPE
QL, KVL = 384, 256
MLA_IN = QL + KVL + ROPE
MLA_SCALE = QK ** -0.5
WINDOWS = (2, 4, 8, 16)
PG, PC = 4, 64
PW = PG * PC
RH, RD = 4, 64
RW = RH * RD
LORA, GLORA = 32, 64
RIN = 3 * RW + 4 * LORA + GLORA
INW = MLA_IN + PW + RIN
GN_EPS = 64e-5
C = 64
NPAIR = RH // 2
E, TOPK, FF, NG, TG = 64, 6, 256, 8, 4
EG = E // NG
ROUTED = 2.5
CAP = 128
OUT_OF_RANGE = 65536.0
DECAY = -float(np.exp(-0.5))


def lay_constants():
    t = np.arange(P)
    same = (t[:, None] // C) == (t[None, :] // C)
    parts = {}
    parts["ident"] = np.eye(P)
    strict = (t[:, None] < t[None, :]) & same
    incl = (t[:, None] <= t[None, :]) & same
    parts["mask_st"] = np.concatenate([strict, incl, strict.T, incl.T], 1)
    parts["cum"] = np.concatenate([incl, incl.T], 1)
    lv = []
    for d in range(2):
        for s in [1, 2, 4, 8, 16, 32]:
            blk = (t[:, None] // (2 * s)) == (t[None, :] // (2 * s))
            m = blk & ((t[:, None] // s) % 2 == 1) & ((t[None, :] // s) % 2 == 0)
            lv.append(-(m if d == 0 else m.T).astype(np.float64))
    parts["levels"] = np.concatenate(lv, 1)
    parts["chunk_of"] = np.stack([t < C, t >= C], 1)
    tt = np.arange(SEQ)
    sh = 0.5 * (np.abs(tt[:, None] - tt[None, :]) == 1) - np.eye(SEQ)
    parts["shift"] = np.concatenate([sh[0:P], sh[P:SEQ]], 1)
    row, col = tt // GRID_W, tt % GRID_W
    inv = np.float32(10000.0) ** (-np.arange(ROPE // 4, dtype=np.float32) / np.float32(ROPE // 4))
    ang = np.concatenate([row[:, None].astype(np.float32) * inv, col[:, None].astype(np.float32) * inv], 1)
    for nm, f in (("cos", np.cos), ("sin", np.sin)):
        v = f(ang.astype(np.float32))
        parts[nm] = np.concatenate([v[0:P], v[P:SEQ]], 1)
    parts["iota"] = np.broadcast_to(np.arange(P)[None, :], (P, P))
    parts["before"] = t[:, None] < t[None, :]
    parts["tok"] = t[:, None]
    parts["eye2"] = np.tile(np.eye(C), (2, 1))
    parts["ones"] = np.ones((P, P))
    at, cols, n = {}, [], 0
    for k, v in parts.items():
        v = np.asarray(v, np.float32)
        at[k] = (n, n + v.shape[1])
        n += v.shape[1]
        cols.append(v)
    pool = []
    for w in WINDOWS:
        lo, hi = np.clip(tt - w // 2, 0, SEQ), np.clip(tt + w // 2, 0, SEQ)
        m = ((tt[None, :] >= lo[:, None]) & (tt[None, :] < hi[:, None])) / (hi - lo)[:, None] - np.eye(SEQ)
        pool.append(m.T)
    pool = np.stack(pool, 0).reshape(PG, 2, P, SEQ).transpose(2, 1, 0, 3).reshape(P, 2 * PG * SEQ)
    return np.ascontiguousarray(np.concatenate(cols, 1)), at, np.ascontiguousarray(pool, np.float32)


class Seen:

    def __init__(self):
        self.n = {}

    def __call__(self, sem, by=1):
        self.n[id(sem)] = self.n.get(id(sem), 0) + by
        return self.n[id(sem)]


class Region:

    def __init__(self, arena, start, end):
        self.arena, self.at, self.end = arena, start, end

    def take(self, n, dt=F32):
        a = self.arena[:, self.at:self.at + n]
        self.at += n
        assert self.at <= self.end, (self.at, self.end)
        return a if dt == F32 else a.bitcast(dt)


def trunk_kernel(nc, A, out):
    const_cols, at, _ = lay_constants()
    NCONST = const_cols.shape[1]
    ctx = ExitStack()
    with ctx:
        def sem(name):
            return ctx.enter_context(nc.semaphore(name))

        mod_dram = nc.dram_tensor("mod_rows", [DEPTH, 2, 6 * D], F32).ap()
        h_dram = nc.dram_tensor("h_rows", [NT * P, D], F32).ap()
        y_dram = nc.dram_tensor("y_rows", [NT * P * TOPK, D], F32).ap()

        AR = 53100
        arena = ctx.enter_context(nc.sbuf_tensor("arena", [P, AR], F32))
        pb = ctx.enter_context(nc.psum_tensor("pb", [P, 8, 512], F32))

        fixed = Region(arena, 0, AR)
        x = fixed.take(NT * D).rearrange("p (i d) -> p i d", i=NT)
        cst = fixed.take(NCONST)
        small = fixed.take(2048)
        ones_bf = fixed.take(64, BF16)
        before_bf = fixed.take(64, BF16)
        R0 = fixed.at

        def c_(name):
            return cst[:, at[name][0]:at[name][1]]

        ident = c_("ident")
        masks = c_("mask_st").rearrange("p (d m t) -> p d m t", d=2, m=2)
        cum = c_("cum").rearrange("p (d t) -> p d t", d=2)
        levels = c_("levels").rearrange("p (d l t) -> p d l t", d=2, l=6)
        shift = c_("shift").rearrange("p (k t) -> p k t", k=2)
        cos = c_("cos").rearrange("p (i f) -> p i f", i=NL)
        sin = c_("sin").rearrange("p (i f) -> p i f", i=NL)

        sreg = Region(small, 0, 2048)
        cs = sreg.take(2 * KD).rearrange("p (k s) -> p k s", s=2)
        craw = sreg.take(2 * KD).rearrange("p (s k) -> p s k", s=2)
        ssq = sreg.take(16)
        root = sreg.take(8)
        minus_half = sreg.take(8)
        qcol = sreg.take(QL // P)
        kvcol = sreg.take(KVL // P)
        gk = sreg.take(NT * 8).rearrange("p (i k) -> p i k", i=NT)

        phase_end = sem("phase_end")
        phases = {}

        def end_phase(eng, name):
            phases[name] = phases.get(name, 0) + 1
            eng.drain().then_inc(phase_end, 1)
            eng.wait_ge(phase_end, 5 * phases[name])

        start_in = sem("start_in")
        c_in = sem("c_in")
        ada_in = [sem(f"ada_in{j}") for j in range(4)]
        ada_rows_in = sem("ada_rows_in")
        silu_c = sem("silu_c")
        ada_sum = sem("ada_sum")
        ada_row = sem("ada_row")
        mod_rows = sem("mod_rows_ready")
        mod_out = sem("mod_out")
        bc_in = sem("bc_in")
        h_ready = sem("h_ready")
        hT_sum = sem("hT_sum")
        hT_ready = sem("hT_ready")
        w_in_in = sem("w_in_in")
        z_sum = sem("z_sum")
        z_ready = sem("z_ready")
        mla_in = sem("mla_in")
        zn_ready = sem("zn_ready")
        znT_sum = sem("znT_sum")
        znT_ready = sem("znT_ready")
        qkv_sum = sem("qkv_sum")
        qkv_raw = sem("qkv_raw")
        qk_ready = sem("qk_ready")
        qkT_sum = sem("qkT_sum")
        qkT_ready = sem("qkT_ready")
        score_sum = sem("score_sum")
        max_ready = sem("max_ready")
        probs_ready = sem("probs_ready")
        probsT_sum = sem("probsT_sum")
        probsT_ready = sem("probsT_ready")
        att_sum = sem("att_sum")
        att_ready = sem("att_ready")
        pool_in = sem("pool_in")
        diff_sum = sem("diff_sum")
        diff_ready = sem("diff_ready")
        pool_sum = sem("pool_sum")
        pool_ready = sem("pool_ready")
        w_out_in = sem("w_out_in")
        mixT_sum = sem("mixT_sum")
        mixT_ready = sem("mixT_ready")
        y_sum = sem("y_sum")
        y_sq = sem("y_sq")
        y_used = sem("y_used")

        root_in = sem("root_in")
        root_out = sem("root_out")
        dve_step = sem("dve_step")
        act_step = sem("act_step")
        pool_step = sem("pool_step")
        steps = {}

        def link(eng, ins, s):
            steps[id(s)] = steps.get(id(s), 0) + 1
            ins.then_inc(s, 1)
            eng.wait_ge(s, steps[id(s)])

        r = Region(arena, R0, AR - KD * INW)
        ada_ring = r.take(4 * KD * 512).rearrange("p (j k n) -> p j k n", j=4, k=KD)
        modrow = r.take(6 * D)
        grow = r.take(4 * D)
        r = Region(arena, R0, AR - KD * INW)
        hT = r.take(KD * NT * P).rearrange("p (k t) -> p k t", k=KD)
        mix = r.take(NT * D).rearrange("p (i d) -> p i d", i=NT)
        R_ZR = r.at
        zr = r.take(NT * RIN).rearrange("p (i n) -> p i n", i=NT)
        R_RWKV = r.at
        za = r.take(NT * (INW - RIN)).rearrange("p (i n) -> p i n", i=NT)
        R1 = r.at
        htmp = r.take(D)
        hbuf = r.take(2 * D).rearrange("p (j d) -> p j d", j=2)
        bc = r.take(4 * D).rearrange("p (j d) -> p j d", j=4)
        R2 = r.at
        NY = 3
        ybuf = r.take(NY * D).rearrange("p (j d) -> p j d", j=NY)
        fbc = r.take(2 * D).rearrange("p (s d) -> p s d", s=2)
        w_in = Region(arena, AR - KD * INW, AR).take(KD * INW).rearrange("p (k n) -> p k n", k=KD)
        ZA = INW - RIN
        r = Region(arena, R2, AR - KD * INW)
        w_q = r.take(3 * H * QK).rearrange("p (k n) -> p k n", k=3)
        w_kv = r.take(2 * H * (NOPE + VH)).rearrange("p (k n) -> p k n", k=2)
        R3 = r.at
        r = Region(arena, R1, R2)
        zn = r.take(2 * (QL + KVL)).rearrange("p (j n) -> p j n", j=2)
        znT = r.take(2 * (QL + KVL)).rearrange("p (j k t) -> p j k t", j=2, k=5)
        qraw = r.take(2 * H * QK).rearrange("p (j h n) -> p j h n", j=2, h=H)
        kk_ = r.take(2 * H * QK).rearrange("p (j h n) -> p j h n", j=2, h=H)
        rtmp = r.take(2 * H * ROPE // 2).rearrange("p (j h n) -> p j h n", j=2, h=H)
        probs = r.take(2 * 512).rearrange("p (j t) -> p j t", j=2)
        mrow = r.take(2)
        rsum = r.take(NT * H).rearrange("p (i h) -> p i h", i=NT)
        rinv = r.take(NT * H).rearrange("p (i h) -> p i h", i=NT)
        NPAR = 10 * RW + RIN + 4 * RW
        r = Region(arena, R3, AR - NPAR)
        qT = r.take(H * NT * P).rearrange("p (h t) -> p h t", h=H)
        kT = r.take(H * NT * P).rearrange("p (h t) -> p h t", h=H)
        vv = r.take(NT * H * VH).rearrange("p (i n) -> p i n", i=NT)
        probsT = r.take(2 * 512).rearrange("p (j k t) -> p j k t", j=2, k=4)
        r = Region(arena, R0, R0 + KD * NT * P)
        poolm = r.take(2 * PG * SEQ).rearrange("p (k g t) -> p k g t", k=2, g=PG)
        pool_w = r.take(PG * PC).rearrange("p (g n) -> p g n", g=PG)
        pool_s = r.take(PW)
        diffT = r.take(2 * SEQ).rearrange("p (j t) -> p j t", j=2)

        r = Region(arena, R_RWKV, AR - NPAR)
        rb = {}
        UD = 2 * NPAIR
        NC = NT * 2
        hr = Region(arena, R0, R0 + KD * NT * P)
        rb["TT"] = hr.take(2 * NPAIR * NC * C).rearrange("p (d q c k) -> p d q c k", d=2, q=NPAIR, c=NC)
        rb["W"] = hr.take(2 * NPAIR * NC * C).rearrange("p (d q c k) -> p d q c k", d=2, q=NPAIR, c=NC)
        rb["Z"] = r.take(2 * NPAIR * NC * C).rearrange("p (d q c k) -> p d q c k", d=2, q=NPAIR, c=NC)
        rb["RQT"] = r.take(2 * NPAIR * NT * P).rearrange("p (d q t) -> p d q t", d=2, q=NPAIR)
        rb["AC"] = r.take(2 * NPAIR * NC).rearrange("p (d q c) -> p d q c", d=2, q=NPAIR)
        rb["YV"] = r.take(NT * RW).rearrange("p (i n) -> p i n", i=NT)
        rb["g"] = r.take(NT * RW).rearrange("p (i n) -> p i n", i=NT)
        rb["bonus"] = r.take(NT * RW).rearrange("p (i n) -> p i n", i=NT)
        rp = Region(arena, AR - NPAR, AR)
        rb["loraW"] = rp.take(4 * RW)
        rb["g2"] = rp.take(RW)
        rb["mu"] = rp.take(RIN)
        rb["wbias"] = rp.take(4 * RW)
        for nm in ("k_k", "k_a", "r_k", "ln_w", "ln_b"):
            rb[nm] = rp.take(RW)
        rb["zs2"] = r.take(2 * RIN).rearrange("p (j n) -> p j n", j=2)
        rb["lo"] = r.take(4 * LORA + GLORA)
        rb["loT"] = r.take(2 * P).rearrange("p (j t) -> p j t", j=2)
        rb["xwa"] = r.take(4 * RW).rearrange("p (a d n) -> p a d n", a=2, d=2)
        rb["kk"] = r.take(RW)
        rb["s1"] = r.take(2 * RW).rearrange("p (d n) -> p d n", d=2)
        rb["s2"] = r.take(2 * RW).rearrange("p (d n) -> p d n", d=2)
        R_DEAD = r.at
        rb["arr2"] = r.take(2 * 4 * 2 * RW).rearrange("p (j a d n) -> p j a d n", j=2, a=4, d=2)
        rb["arrT"] = r.take(4 * 2 * RW).rearrange("p (d q a t) -> p d q a t", d=2, q=NPAIR, a=4)
        rb["LG"] = r.take(2 * RH * 2 * P).rearrange("p (d h m t) -> p d h m t", d=2, h=RH, m=2)
        rb["MG"] = r.take(2 * RH * 2 * P).rearrange("p (d h m t) -> p d h m t", d=2, h=RH, m=2)
        rb["X"] = r.take(2 * RH * P).rearrange("p (d h t) -> p d h t", d=2, h=RH)
        rb["XT"] = r.take(2 * RH * P).rearrange("p (d h t) -> p d h t", d=2, h=RH)
        rb["T1"] = r.take(2 * RH * P).rearrange("p (d h t) -> p d h t", d=2, h=RH)
        rb["KMV"] = rb["X"].rearrange("p d h (m n) -> p d h m n", m=2)
        rb["tmp"] = r.take(2 * RW).rearrange("p (j n) -> p j n", j=2)
        rb["nX"] = r.take(2 * 2 * RW).rearrange("p (d m h n) -> p d m h n", d=2, m=2, h=RH)
        rb["st"] = r.take(32)
        r = Region(arena, R_DEAD, AR - NPAR)
        w_out = r.take(KD * D).rearrange("p (k n) -> p k n", k=KD)
        gbc = r.take(2 * D).rearrange("p (s d) -> p s d", s=2)
        R_OUT = r.at
        r = Region(arena, R_ZR, R_RWKV)
        mixT = r.take(2 * KD * P).rearrange("p (j k t) -> p j k t", j=2, k=KD)
        ytmp = r.take(D)

        rs = {n: sem("r_" + n) for n in (
            "in", "zero", "shift_sum", "zs_ready", "lo_ready", "loT_sum", "loT_ready", "lora_sum", "xwa_ready",
            "th_ready", "lw_ready", "cum_sum", "eL_ready", "Lx_ready", "eLx_ready", "arr_ready", "arrT_sum",
            "arrT_ready", "mats_sum", "mats_ready", "mv_sum", "kmv_ready", "t1_sum", "t1_ready", "x_sum",
            "x_ready", "nx_sum", "nx_ready", "fin_sum", "fin_ready", "chain_sum", "chain_ready", "inter_sum",
            "inter_used")}
        ORDER = [list(range(2 * NL, NC)) + list(range(2 * NL)), list(range(NC - 1, 2 * NL - 1, -1)) + list(range(2 * NL - 1, -1, -1))]
        r = Region(arena, R0 + 2 * KD * NT * P, AR)
        acc = mix
        ring = r.take(4 * 6 * D).rearrange("p (j n) -> p j n", j=4)
        ring_gu = ring[:, :, 0:4 * D].rearrange("p j (m k n) -> p j m k n", m=2, k=KD)
        ring_dn = ring[:, :, 4 * D:6 * D].rearrange("p j (k n) -> p j k n", k=2)
        r2 = Region(arena, R_RWKV, R_DEAD)
        mbc = r2.take(4 * D).rearrange("p (j d) -> p j d", j=4)
        rw = r2.take(KD * E).rearrange("p (k e) -> p k e", k=KD)
        sh_gu = r2.take(4 * D).rearrange("p (m k n) -> p m k n", m=2, k=KD)
        sh_dn = r2.take(2 * D).rearrange("p (k n) -> p k n", k=2)
        rbias = r2.take(E)
        r2 = Region(arena, R_DEAD, r.at)
        mtmp = r2.take(D)
        mh = r2.take(2 * D).rearrange("p (j d) -> p j d", j=2)
        sh_sg = r2.take(FF)
        sh_act = r2.take(FF)
        sh_aT = r2.take(2 * P).rearrange("p (k t) -> p k t", k=2)
        sc_ = r2.take(E)
        ex = r2.take(E)
        sel = r2.take(E)
        incl = r2.take(E)
        zero64 = r2.take(E)
        g8 = r2.take(NG * 8).rearrange("p (g n) -> p g n", g=NG)
        small8 = r2.take(64).rearrange("p (a n) -> p a n", n=8)
        idx8 = r2.take(8, U32)
        eq = r2.take(8 * E)
        r3 = Region(arena, R0 + 2 * KD * NT * P + 6 * D, r.at)
        tabf = r3.take(4 * E).rearrange("p (a e) -> p a e", a=4)
        posb = r3.take(NT * E).rearrange("p (i e) -> p i e", i=NT)
        onehot = r3.take(NT * E * CAP // 2, BF16).rearrange("p (i e s) -> p i e s", i=NT, e=E)
        gx = arena[:, R0:R0 + 4 * D].rearrange("p (j d) -> p j d", j=4)
        gT = r.take(2 * D).rearrange("p (j k t) -> p j k t", j=2, k=KD)
        yx = r.take(4 * D).rearrange("p (j d) -> p j d", j=4)
        sg = r.take(2 * FF).rearrange("p (j n) -> p j n", j=2)
        actx = r.take(2 * FF).rearrange("p (j n) -> p j n", j=2)
        aT = r.take(2 * 2 * P).rearrange("p (j k t) -> p j k t", j=2, k=2)
        mask = r.take(NT * E).rearrange("p (i e) -> p i e", i=NT)
        gates = r.take(E)
        posm = r.take(NT * E).rearrange("p (i e) -> p i e", i=NT)
        mask_bf = r.take(NT * E // 2, BF16).rearrange("p (i e) -> p i e", i=NT)
        meta = r.take(NT * E * 4 // 2, BF16).rearrange("p (i e c) -> p i e c", i=NT, e=E)
        gi = r.take(E, U32)
        si = r.take(E, U32)
        idx_now = r.take(8, U32)
        cntf = r.take(1)
        cnti = r.take(1, I32)
        ms = {n: sem("m_" + n) for n in ("in", "h_out", "logit_sum", "shgu_sum", "ex_ready", "shg_ready", "act_ready", "aT_sum",
                                         "aT_ready", "dn_sum", "sh_ready", "mask_ready", "pos_sum", "count_ready",
                                         "onehot_ready", "tab_sum", "tab_ready", "f_in", "y_used", "out_done")}
        y_in = [sem(f"y_in{j}") for j in range(NY)]

        class Pass:

            def __init__(self, tag):
                self.gT_sum = sem(f"{tag}_gT_sum")
                self.gT_ready = sem(f"{tag}_gT_ready")
                self.gu_sum = sem(f"{tag}_gu_sum")
                self.sg_ready = sem(f"{tag}_sg_ready")
                self.act_ready = sem(f"{tag}_act_ready")
                self.aT_sum = sem(f"{tag}_aT_sum")
                self.aT_ready = sem(f"{tag}_aT_ready")
                self.dn_sum = sem(f"{tag}_dn_sum")
                self.y_ready = sem(f"{tag}_y_ready")
                self.gather_idx = sem(f"{tag}_gather_idx")
                self.scatter_idx = sem(f"{tag}_scatter_idx")
                self.w_in = [sem(f"{tag}_w_in{j}") for j in range(4)]
                self.g_in = [sem(f"{tag}_g_in{j}") for j in range(4)]
                self.y_out = [sem(f"{tag}_y_out{j}") for j in range(4)]

        main = Pass("main")
        x_chain = [sem(f"extra{l}_chain") for l in range(DEPTH)]
        x_in = [sem(f"extra{l}_in") for l in range(DEPTH)]
        x_rows = [sem(f"extra{l}_rows") for l in range(DEPTH)]
        x_out = [sem(f"extra{l}_out") for l in range(DEPTH)]
        x_step = [sem(f"extra{l}_step") for l in range(DEPTH)]
        X_TAB = 3
        (X_IDX, X_TURN, X_TURNED, X_GU, X_SILU, X_ACT, X_AT, X_ATC, X_DN, X_Y, X_SIDX, X_OUT) = range(1, 13)

        wait_held = sem("wait_held")

        def x_at(b, e, s=0):
            return (b - 1) * (X_TAB + E * X_OUT) + X_TAB + e * X_OUT + s

        def walk(eng, body):
            n = E // 4
            body(0, True, False)
            with eng.Fori(1, n - 1) as it:
                body(it, False, False)
            body(n - 1, False, True)

        block = ctx.enter_context(nc.Block())

        def tiles_of(l):
            return range(NT if l < DEPTH - 1 else NL)

        SCORE_BANK = (0, 1, 6)

        def head_rows(h):
            return (h % 2) * RD, (h % 2) * RD + RD

        @block.sync
        def _(sp):
            seen = Seen()
            sp.dma_start(craw[:, 0, :], A["c"].rearrange("a (p k) -> p (a k)", p=P)).then_inc(c_in, 16)
            sp.dma_start(craw[:, 1, :], A["c_ctx"].rearrange("(p k) -> p k", p=P)).then_inc(c_in, 16)

            def mod_inputs(l):
                sp.dma_start(modrow[0:2, :], A["ada_b"][l:l + 1, :].broadcast_to([2, 6 * D])).then_inc(ada_rows_in, 16)
                for g, nm in enumerate(("pre_mix_g", "post_mix_g", "pre_ffn_g", "post_ffn_g")):
                    sp.dma_start(grow[0:2, g * D:(g + 1) * D], A[nm][l:l + 1, :].broadcast_to([2, D])).then_inc(ada_rows_in, 16)

            def mod_store(l):
                sp.wait_ge(mod_rows, l + 1)
                sp.dma_start(mod_dram[l], modrow[0:2, :]).then_inc(mod_out, 16)
                sp.wait_ge(mod_out, 16 * (l + 1))

            def load_w_in(l, k):
                sp.dma_start(w_in[:, k:k + 1, :], A["w_in"][l].rearrange("(p k) n -> p k n", p=P)[:, k:k + 1, :]).then_inc(w_in_in, 16)

            for n in range(12 * DEPTH):
                l, c = n // 12, n % 12
                if n >= 4:
                    sp.wait_ge(ada_sum, n - 3)
                sp.dma_start(ada_ring[:, n % 4], A["ada_w"][l].rearrange("(p k) n -> p k n", p=P)[:, :, c * 512:(c + 1) * 512]
                             ).then_inc(ada_in[n % 4], 16)
                if n == 0:
                    mod_inputs(0)
                if n == 3:
                    sp.dma_start(cst, A["shape_consts"]).then_inc(start_in, 16)
                    sp.dma_start(x[:, 0:NL, :], A["x"].rearrange("a (i p) d -> p (a i) d", p=P)).then_inc(start_in, 16)
                    sp.dma_start(x[:, NL:NT, :], A["ctx"].rearrange("a (i p) d -> p (a i) d", p=P)).then_inc(start_in, 16)
                if c == 3 and l > 0:
                    mod_store(l - 1)
                    mod_inputs(l)
            for k in range(KD):
                load_w_in(0, k)
            mod_store(DEPTH - 1)
            end_phase(sp, "sp")

            def row(l, s, j):
                return mod_dram[l][s:s + 1, j * D:(j + 1) * D].broadcast_to([P, D])

            def load_bc(l):
                for s in range(2):
                    sp.dma_start(bc[:, 2 * s, :], row(l, s, 1)).then_inc(bc_in, 16)
                    sp.dma_start(bc[:, 2 * s + 1, :], row(l, s, 0)).then_inc(bc_in, 16)

            def load_mla(l):
                sp.dma_start(w_q, A["mla_w_q_b"][l].rearrange("(k p) n -> p k n", p=P)).then_inc(mla_in, 16)
                sp.dma_start(w_kv, A["mla_w_kv_b"][l].rearrange("(k p) n -> p k n", p=P)).then_inc(mla_in, 16)
                sp.dma_start(qcol, A["mla_q_norm"][l].rearrange("(k p) -> p k", p=P), allow_slow_non_contiguous=True).then_inc(mla_in, 16)
                sp.dma_start(kvcol, A["mla_kv_norm"][l].rearrange("(k p) -> p k", p=P), allow_slow_non_contiguous=True).then_inc(mla_in, 16)

            for l in range(DEPTH):
                if l == 0:
                    load_bc(l)
                load_mla(l)
                end_phase(sp, "sp")
                sp.dma_start(poolm, A["pool_matrix"].rearrange("p (k g t) -> p k g t", k=2, g=PG)).then_inc(pool_in, 16)
                sp.dma_start(pool_w[0:PC], A["pool_w"][l].rearrange("g c n -> c g n")).then_inc(pool_in, 16)
                sp.dma_start(pool_s, A["pool_scale"][l:l + 1, :].broadcast_to([P, PW])).then_inc(pool_in, 16)
                for nm, src, n in (("mu", A["rwkv_mu"][l:l + 1, :], RIN), ("k_k", A["rwkv_k_k"][l:l + 1, :], RW),
                                   ("k_a", A["rwkv_k_a"][l:l + 1, :], RW), ("r_k", A["rwkv_r_k"][l:l + 1].rearrange("a h n -> a (h n)"), RW),
                                   ("ln_w", A["rwkv_ln_w"][l:l + 1, :], RW), ("ln_b", A["rwkv_ln_b"][l:l + 1, :], RW)):
                    sp.dma_start(rb[nm], src.broadcast_to([P, n])).then_inc(rs["in"], 16)
                for a, nm in enumerate(("rwkv_w0", "rwkv_a0")):
                    sp.dma_start(rb["wbias"][:, a * 2 * RW:(a + 1) * 2 * RW], A[nm][l:l + 1].rearrange("a d n -> a (d n)").broadcast_to([P, 2 * RW])
                                 ).then_inc(rs["in"], 16)
                sp.dma_start(rb["g2"][0:GLORA], A["rwkv_g2"][l]).then_inc(rs["in"], 16)
                sp.wait_ge(rs["zero"], l + 1)
                for a, nm in enumerate(("rwkv_w2", "rwkv_a2")):
                    for d in range(2):
                        j = 2 * a + d
                        sp.dma_start(rb["loraW"][j * LORA:(j + 1) * LORA, j * RW:(j + 1) * RW], A[nm][l, d]).then_inc(rs["in"], 16)
                for k in range(2, 4):
                    end_phase(sp, "sp")
                sp.wait_ge(rs["fin_ready"], NT * (l + 1))
                for k in range(4):
                    sp.dma_start(w_out[:, 2 * k:2 * k + 2, :], A["w_out"][l].rearrange("(k p) n -> p k n", p=P)[:, 2 * k:2 * k + 2, :]
                                 ).then_inc(w_out_in, 16)
                for s in range(2):
                    sp.dma_start(gbc[:, s, :], row(l, s, 2)).then_inc(w_out_in, 16)
                end_phase(sp, "sp")
                for s in range(2 if l < DEPTH - 1 else 1):
                    sp.dma_start(mbc[:, 2 * s, :], row(l, s, 4)).then_inc(ms["in"], 16)
                    sp.dma_start(mbc[:, 2 * s + 1, :], row(l, s, 3)).then_inc(ms["in"], 16)
                sp.dma_start(rw, A["router_w"][l].rearrange("(p k) e -> p k e", p=P)).then_inc(ms["in"], 16)
                sp.dma_start(rbias, A["router_bias"][l:l + 1, :].broadcast_to([P, E])).then_inc(ms["in"], 16)
                for m, nm in enumerate(("sh_w_gate", "sh_w_up")):
                    sp.dma_start(sh_gu[:, m], A[nm][l].rearrange("(p k) n -> p k n", p=P)).then_inc(ms["in"], 16)
                sp.dma_start(sh_dn, A["sh_w_down"][l].rearrange("(p k) n -> p k n", p=P)).then_inc(ms["in"], 16)
                end_phase(sp, "sp")
                for i in tiles_of(l):
                    sp.wait_ge(h_ready, NT * (l + 1) + sum(len(tiles_of(a)) for a in range(l)) + i + 1)
                    sp.dma_start(h_dram[i * P:(i + 1) * P, :], mh[:, i % 2, :]).then_inc(ms["h_out"], 16)
                    sp.wait_ge(ms["h_out"], seen(ms["h_out"], 16))
                end_phase(sp, "sp")

                def load_expert(S, e, j):
                    for m, nm in enumerate(("exp_w_gate", "exp_w_up")):
                        sp.dma_start(ring_gu[:, j, m], A[nm][l, bass.ds(e, 1)].rearrange("a (p k) n -> p (a k) n", p=P)).then_inc(S.w_in[j], 16)
                    sp.dma_start(ring_dn[:, j], A["exp_w_down"][l, bass.ds(e, 1)].rearrange("a (p k) n -> p (a k) n", p=P)).then_inc(S.w_in[j], 16)

                def load_walk(S, base):
                    def body(it, first, last):
                        for j in range(4):
                            e = it * 4 + j
                            if first and j == 0:
                                load_expert(S, 0, 0)
                                end_phase(sp, "sp")
                                continue
                            if not first:
                                sp.wait_ge(S.dn_sum, base + e - 3)
                            load_expert(S, e, j)
                    walk(sp, body)

                load_walk(main, E * l)
                end_phase(sp, "sp")
                sp.wait_ge(ms["count_ready"], l + 1)
                most = sp.value_load(cnti[0:1, 0:1], min_val=0, max_val=NT * P)
                with sp.If(most > CAP):
                    for b in range(1, len(tiles_of(l))):
                        with sp.Fori(0, E) as e:
                            sp.wait_ge(x_chain[l], x_at(b, e))
                            for m, nm in enumerate(("exp_w_gate", "exp_w_up")):
                                sp.dma_start(ring_gu[:, 0, m], A[nm][l, bass.ds(e, 1)].rearrange("a (p k) n -> p (a k) n", p=P)).then_inc(x_in[l], 16)
                            sp.dma_start(ring_dn[:, 0], A["exp_w_down"][l, bass.ds(e, 1)].rearrange("a (p k) n -> p (a k) n", p=P)).then_inc(x_in[l], 16)
                end_phase(sp, "sp")
                for s in range(len(tiles_of(l)) // 2):
                    sp.dma_start(fbc[:, s, :], row(l, s, 5)).then_inc(ms["f_in"], 16)
                if l < DEPTH - 1:
                    load_bc(l + 1)
                before = sum(len(tiles_of(a)) for a in range(l))
                for n in range(TOPK * len(tiles_of(l))):
                    i, k, m = n // TOPK, n % TOPK, n + TOPK * before
                    if n >= NY:
                        sp.wait_ge(ms["y_used"], m + 1 - NY)
                    sp.dma_start(ybuf[:, m % NY], y_dram[i * P * TOPK:(i + 1) * P * TOPK, :].rearrange("(p k) d -> p k d", k=TOPK)[:, k, :]
                                 ).then_inc(y_in[m % NY], 16)
                    if l < DEPTH - 1 and NY <= n < NY + KD:
                        load_w_in(l + 1, n - NY)
                if l < DEPTH - 1:
                    sp.wait_ge(h_ready, NT * (l + 2) + before + len(tiles_of(l)))
                if l == DEPTH - 1:
                    end_phase(sp, "sp")
                    sp.dma_start(out[0].rearrange("(i p) d -> p i d", p=P), x[:, 0:NL, :]).then_inc(ms["out_done"], 16)
                    sp.wait_ge(ms["out_done"], 16)

        @block.tensor
        def _(pe):
            seen = Seen()
            mm = nc.tensor.matmul
            tr = nc.tensor.transpose
            pe.wait_ge(silu_c, 1)
            for n in range(12 * DEPTH):
                pe.wait_ge(ada_in[n % 4], 16 * (n // 4 + 1))
                if n >= 8:
                    pe.wait_ge(ada_row, n - 7)
                for k in range(KD):
                    last = mm(pb[0:2, n % 8, :], cs[:, k, :], ada_ring[:, n % 4, k, :], start=(k == 0), stop=(k == KD - 1))
                last.then_inc(ada_sum, 1)
            pe.wait_ge(start_in, 48)
            end_phase(pe, "pe")

            def turn_tile(src, first_bank):
                for k in range(KD):
                    last = tr(pb[:, first_bank + k // 4, (k % 4) * P:(k % 4 + 1) * P], src[:, k * P:(k + 1) * P], ident)
                return last

            for l in range(DEPTH):
                turned = seen(hT_ready, 0)

                def h_turn(i):
                    pe.wait_ge(h_ready, seen(h_ready))
                    turn_tile(hbuf[:, i % 2, :], 2 * (i % 2)).then_inc(hT_sum, 1)

                h_turn(0)
                n = 0
                for i in range(NT):
                    if i + 1 < NT:
                        h_turn(i + 1)
                    pe.wait_ge(hT_ready, turned + i + 1)
                    if i == 0:
                        pe.wait_ge(w_in_in, seen(w_in_in, 16 * KD))
                    for c in range(4):
                        if n >= 4:
                            pe.wait_ge(z_ready, seen(z_ready))
                        w0, wn = (c * ZA // 2, ZA // 2) if c < 2 else (ZA + (c - 2) * RIN // 2, RIN // 2)
                        for k in range(KD):
                            last = mm(pb[:, 4 + n % 4, 0:wn], hT[:, k, i * P:(i + 1) * P], w_in[:, k, w0:w0 + wn],
                                      start=(k == 0), stop=(k == KD - 1))
                        last.then_inc(z_sum, 1)
                        n += 1
                seen(z_ready, 4)
                seen(hT_ready, NT)
                end_phase(pe, "pe")

                pe.wait_ge(mla_in, seen(mla_in, 64))
                def project(i):
                    pe.wait_ge(zn_ready, seen(zn_ready))
                    for k in range(5):
                        last = tr(pb[:, k // 4, (k % 4) * P:(k % 4 + 1) * P], zn[:, i % 2, k * P:(k + 1) * P], ident)
                    last.then_inc(znT_sum, 1)
                    pe.wait_ge(znT_ready, seen(znT_ready))
                    if i >= 1:
                        pe.wait_ge(qkv_raw, seen(qkv_raw))
                    for c in range(2):
                        for k in range(3):
                            mm(pb[:, 2 + c, 0:384], znT[:, i % 2, k, :], w_q[:, k, c * 384:(c + 1) * 384], start=(k == 0), stop=(k == 2))
                    for c in range(2):
                        for k in range(2):
                            last = mm(pb[:, 4 + c, :], znT[:, i % 2, 3 + k, :], w_kv[:, k, c * 512:(c + 1) * 512], start=(k == 0), stop=(k == 1))
                    last.then_inc(qkv_sum, 1)

                project(0)
                for i in range(NT):
                    if i + 1 < NT:
                        project(i + 1)
                    pe.wait_ge(qk_ready, seen(qk_ready))
                    for m, src in enumerate((qraw, kk_)):
                        if i >= 1 or m == 1:
                            pe.wait_ge(qkT_ready, seen(qkT_ready))
                        for h in range(H):
                            last = tr(pb[0:QK, 6 + h // 4, (h % 4) * P:(h % 4 + 1) * P], src[:, i % 2, h, :], ident)
                        last.then_inc(qkT_sum, 1)
                pe.wait_ge(qkT_ready, seen(qkT_ready))
                seen(qkv_raw)

                units = [(i, h) for i in tiles_of(l) for h in range(H)]
                keys = lambda i: (0, NT) if i < NL else (NL, NT)
                exped, copied = seen(probs_ready, 0), seen(probsT_ready, 0)

                def score(u):
                    i, h = units[u]
                    a, b = keys(i)
                    mm(pb[:, SCORE_BANK[u % 3], 0:(b - a) * P], qT[0:QK, h, i * P:(i + 1) * P], kT[0:QK, h, a * P:b * P],
                       start=True, stop=True).then_inc(score_sum, 1)

                def attend(u):
                    i, h = units[u]
                    a, b = keys(i)
                    pe.wait_ge(probsT_ready, copied + u + 1)
                    if h == 0 and i >= 2:
                        pe.wait_ge(att_ready, seen(att_ready))
                    for k in range(a, b):
                        last = mm(pb[:, 4 + i % 2, h * VH:(h + 1) * VH], probsT[:, u % 2, k - a, :], vv[:, k, h * VH:(h + 1) * VH],
                                  start=(k == a), stop=(k == b - 1))
                    last.then_inc(att_sum, 1)

                score(0)
                score(1)
                for u, (i, h) in enumerate(units):
                    a, b = keys(i)
                    pe.wait_ge(probs_ready, exped + u + 1)
                    for k in range(b - a):
                        last = tr(pb[:, 2 + u % 2, k * P:(k + 1) * P], probs[:, u % 2, k * P:(k + 1) * P], ident)
                    last.then_inc(probsT_sum, 1)
                    if u + 2 < len(units):
                        score(u + 2)
                    if u >= 1:
                        attend(u - 1)
                attend(len(units) - 1)
                seen(probs_ready, len(units))
                seen(probsT_ready, len(units))
                pe.wait_ge(att_ready, seen(att_ready, 2))
                end_phase(pe, "pe")

                pe.wait_ge(pool_in, seen(pool_in, 48))
                groups = [(s, g) for s in range(len(tiles_of(l)) // 2) for g in range(PG)]
                for u, (s, g) in enumerate(groups):
                    for k in range(2):
                        last = mm(pb[0:PC, u % 2, 0:SEQ], za[:, 2 * s + k, MLA_IN + g * PC:MLA_IN + (g + 1) * PC], poolm[:, k, g, :],
                                  start=(k == 0), stop=(k == 1))
                    last.then_inc(diff_sum, 1)
                    pe.wait_ge(diff_ready, seen(diff_ready))
                    for t in range(2):
                        last = mm(pb[:, 2 + 2 * s + t, g * PC:(g + 1) * PC], diffT[0:PC, u % 2, t * P:(t + 1) * P], pool_w[0:PC, g, :],
                                  start=True, stop=True)
                    last.then_inc(pool_sum, 1)
                end_phase(pe, "pe")

                R = rs
                pe.wait_ge(R["in"], seen(R["in"], 16 * 13))

                def front(i):
                    s = i // 2
                    for c in range(2):
                        for k in range(2):
                            last = mm(pb[:, 6 + c, 0:RIN // 2], shift[:, k, (i % 2) * P:(i % 2 + 1) * P],
                                      zr[:, 2 * s + k, c * RIN // 2:(c + 1) * RIN // 2], start=(k == 0), stop=(k == 1))
                    last.then_inc(R["shift_sum"], 1)
                    yield
                    pe.wait_ge(R["lo_ready"], seen(R["lo_ready"]))
                    tr(pb[:, 6, 0:P], rb["lo"][:, 0:P], ident)
                    tr(pb[0:GLORA, 6, P:2 * P], rb["lo"][:, P:P + GLORA], ident).then_inc(R["loT_sum"], 1)
                    yield
                    pe.wait_ge(R["loT_ready"], seen(R["loT_ready"]))
                    for c in range(2):
                        last = mm(pb[:, 6 + c, :], rb["loT"][:, 0, :], rb["loraW"][:, c * 512:(c + 1) * 512], start=True, stop=True)
                    last.then_inc(R["lora_sum"], 1)
                    yield
                    pe.wait_ge(R["lw_ready"], seen(R["lw_ready"]))
                    for d in range(2):
                        mm(pb[:, 6, d * RW:(d + 1) * RW], cum[:, d, :], rb["xwa"][:, 0, d, :], start=True, stop=True)
                    mm(pb[:, 7, 8:8 + RW], rb["loT"][0:GLORA, 1, :], rb["g2"][0:GLORA], start=True, stop=True)
                    for d in range(2):
                        for q in range(NPAIR):
                            last = mm(pb[:, 7, (2 * d + q) * 2:(2 * d + q) * 2 + 2], rb["xwa"][:, 0, d, q * P:(q + 1) * P], c_("chunk_of"),
                                      start=True, stop=True)
                    last.then_inc(R["cum_sum"], 1)
                    yield
                    for d in range(2):
                        if d == 0:
                            pe.wait_ge(R["arr_ready"], seen(R["arr_ready"]))
                        else:
                            pe.wait_ge(R["arrT_ready"], seen(R["arrT_ready"]))
                        for q in range(NPAIR):
                            for a in range(4):
                                last = tr(pb[:, 6 + q, a * P:(a + 1) * P], rb["arr2"][:, i % 2, a, d, q * P:(q + 1) * P], ident)
                        last.then_inc(R["arrT_sum"], 1)
                        yield

                ahead = front(0)
                for _ in ahead:
                    pass
                for i in range(NT):
                    arr = rb["arr2"][:, i % 2]
                    zs = rb["zs2"][:, i % 2]
                    v_ = lambda h: zs[:, 2 * RW + h * RD:2 * RW + (h + 1) * RD]
                    ahead = front(i + 1) if i + 1 < NT else iter(())
                    pe.wait_ge(R["arrT_ready"], seen(R["arrT_ready"]))
                    for d in range(2):
                        if d == 1:
                            pe.wait_ge(R["mats_ready"], seen(R["mats_ready"]))
                        for h in range(RH):
                            a, b = head_rows(h)
                            q = h // 2
                            T = rb["arrT"][a:b, d, q]
                            mm(pb[:, 4 + h % 2, q * P:(q + 1) * P], T[:, 0, :], T[:, 2, :], start=True, stop=True)
                            kr = T[:, 0:2, :].rearrange("p a t -> p (a t)")
                            mm(pb[:, h % 2, q * 256:(q + 1) * 256], T[:, 2, :], kr, start=True, stop=True)
                            last = mm(pb[:, 2 + h % 2, q * 256:(q + 1) * 256], T[:, 3, :], kr, start=True, stop=True)
                        last.then_inc(R["mats_sum"], 1)
                    pe.wait_ge(R["mats_ready"], seen(R["mats_ready"]))
                    for lv in range(1, 6):
                        for d in range(2):
                            if lv > 1:
                                pe.wait_ge(R["x_ready"], seen(R["x_ready"]))
                            for h in range(RH):
                                last = mm(pb[:, 4 + d, h * P:(h + 1) * P], rb["LG"][:, d, h, 0, :], rb["X"][:, d, h, :], start=True, stop=True)
                            last.then_inc(R["t1_sum"], 1)
                        if lv == 5:
                            for d in range(2):
                                for h in range(RH):
                                    last = mm(pb[:, d, h * RD:(h + 1) * RD], rb["MG"][:, d, h, 0, :], v_(h), start=True, stop=True)
                                last.then_inc(R["mv_sum"], 1)
                        for d in range(2):
                            pe.wait_ge(R["t1_ready"], seen(R["t1_ready"]))
                            for h in range(RH):
                                if lv < 5:
                                    mm(pb[:, d, h * P:(h + 1) * P], rb["XT"][:, d, h, :], rb["T1"][:, d, h, :], start=True, stop=True)
                                last = mm(pb[:, 2 + d, h * P:(h + 1) * P], rb["T1"][:, d, h, :], rb["XT"][:, d, h, :], start=True, stop=True)
                            last.then_inc(R["x_sum"], 1)
                        if lv < 5:
                            next(ahead, None)
                    for d in range(2):
                        pe.wait_ge(R["x_ready"], seen(R["x_ready"]))
                        pe.wait_ge(R["kmv_ready"], seen(R["kmv_ready"]))
                        for h in range(RH):
                            last = mm(pb[:, 4 + d, h * P:(h + 1) * P], rb["XT"][:, d, h, :], rb["KMV"][:, d, h].rearrange("p m n -> p (m n)"),
                                      start=True, stop=True)
                        last.then_inc(R["nx_sum"], 1)
                    next(ahead, None)
                    pe.wait_ge(R["nx_ready"], seen(R["nx_ready"], 2))
                    for h in range(RH):
                        for d in range(2):
                            mm(pb[:, 0, h * RD:(h + 1) * RD], rb["MG"][:, d, h, 1, :], v_(h), start=(d == 0), stop=False)
                            mm(pb[:, 0, h * RD:(h + 1) * RD], rb["LG"][:, d, h, 1, :], rb["nX"][:, d, 1, h, :], start=False, stop=(d == 1))
                    for d in range(2):
                        for h in range(RH):
                            a, b = head_rows(h)
                            dq = 2 * d + h // 2
                            mm(pb[a:b, 1, dq * P:(dq + 1) * P], rb["nX"][:, d, 0, h, :], rb["LG"][:, d, h, 1, :], start=True, stop=True)
                            for c in range(2):
                                ca, cb = c * C, (c + 1) * C
                                o = dq * C
                                beta = arr[ca:cb, 2, d, h * RD:(h + 1) * RD]
                                khat = arr[ca:cb, 3, d, h * RD:(h + 1) * RD]
                                mm(pb[a:b, 2 + 2 * c, o:o + C], rb["nX"][ca:cb, d, 0, h, :], beta, start=True, stop=True)
                                mm(pb[a:b, 3 + 2 * c, o:o + C], khat, zs[ca:cb, 2 * RW + h * RD:2 * RW + (h + 1) * RD], start=True, stop=False)
                                last = mm(pb[a:b, 3 + 2 * c, o:o + C], beta, rb["nX"][ca:cb, d, 1, h, :], start=False, stop=True)
                    last.then_inc(R["fin_sum"], 1)
                    next(ahead, None)
                    pe.wait_ge(R["fin_ready"], seen(R["fin_ready"]))
                for n in range(1, NC - 1):
                    for d in range(2):
                        pe.wait_ge(R["chain_ready"], seen(R["chain_ready"]))
                        cp = ORDER[d][n]
                        for h in range(RH):
                            a, b = head_rows(h)
                            last = mm(pb[a:b, d, (h // 2) * RD:(h // 2 + 1) * RD], rb["TT"][a:b, d, h // 2, cp, :], rb["Z"][a:b, d, h // 2, cp, :],
                                      start=True, stop=True)
                        last.then_inc(R["chain_sum"], 1)
                pe.wait_ge(R["chain_ready"], seen(R["chain_ready"], 2))
                for i in tiles_of(l):
                    if i >= 2:
                        pe.wait_ge(R["inter_used"], seen(R["inter_used"]))
                    for h in range(RH):
                        a, b = head_rows(h)
                        for j in range(2):
                            c = 2 * i + j
                            ds = [d for d in range(2) if c != ORDER[d][0]]
                            for d in ds:
                                last = mm(pb[j * C:(j + 1) * C, 4 + 2 * (i % 2) + h % 2, (h // 2) * RD:(h // 2 + 1) * RD], rb["RQT"][a:b, d, h // 2, c * C:(c + 1) * C],
                                          rb["Z"][a:b, d, h // 2, c, :], start=(d == ds[0]), stop=(d == ds[-1]))
                    last.then_inc(R["inter_sum"], 1)
                pe.wait_ge(R["inter_used"], seen(R["inter_used"], 2))
                end_phase(pe, "pe")

                pe.wait_ge(w_out_in, seen(w_out_in, 96))
                for i in tiles_of(l):
                    turn_tile(mix[:, i, :], 0).then_inc(mixT_sum, 1)
                    pe.wait_ge(mixT_ready, seen(mixT_ready))
                    if i >= 2:
                        pe.wait_ge(y_used, seen(y_used))
                    for c in range(2):
                        for k in range(KD):
                            last = mm(pb[:, 4 + 2 * (i % 2) + c, :], mixT[:, i % 2, k, :], w_out[:, k, c * 512:(c + 1) * 512],
                                      start=(k == 0), stop=(k == KD - 1))
                    last.then_inc(y_sum, 1)
                pe.wait_ge(y_used, seen(y_used, 2))
                end_phase(pe, "pe")
                pe.wait_ge(ms["in"], seen(ms["in"], 16 * (5 + 2 * (len(tiles_of(l)) // 2))))
                for i in tiles_of(l):
                    pe.wait_ge(h_ready, seen(h_ready))
                    turn_tile(mh[:, i % 2, :], 2 * (i % 2)).then_inc(hT_sum, 1)
                    pe.wait_ge(hT_ready, seen(hT_ready))
                    own = slice(i * P, (i + 1) * P)
                    for k in range(KD):
                        last = mm(pb[:, 4, 0:E], hT[:, k, own], rw[:, k, :], start=(k == 0), stop=(k == KD - 1))
                    last.then_inc(ms["logit_sum"], 1)
                    for k in range(KD):
                        last = mm(pb[:, 5, :], hT[:, k, own], sh_gu[:, :, k, :], start=(k == 0), stop=(k == KD - 1))
                    last.then_inc(ms["shgu_sum"], 1)
                    pe.wait_ge(ms["act_ready"], seen(ms["act_ready"]))
                    for k in range(2):
                        last = tr(pb[:, 4, k * P:(k + 1) * P], sh_act[:, k * P:(k + 1) * P], ident)
                    last.then_inc(ms["aT_sum"], 1)
                    pe.wait_ge(ms["aT_ready"], seen(ms["aT_ready"]))
                    for c in range(2):
                        for k in range(2):
                            last = mm(pb[:, 6 + c, :], sh_aT[:, k, :], sh_dn[:, k, c * 512:(c + 1) * 512], start=(k == 0), stop=(k == 1))
                    last.then_inc(ms["dn_sum"], 1)
                    pe.wait_ge(ms["sh_ready"], seen(ms["sh_ready"]))
                pe.wait_ge(ms["mask_ready"], seen(ms["mask_ready"], len(tiles_of(l))))
                nt = len(tiles_of(l))
                for i in range(nt):
                    for j in range(i + 1):
                        mm(pb[:, 0, i * E:(i + 1) * E], before_bf if j == i else ones_bf, mask_bf[:, j, :], start=(j == 0), stop=(j == i))
                for j in range(nt):
                    last = mm(pb[:, 0, nt * E:(nt + 1) * E], ones_bf, mask_bf[:, j, :], start=(j == 0), stop=(j == nt - 1))
                last.then_inc(ms["pos_sum"], 1)
                end_phase(pe, "pe")

                def tables(done):
                    for e in range(E):
                        for i in range(nt):
                            last = mm(pb[:, 0, 4 * e:4 * e + 4], onehot[:, i, e, :], meta[:, i, e, :], start=(i == 0), stop=(i == nt - 1))
                    last.then_inc(done, 1)

                pe.wait_ge(ms["onehot_ready"], seen(ms["onehot_ready"]))
                tables(ms["tab_sum"])
                end_phase(pe, "pe")

                def ffn_walk(S, base):
                    def turn(m, j):
                        pe.wait_ge(S.g_in[j], m)
                        turn_tile(gx[:, j, :], 0).then_inc(S.gT_sum, 1)

                    def down(n, j, waits):
                        pe.wait_ge(S.aT_ready, n + 1)
                        if waits:
                            pe.wait_ge(S.y_ready, n)
                        for c in range(2):
                            for k in range(2):
                                last = mm(pb[:, 5 + c, :], aT[:, j % 2, k, :], ring_dn[:, j % 4, k, c * 512:(c + 1) * 512], start=(k == 0), stop=(k == 1))
                        last.then_inc(S.dn_sum, 1)

                    def gathered(it, j):
                        return 16 * (base // 4 + it + 1)

                    def body(it, first, last_):
                        for j in range(4):
                            n = it * 4 + j + base
                            if first and j == 0:
                                turn(gathered(0, 0), 0)
                            pe.wait_ge(S.w_in[j], 48 * (it + 1 + base // 4))
                            pe.wait_ge(S.gT_ready, n + 1)
                            if not (first and j < 2):
                                pe.wait_ge(S.act_ready, n - 1)
                            for k in range(KD):
                                last = mm(pb[:, 2 + j % 2, :], gT[:, j % 2, k, :], ring_gu[:, j, :, k, :], start=(k == 0), stop=(k == KD - 1))
                            last.then_inc(S.gu_sum, 1)
                            if not (last_ and j == 3):
                                turn(gathered(it, j + 1) if j < 3 else gathered(it + 1, 0), (j + 1) % 4)
                            if not (first and j == 0):
                                down(n - 1, j - 1, not (first and j == 1))
                            pe.wait_ge(S.act_ready, n + 1)
                            if not (first and j == 0):
                                pe.wait_ge(S.aT_ready, n)
                            for k in range(2):
                                last = tr(pb[:, 4, k * P:(k + 1) * P], actx[:, j % 2, k * P:(k + 1) * P], ident)
                            last.then_inc(S.aT_sum, 1)
                    walk(pe, body)
                    down(base + E - 1, 3, True)

                ffn_walk(main, E * l)
                end_phase(pe, "pe")
                pe.wait_ge(ms["count_ready"], l + 1)
                most = pe.value_load(cnti[0:1, 0:1], min_val=0, max_val=NT * P)
                with pe.If(most > CAP):
                    for b in range(1, nt):
                        pe.wait_ge(x_chain[l], x_at(b, 0) - 2)
                        tables(x_chain[l])
                        with pe.Fori(0, E) as e:
                            pe.wait_ge(x_in[l], 48 * ((b - 1) * E + e + 1))
                            pe.wait_ge(x_rows[l], 16 * ((b - 1) * E + e + 1))
                            turn_tile(gx[:, 0, :], 0).then_inc(x_chain[l], 1)
                            pe.wait_ge(x_chain[l], x_at(b, e, X_TURNED))
                            for k in range(KD):
                                last = mm(pb[:, 2, :], gT[:, 0, k, :], ring_gu[:, 0, :, k, :], start=(k == 0), stop=(k == KD - 1))
                            last.then_inc(x_chain[l], 1)
                            pe.wait_ge(x_chain[l], x_at(b, e, X_ACT))
                            for k in range(2):
                                last = tr(pb[:, 4, k * P:(k + 1) * P], actx[:, 0, k * P:(k + 1) * P], ident)
                            last.then_inc(x_chain[l], 1)
                            pe.wait_ge(x_chain[l], x_at(b, e, X_ATC))
                            for c in range(2):
                                for k in range(2):
                                    last = mm(pb[:, 5 + c, :], aT[:, 0, k, :], ring_dn[:, 0, k, c * 512:(c + 1) * 512], start=(k == 0), stop=(k == 1))
                            last.then_inc(x_chain[l], 1)
                end_phase(pe, "pe")
                if l == DEPTH - 1:
                    end_phase(pe, "pe")

        @block.scalar
        def _(act):
            seen = Seen()
            ac = nc.scalar.activation
            act.wait_ge(c_in, 32)
            ac(cs.rearrange("p k s -> p s k"), craw, ACT.Silu).then_inc(silu_c, 1)
            end_phase(act, "act")
            for l in range(DEPTH):
                def turned(i):
                    act.wait_ge(hT_sum, seen(hT_sum))
                    ac(hT[:, :, i * P:(i + 1) * P], pb[:, 2 * (i % 2):2 * (i % 2) + 2, :].rearrange("p b (k t) -> p (b k) t", k=4), ACT.Copy
                       ).then_inc(hT_ready, 1)

                turned(0)
                for i in range(NT):
                    if i + 1 < NT:
                        turned(i + 1)
                    for c in range(4):
                        act.wait_ge(z_sum, seen(z_sum))
                        wn = ZA // 2 if c < 2 else RIN // 2
                        dst = za[:, i, c * wn:(c + 1) * wn] if c < 2 else zr[:, i, (c - 2) * wn:(c - 1) * wn]
                        ac(dst, pb[:, 4 + (4 * i + c) % 4, 0:wn], ACT.Copy).then_inc(z_ready, 1)
                end_phase(act, "act")
                act.wait_ge(mla_in, seen(mla_in, 64))
                def project(i):
                    act.wait_ge(znT_sum, seen(znT_sum))
                    for k in range(5):
                        col = qcol[:, k:k + 1] if k < 3 else kvcol[:, k - 3:k - 2]
                        last = ac(znT[:, i % 2, k, :], pb[:, k // 4, (k % 4) * P:(k % 4 + 1) * P], ACT.Copy, scale=col)
                    last.then_inc(znT_ready, 1)
                    act.wait_ge(qkv_sum, seen(qkv_sum))
                    if i >= 2:
                        act.wait_ge(qkT_sum, qk_turned + 2 * (i - 1))
                    for c in range(2):
                        ac(qraw[:, i % 2, 4 * c:4 * c + 4, :], pb[:, 2 + c, 0:384].rearrange("p (h n) -> p h n", h=4), ACT.Copy)
                        kv = pb[:, 4 + c, :].rearrange("p (h n) -> p h n", h=4)
                        ac(kk_[:, i % 2, 4 * c:4 * c + 4, 0:NOPE], kv[:, :, 0:NOPE], ACT.Copy)
                        last = ac(vv[:, i, 4 * c * VH:4 * (c + 1) * VH].rearrange("p (h n) -> p h n", h=4), kv[:, :, NOPE:NOPE + VH], ACT.Copy)
                    last.then_inc(qkv_raw, 1)

                qk_turned = seen(qkT_sum, 0)
                project(0)
                for i in range(NT):
                    if i + 1 < NT:
                        project(i + 1)
                    for m, dst in enumerate((qT, kT)):
                        act.wait_ge(qkT_sum, qk_turned + 2 * i + m + 1)
                        ac(dst[0:QK, :, i * P:(i + 1) * P], pb[0:QK, 6:8, :].rearrange("p b (h t) -> p (b h) t", h=4), ACT.Copy
                           ).then_inc(qkT_ready, 1)
                seen(qkT_sum, 2 * NT)
                units = [(i, h) for i in tiles_of(l) for h in range(H)]
                for u, (i, h) in enumerate(units):
                    nk = (NT if i < NL else NT - NL) * P
                    act.wait_ge(max_ready, seen(max_ready))
                    if u >= 2:
                        act.wait_ge(probsT_sum, seen(probsT_sum))
                    ac(probs[:, u % 2, 0:nk], pb[:, SCORE_BANK[u % 3], 0:nk], ACT.Exp, bias=mrow[:, u % 2:u % 2 + 1], scale=MLA_SCALE,
                       accum_out=rsum[:, i, h:h + 1]).then_inc(probs_ready, 1)
                seen(probsT_sum, 2)
                end_phase(act, "act")
                for u in range(len(tiles_of(l)) // 2 * PG):
                    act.wait_ge(diff_sum, seen(diff_sum))
                    if u >= 2:
                        act.wait_ge(pool_sum, seen(pool_sum))
                    ac(diffT[0:PC, u % 2, :], pb[0:PC, u % 2, 0:SEQ], ACT.Copy).then_inc(diff_ready, 1)
                seen(pool_sum, 2)
                end_phase(act, "act")
                R = rs
                for i in range(NT):
                    zs, arr = rb["zs2"][:, i % 2], rb["arr2"][:, i % 2]
                    act.wait_ge(R["zs_ready"], seen(R["zs_ready"]))
                    if i >= 1:
                        act.wait_ge(R["loT_sum"], NT * l + i)
                    ac(rb["lo"][:, 0:2 * LORA], zs[:, 3 * RW:3 * RW + 2 * LORA], ACT.Tanh)
                    ac(rb["lo"][:, 2 * LORA:4 * LORA], zs[:, 3 * RW + 2 * LORA:3 * RW + 4 * LORA], ACT.Copy)
                    link(act, ac(rb["lo"][:, 4 * LORA:], zs[:, 3 * RW + 4 * LORA:RIN], ACT.Tanh, scale=0.5), act_step)
                    ac(rb["lo"][:, 4 * LORA:], rb["lo"][:, 4 * LORA:], ACT.Copy, scale=0.5, bias=0.5).then_inc(R["lo_ready"], 1)
                    act.wait_ge(R["loT_sum"], seen(R["loT_sum"]))
                    ac(rb["loT"][:, 0, :], pb[:, 6, 0:P], ACT.Copy)
                    ac(rb["loT"][0:GLORA, 1, :], pb[0:GLORA, 6, P:2 * P], ACT.Copy).then_inc(R["loT_ready"], 1)
                    act.wait_ge(R["xwa_ready"], seen(R["xwa_ready"]))
                    ac(rb["xwa"], rb["xwa"], ACT.Tanh, scale=0.5).then_inc(R["th_ready"], 1)
                    act.wait_ge(R["cum_sum"], seen(R["cum_sum"]))
                    ac(arr[:, 1].rearrange("p d n -> p (d n)"), pb[:, 6, :], ACT.Exp)
                    ac(rb["s1"].rearrange("p d n -> p (d n)"), pb[:, 6, :], ACT.Exp, scale=-1.0)
                    ac(rb["AC"].rearrange("p d q c -> p (d q) c")[:, :, 2 * i:2 * i + 2], pb[:, 7, 0:8].rearrange("p (a c) -> p a c", c=2), ACT.Exp
                       ).then_inc(R["eL_ready"], 1)
                    act.wait_ge(R["Lx_ready"], seen(R["Lx_ready"]))
                    ac(arr[:, 0], rb["s2"], ACT.Exp).then_inc(R["eLx_ready"], 1)
                    for d in range(2):
                        act.wait_ge(R["arrT_sum"], seen(R["arrT_sum"]))
                        for q in range(NPAIR):
                            ac(rb["arrT"][:, d, q].rearrange("p a t -> p (a t)"), pb[:, 6 + q, :], ACT.Copy)
                            last = ac(rb["RQT"][:, d, q, i * P:(i + 1) * P], pb[:, 6 + q, P:2 * P], ACT.Copy)
                        last.then_inc(R["arrT_ready"], 1)
                end_phase(act, "act")
                for i in tiles_of(l):
                    act.wait_ge(mixT_sum, seen(mixT_sum))
                    ac(mixT[:, i % 2], pb[:, 0:2, :].rearrange("p b (k t) -> p (b k) t", k=4), ACT.Copy).then_inc(mixT_ready, 1)
                    act.wait_ge(y_sum, seen(y_sum))
                    if i >= 1:
                        act.wait_ge(y_used, seen(y_used))
                    ac(ytmp, pb[:, 4 + 2 * (i % 2):6 + 2 * (i % 2), :].rearrange("p b n -> p (b n)"), ACT.Square,
                       accum_out=ssq[:, i:i + 1]).then_inc(y_sq, 1)
                seen(y_used, 1)
                end_phase(act, "act")
                for i in tiles_of(l):
                    act.wait_ge(hT_sum, seen(hT_sum))
                    ac(hT[:, :, i * P:(i + 1) * P], pb[:, 2 * (i % 2):2 * (i % 2) + 2, :].rearrange("p b (k t) -> p (b k) t", k=4), ACT.Copy
                       ).then_inc(hT_ready, 1)
                    act.wait_ge(ms["logit_sum"], seen(ms["logit_sum"]))
                    if i >= 1:
                        act.wait_ge(ms["mask_ready"], seen(ms["mask_ready"]))
                    ac(ex, pb[:, 4, 0:E], ACT.Exp, scale=-1.0).then_inc(ms["ex_ready"], 1)
                    act.wait_ge(ms["shgu_sum"], seen(ms["shgu_sum"]))
                    ac(sh_sg, pb[:, 5, 0:FF], ACT.Silu).then_inc(ms["shg_ready"], 1)
                    act.wait_ge(ms["aT_sum"], seen(ms["aT_sum"]))
                    ac(sh_aT.rearrange("p k t -> p (k t)"), pb[:, 4, 0:2 * P], ACT.Copy).then_inc(ms["aT_ready"], 1)
                    act.wait_ge(ms["dn_sum"], seen(ms["dn_sum"]))
                    ac(acc[:, i, :], pb[:, 6:8, :].rearrange("p b n -> p (b n)"), ACT.Copy).then_inc(ms["sh_ready"], 1)
                seen(ms["mask_ready"])
                end_phase(act, "act")
                end_phase(act, "act")

                def act_walk(S, base):
                    def turned(n, j):
                        act.wait_ge(S.gT_sum, n + 1)
                        ac(gT[:, j % 2].rearrange("p k t -> p (k t)"), pb[:, 0:2, :].rearrange("p b n -> p (b n)"), ACT.Copy).then_inc(S.gT_ready, 1)

                    def body(it, first, last_):
                        for j in range(4):
                            n = it * 4 + j + base
                            if first and j == 0:
                                turned(n, 0)
                            act.wait_ge(S.gu_sum, n + 1)
                            if not (first and j < 2):
                                act.wait_ge(S.act_ready, n - 1)
                            ac(sg[:, j % 2], pb[:, 2 + j % 2, 0:FF], ACT.Silu).then_inc(S.sg_ready, 1)
                            if not (last_ and j == 3):
                                turned(n + 1, j + 1)
                    walk(act, body)

                act_walk(main, E * l)
                end_phase(act, "act")
                act.wait_ge(ms["count_ready"], l + 1)
                most = act.value_load(cnti[0:1, 0:1], min_val=0, max_val=NT * P)
                with act.If(most > CAP):
                    for b in range(1, len(tiles_of(l))):
                        with act.Fori(0, E) as e:
                            act.wait_ge(x_chain[l], x_at(b, e, X_TURN))
                            ac(gT[:, 0].rearrange("p k t -> p (k t)"), pb[:, 0:2, :].rearrange("p b n -> p (b n)"), ACT.Copy).then_inc(x_chain[l], 1)
                            act.wait_ge(x_chain[l], x_at(b, e, X_GU))
                            ac(sg[:, 0], pb[:, 2, 0:FF], ACT.Silu).then_inc(x_chain[l], 1)
                end_phase(act, "act")
                if l == DEPTH - 1:
                    end_phase(act, "act")

        @block.vector
        def _(dve):
            seen, sent = Seen(), Seen()
            V = nc.vector

            def step(ins):
                link(dve, ins, dve_step)

            def power(last):
                last.then_inc(root_in, 1)
                dve.wait_ge(root_out, seen(root_out))

            def inv_root(src, n, eps):
                dst = root[:, 0:src.shape[1]]
                power(V.tensor_scalar(dst, src, 1.0 / n, eps, ALU.mult, ALU.add))
                return dst

            def norm_tile(i, gain, shift_row, dst, tmp):
                step(V.tensor_tensor_reduce(tmp, x[:, i, :], x[:, i, :], 1.0, 0.0, ALU.mult, ALU.add, ssq[:, i:i + 1]))
                rstd = inv_root(ssq[:, i:i + 1], D, EPS)
                step(V.scalar_tensor_tensor(tmp, x[:, i, :], rstd, gain, ALU.mult, ALU.mult))
                return V.tensor_tensor(dst.rearrange("p (k q) -> p q k", k=KD), tmp.rearrange("p (q k) -> p q k", k=KD),
                                       shift_row.rearrange("p (q k) -> p q k", k=KD), ALU.add)

            def residual(i, y, gain, tmp):
                rstd = inv_root(ssq[:, i:i + 1], D, EPS)
                step(V.scalar_tensor_tensor(tmp, y, rstd, gain, ALU.mult, ALU.mult))
                return V.tensor_tensor(x[:, i, :], x[:, i, :], tmp, ALU.add)

            V.memset(minus_half, -0.5)
            step(V.memset(root, 1.0))
            dve.wait_ge(start_in, 48)
            V.tensor_copy(ones_bf, c_("ones"))
            V.tensor_copy(before_bf, c_("before"))
            for l in range(DEPTH):
                dve.wait_ge(ada_rows_in, 80 * (l + 1))
                for c in range(12):
                    dve.wait_ge(ada_sum, 12 * l + c + 1)
                    part = modrow[0:2, c * 512:(c + 1) * 512]
                    last = V.tensor_tensor(part, pb[0:2, (12 * l + c) % 8, :], part, ALU.add)
                    last.then_inc(ada_row, 1)
                dve.wait_ge(ada_row, 12 * (l + 1))
                def mr(j):
                    return modrow[0:2, j * D:(j + 1) * D]
                V.scalar_tensor_tensor(mr(1), mr(1), 1.0, grow[0:2, 0:D], ALU.add, ALU.mult)
                V.tensor_tensor(mr(2), mr(2), grow[0:2, D:2 * D], ALU.mult)
                V.scalar_tensor_tensor(mr(4), mr(4), 1.0, grow[0:2, 2 * D:3 * D], ALU.add, ALU.mult)
                V.tensor_tensor(mr(5), mr(5), grow[0:2, 3 * D:4 * D], ALU.mult).then_inc(mod_rows, 1)
                dve.wait_ge(mod_rows, sent(mod_rows))
            end_phase(dve, "dve")

            def combine(l, i):
                for k in range(TOPK):
                    n = TOPK * (i + sum(len(tiles_of(a)) for a in range(l))) + k
                    dve.wait_ge(y_in[n % NY], 16 * (n // NY + 1))
                    V.scalar_tensor_tensor(acc[:, i, :], ybuf[:, n % NY, :], gk[:, i, k:k + 1], acc[:, i, :], ALU.mult, ALU.add).then_inc(ms["y_used"], 1)
                    dve.wait_ge(ms["y_used"], sent(ms["y_used"]))
                step(V.tensor_tensor_reduce(htmp, acc[:, i, :], acc[:, i, :], 1.0, 0.0, ALU.mult, ALU.add, ssq[:, i:i + 1]))
                step(residual(i, acc[:, i, :], fbc[:, i // NL, :], htmp))

            for l in range(DEPTH):
                dve.wait_ge(bc_in, seen(bc_in, 64))
                if l > 0:
                    dve.wait_ge(ms["f_in"], seen(ms["f_in"], 32))
                for i in range(NT):
                    if l > 0:
                        combine(l - 1, i)
                    if i >= 2:
                        dve.wait_ge(hT_sum, seen(hT_sum))
                    s = i // NL
                    norm_tile(i, bc[:, 2 * s, :], bc[:, 2 * s + 1, :], hbuf[:, i % 2, :], htmp).then_inc(h_ready, 1)
                    dve.wait_ge(h_ready, sent(h_ready))
                seen(hT_sum, 2)
                end_phase(dve, "dve")
                def rope(pe_, co, si, t):
                    n = ROPE // 2
                    V.tensor_tensor(t[:, 0], pe_[:, :, 0:n], si, ALU.mult)
                    step(V.tensor_tensor(t[:, 1], pe_[:, :, n:2 * n], si, ALU.mult))
                    V.tensor_tensor(pe_[:, :, 0:n], pe_[:, :, 0:n], co, ALU.mult)
                    step(V.tensor_tensor(pe_[:, :, n:2 * n], pe_[:, :, n:2 * n], co, ALU.mult))
                    V.tensor_tensor(pe_[:, :, 0:n], pe_[:, :, 0:n], t[:, 1], ALU.subtract)
                    return V.tensor_tensor(pe_[:, :, n:2 * n], pe_[:, :, n:2 * n], t[:, 0], ALU.add)

                def mla_norm(i):
                    zt, zz = za[:, i, :], zn[:, i % 2, :]
                    if i >= 2:
                        dve.wait_ge(znT_sum, NT * l + i - 1)
                    V.tensor_tensor_reduce(zz[:, 0:QL], zt[:, 0:QL], zt[:, 0:QL], 1.0, 0.0, ALU.mult, ALU.add, ssq[:, 0:1])
                    step(V.tensor_tensor_reduce(zz[:, QL:QL + KVL], zt[:, QL:QL + KVL], zt[:, QL:QL + KVL], 1.0, 0.0, ALU.mult, ALU.add, ssq[:, 1:2]))
                    V.tensor_scalar(root[:, 0:1], ssq[:, 0:1], 1.0 / QL, EPS, ALU.mult, ALU.add)
                    power(V.tensor_scalar(root[:, 1:2], ssq[:, 1:2], 1.0 / KVL, EPS, ALU.mult, ALU.add))
                    V.tensor_scalar(zz[:, 0:QL], zt[:, 0:QL], root[:, 0:1], None, ALU.mult)
                    V.tensor_scalar(zz[:, QL:QL + KVL], zt[:, QL:QL + KVL], root[:, 1:2], None, ALU.mult).then_inc(zn_ready, 1)
                    dve.wait_ge(zn_ready, sent(zn_ready))

                def mla_rotate(i):
                    zt = za[:, i, :]
                    k_pe = zt[:, QL + KVL:MLA_IN].rearrange("p (a n) -> p a n", a=1)
                    if i < NL:
                        step(rope(k_pe, cos[:, i:i + 1, :], sin[:, i:i + 1, :], rtmp[:, :, 0:1, :]))
                    dve.wait_ge(qkv_raw, seen(qkv_raw))
                    last = V.tensor_copy(kk_[:, i % 2, :, NOPE:QK], k_pe.broadcast_to([P, H, ROPE]))
                    if i < NL:
                        last = rope(qraw[:, i % 2, :, NOPE:QK], cos[:, i:i + 1, :].broadcast_to([P, H, ROPE // 2]),
                                    sin[:, i:i + 1, :].broadcast_to([P, H, ROPE // 2]), rtmp)
                    last.then_inc(qk_ready, 1)
                    dve.wait_ge(qk_ready, sent(qk_ready))

                mla_norm(0)
                for i in range(NT):
                    if i + 1 < NT:
                        mla_norm(i + 1)
                    mla_rotate(i)
                units = [(i, h) for i in tiles_of(l) for h in range(H)]

                attended = seen(att_sum, 0)

                def maximum(u):
                    i, h = units[u]
                    nk = (NT if i < NL else NT - NL) * P
                    dve.wait_ge(score_sum, seen(score_sum))
                    if u >= 2:
                        dve.wait_ge(probs_ready, seen(probs_ready))
                    step(V.tensor_reduce(mrow[:, u % 2:u % 2 + 1], pb[:, SCORE_BANK[u % 3], 0:nk], AX.X, ALU.max))
                    V.tensor_scalar(mrow[:, u % 2:u % 2 + 1], mrow[:, u % 2:u % 2 + 1], -MLA_SCALE, None, ALU.mult).then_inc(max_ready, 1)
                    dve.wait_ge(max_ready, sent(max_ready))

                def copy_probs(u):
                    i, h = units[u]
                    nk = (NT if i < NL else NT - NL) * P
                    dve.wait_ge(probsT_sum, seen(probsT_sum))
                    if u >= 2:
                        dve.wait_ge(att_sum, attended + u - 1)
                    V.tensor_copy(probsT[:, u % 2].rearrange("p k t -> p (k t)")[:, 0:nk], pb[:, 2 + u % 2, 0:nk]).then_inc(probsT_ready, 1)
                    dve.wait_ge(probsT_ready, sent(probsT_ready))

                def scale_out(i):
                    dve.wait_ge(att_sum, attended + (i + 1) * H)
                    step(V.reciprocal(rinv[:, i, :], rsum[:, i, :]))
                    V.tensor_tensor(mix[:, i, 0:H * VH].rearrange("p (h n) -> p h n", h=H), pb[:, 4 + i % 2, :].rearrange("p (h n) -> p h n", h=H),
                                    rinv[:, i, :].rearrange("p (h a) -> p h a", a=1).broadcast_to([P, H, VH]), ALU.mult).then_inc(att_ready, 1)
                    dve.wait_ge(att_ready, sent(att_ready))

                maximum(0)
                maximum(1)
                for u, (i, h) in enumerate(units):
                    copy_probs(u)
                    if u + 2 < len(units):
                        maximum(u + 2)
                    if h == 2 and i >= 1:
                        scale_out(i - 1)
                scale_out(i)
                seen(att_sum, len(units))
                seen(probs_ready, 2)
                end_phase(dve, "dve")
                dve.wait_ge(pool_in, seen(pool_in, 48))
                for s in range(len(tiles_of(l)) // 2):
                    dve.wait_ge(pool_sum, seen(pool_sum, PG))
                    for t in range(2):
                        V.tensor_tensor(mix[:, 2 * s + t, H * VH:H * VH + PW], pb[:, 2 + 2 * s + t, 0:PW], pool_s, ALU.mult)
                end_phase(dve, "dve")
                R = rs
                dve.wait_ge(R["in"], seen(R["in"], 16 * 13))
                heads = lambda ap: ap.rearrange("p (h n) -> p h n", h=RH)
                over_heads = lambda ap: ap.rearrange("p (h a) -> p h a", a=1).broadcast_to([P, RH, RD])
                over_dirs = lambda ap: ap.rearrange("p (a n) -> p a n", a=1).broadcast_to([P, 2, RW])
                xwa, st, kk, tmp = rb["xwa"], rb["st"], rb["kk"], rb["tmp"]

                def front(i):
                    zs, arr = rb["zs2"][:, i % 2], rb["arr2"][:, i % 2]
                    r_, k_, v_ = zs[:, 0:RW], zs[:, RW:2 * RW], zs[:, 2 * RW:3 * RW]
                    dve.wait_ge(R["shift_sum"], seen(R["shift_sum"]))
                    part = RIN // 2
                    V.tensor_tensor(zs[:, 0:part], pb[:, 6, 0:part], rb["mu"][:, 0:part], ALU.mult)
                    step(V.tensor_tensor(zs[:, part:RIN], pb[:, 7, 0:part], rb["mu"][:, part:RIN], ALU.mult))
                    V.tensor_tensor(zs, zs, zr[:, i, :], ALU.add).then_inc(R["zs_ready"], 1)
                    dve.wait_ge(R["zs_ready"], sent(R["zs_ready"]))
                    step(V.tensor_tensor(kk, k_, rb["k_k"], ALU.mult))
                    step(V.tensor_tensor(tmp[:, 0], kk, kk, ALU.mult))
                    step(V.tensor_reduce(st[:, 0:RH], heads(tmp[:, 0]), AX.X, ALU.add))
                    V.tensor_scalar(root[:, 0:RH], st[:, 0:RH], 1e-24, None, ALU.max).then_inc(root_in, 1)
                    yield
                    dve.wait_ge(root_out, seen(root_out))
                    V.tensor_tensor(heads(kk), heads(kk), over_heads(root[:, 0:RH]), ALU.mult)
                    step(V.tensor_tensor(tmp[:, 0], r_, rb["r_k"], ALU.mult))
                    yield
                    dve.wait_ge(R["lora_sum"], seen(R["lora_sum"]))
                    V.tensor_tensor(xwa.rearrange("p a d n -> p (a d n)"), pb[:, 6:8, :].rearrange("p b n -> p (b n)"), rb["wbias"], ALU.add
                                    ).then_inc(R["xwa_ready"], 1)
                    yield
                    dve.wait_ge(R["th_ready"], seen(R["th_ready"]))
                    V.tensor_scalar(xwa[:, 0], xwa[:, 0], 1.0, 0.5 * DECAY, ALU.add, ALU.mult).then_inc(R["lw_ready"], 1)
                    dve.wait_ge(R["lw_ready"], sent(R["lw_ready"]))
                    step(V.tensor_scalar(xwa[:, 1], xwa[:, 1], 1.0, 0.5, ALU.add, ALU.mult))
                    V.tensor_tensor(arr[:, 2], xwa[:, 1], over_dirs(kk), ALU.mult)
                    step(V.scalar_tensor_tensor(arr[:, 3], xwa[:, 1], -1.0, over_dirs(rb["k_a"]), ALU.add, ALU.mult))
                    step(V.scalar_tensor_tensor(arr[:, 3], arr[:, 3], 1.0, over_dirs(k_), ALU.add, ALU.mult))
                    step(V.tensor_tensor(tmp[:, 1], arr[:, 3, 0, :], arr[:, 3, 1, :], ALU.add))
                    step(V.tensor_tensor(tmp[:, 0], tmp[:, 0], tmp[:, 1], ALU.mult))
                    step(V.tensor_reduce(st[:, RH:2 * RH], heads(tmp[:, 0]), AX.X, ALU.add))
                    V.tensor_tensor(heads(rb["bonus"][:, i, :]), heads(v_), over_heads(st[:, RH:2 * RH]), ALU.mult)
                    yield
                    dve.wait_ge(R["cum_sum"], seen(R["cum_sum"]))
                    dve.wait_ge(R["eL_ready"], seen(R["eL_ready"]))
                    V.tensor_tensor(rb["s2"], pb[:, 6, :].rearrange("p (d n) -> p d n", d=2), xwa[:, 0], ALU.subtract).then_inc(R["Lx_ready"], 1)
                    V.tensor_copy(rb["g"][:, i, :], pb[:, 7, 8:8 + RW])
                    V.tensor_tensor(arr[:, 1], arr[:, 1], over_dirs(r_), ALU.mult)
                    V.tensor_tensor(arr[:, 2], arr[:, 2], rb["s1"], ALU.mult)
                    V.tensor_tensor(arr[:, 3], arr[:, 3], rb["s1"], ALU.mult)
                    dve.wait_ge(R["eLx_ready"], seen(R["eLx_ready"]))
                    V.tensor_tensor(arr[:, 0], arr[:, 0], over_dirs(kk), ALU.mult).then_inc(R["arr_ready"], 1)
                    dve.wait_ge(R["arr_ready"], sent(R["arr_ready"]))

                for _ in front(0):
                    pass
                for i in range(NT):
                    arr = rb["arr2"][:, i % 2]
                    ahead = front(i + 1) if i + 1 < NT else iter(())
                    for d in range(2):
                        dve.wait_ge(R["mats_sum"], seen(R["mats_sum"]))
                        lv0 = lambda dd: levels[:, dd, 0:1, :].broadcast_to([P, NPAIR, P])
                        m2 = masks[:, d].rearrange("p m t -> p (m t)").rearrange("p (a n) -> p a n", a=1).broadcast_to([P, NPAIR, 2 * P])
                        for r in range(2):
                            mine = lambda nm: rb[nm][:, d].rearrange("p (q r) t -> p r q t", r=2)[:, r]
                            mine2 = lambda nm: rb[nm][:, d].rearrange("p (q r) m t -> p r q (m t)", r=2)[:, r]
                            lg = pb[:, r, :].rearrange("p (q n) -> p q n", q=2)
                            mg = pb[:, 2 + r, :].rearrange("p (q n) -> p q n", q=2)
                            V.tensor_tensor(mine("X"), pb[:, 4 + r, 0:2 * P].rearrange("p (q t) -> p q t", q=2), lv0(d), ALU.mult)
                            V.tensor_tensor(mine("XT"), lg[:, :, 0:P], lv0(1 - d), ALU.mult)
                            V.tensor_tensor(mine2("LG"), lg, m2, ALU.mult)
                            last = V.tensor_tensor(mine2("MG"), mg, m2, ALU.mult)
                        step(last)
                        eye = ident.rearrange("p (a t) -> p a t", a=1).broadcast_to([P, RH, P])
                        V.tensor_tensor(rb["X"][:, d], rb["X"][:, d], eye, ALU.add)
                        last = V.tensor_tensor(rb["XT"][:, d], rb["XT"][:, d], eye, ALU.add)
                        last.then_inc(R["mats_ready"], 1)
                        dve.wait_ge(R["mats_ready"], sent(R["mats_ready"]))
                    for lv in range(1, 6):
                        for d in range(2):
                            dve.wait_ge(R["t1_sum"], seen(R["t1_sum"]))
                            V.tensor_tensor(rb["T1"][:, d], pb[:, 4 + d, :].rearrange("p (h t) -> p h t", h=RH),
                                            levels[:, d, lv:lv + 1, :].broadcast_to([P, RH, P]), ALU.mult).then_inc(R["t1_ready"], 1)
                        if lv == 5:
                            for d in range(2):
                                dve.wait_ge(R["mv_sum"], seen(R["mv_sum"]))
                                V.tensor_copy(rb["KMV"][:, d, :, 0, :], heads(arr[:, 0, d, :]))
                                V.tensor_copy(rb["KMV"][:, d, :, 1, :], heads(pb[:, d, 0:RW])).then_inc(R["kmv_ready"], 1)
                        for d in range(2):
                            dve.wait_ge(R["x_sum"], seen(R["x_sum"]))
                            if lv < 5:
                                V.tensor_tensor(rb["X"][:, d], pb[:, d, :].rearrange("p (h t) -> p h t", h=RH), rb["X"][:, d], ALU.add)
                            V.tensor_tensor(rb["XT"][:, d], pb[:, 2 + d, :].rearrange("p (h t) -> p h t", h=RH), rb["XT"][:, d], ALU.add
                                            ).then_inc(R["x_ready"], 1)
                        dve.wait_ge(R["x_ready"], sent(R["x_ready"], 2))
                        next(ahead, None)
                    for d in range(2):
                        dve.wait_ge(R["nx_sum"], seen(R["nx_sum"]))
                        V.tensor_scalar(rb["nX"][:, d].rearrange("p m h n -> p h m n"), pb[:, 4 + d, :].rearrange("p (h m n) -> p h m n", h=RH, m=2),
                                        -1.0, None, ALU.mult).then_inc(R["nx_ready"], 1)
                    dve.wait_ge(R["fin_sum"], seen(R["fin_sum"]))
                    V.tensor_copy(rb["YV"][:, i, :], pb[:, 0, 0:RW])
                    rq = rb["RQT"].rearrange("p d q t -> p (d q) t")[:, :, i * P:(i + 1) * P]
                    V.tensor_tensor(rq, pb[:, 1, :].rearrange("p (a t) -> p a t", a=4), rq, ALU.add)
                    eye2 = c_("eye2").rearrange("p (a k) -> p a k", a=1)
                    for c in range(2):
                        cc = 2 * i + c
                        V.tensor_tensor(rb["TT"].rearrange("p d q c k -> p (d q) c k")[:, :, cc, :], pb[:, 2 + 2 * c, 0:4 * C].rearrange("p (a k) -> p a k", a=4),
                                        eye2.broadcast_to([P, 4, C]), ALU.add)
                        last = V.tensor_tensor(rb["W"].rearrange("p d q c k -> p (d q) c k")[:, :, cc, :], pb[:, 3 + 2 * c, 0:4 * C].rearrange("p (a k) -> p a k", a=4),
                                               rb["AC"].rearrange("p d q c -> p (d q) c")[:, :, cc:cc + 1].broadcast_to([P, 4, C]), ALU.mult)
                    last.then_inc(R["fin_ready"], 1)
                    dve.wait_ge(R["fin_ready"], sent(R["fin_ready"]))
                for d in range(2):
                    c0, c1 = ORDER[d][0], ORDER[d][1]
                    V.tensor_copy(rb["Z"][:, d, :, c1, :], rb["W"][:, d, :, c0, :]).then_inc(R["chain_ready"], 1)
                    dve.wait_ge(R["chain_ready"], sent(R["chain_ready"]))
                for n in range(1, NC - 1):
                    for d in range(2):
                        dve.wait_ge(R["chain_sum"], seen(R["chain_sum"]))
                        cp, cn = ORDER[d][n], ORDER[d][n + 1]
                        for q in range(NPAIR):
                            last = V.scalar_tensor_tensor(rb["Z"][:, d, q, cn, :], pb[:, d, q * RD:(q + 1) * RD], rb["AC"][:, d, q, cp:cp + 1],
                                                          rb["W"][:, d, q, cp, :], ALU.mult, ALU.add)
                        last.then_inc(R["chain_ready"], 1)
                        dve.wait_ge(R["chain_ready"], sent(R["chain_ready"]))
                Y = rb["s1"].rearrange("p d n -> p (d n)")[:, 0:RW]
                SQ = rb["s2"].rearrange("p d n -> p (d n)")[:, 0:RW]
                st = rb["st"]
                for i in tiles_of(l):
                    dve.wait_ge(R["inter_sum"], seen(R["inter_sum"]))
                    for r in range(2):
                        by_pair = lambda ap: ap.rearrange("p (q r n) -> p r q n", r=2, n=RD)[:, r]
                        last = V.tensor_tensor(by_pair(Y), pb[:, 4 + 2 * (i % 2) + r, 0:NPAIR * RD].rearrange("p (q n) -> p q n", n=RD),
                                               by_pair(rb["YV"][:, i, :]), ALU.add)
                    last.then_inc(R["inter_used"], 1)
                    dve.wait_ge(R["inter_used"], sent(R["inter_used"]))
                    step(V.tensor_reduce(st[:, 0:RH], heads(Y), AX.X, ALU.add))
                    step(V.tensor_scalar(st[:, 0:RH], st[:, 0:RH], -1.0 / RD, None, ALU.mult))
                    step(V.tensor_tensor(heads(Y), heads(Y), over_heads(st[:, 0:RH]), ALU.add))
                    step(V.tensor_tensor(SQ, Y, Y, ALU.mult))
                    step(V.tensor_reduce(st[:, RH:2 * RH], heads(SQ), AX.X, ALU.add))
                    step(V.tensor_tensor(heads(Y), heads(Y), over_heads(inv_root(st[:, RH:2 * RH], RD, GN_EPS)), ALU.mult))
                    step(V.tensor_tensor(Y, Y, rb["ln_w"], ALU.mult))
                    step(V.tensor_tensor(Y, Y, rb["ln_b"], ALU.add))
                    step(V.tensor_tensor(Y, Y, rb["bonus"][:, i, :], ALU.add))
                    step(V.tensor_tensor(mix[:, i, H * VH + PW:D], Y, rb["g"][:, i, :], ALU.mult))
                end_phase(dve, "dve")
                dve.wait_ge(w_out_in, seen(w_out_in, 96))
                for i in tiles_of(l):
                    dve.wait_ge(y_sq, seen(y_sq))
                    residual(i, pb[:, 4 + 2 * (i % 2):6 + 2 * (i % 2), :].rearrange("p b n -> p (b n)"), gbc[:, i // NL, :], ytmp).then_inc(y_used, 1)
                    dve.wait_ge(y_used, sent(y_used))
                end_phase(dve, "dve")
                nt = len(tiles_of(l))
                dve.wait_ge(ms["in"], seen(ms["in"], 16 * (5 + 2 * (nt // 2))))
                step(V.memset(zero64, 0.0))
                iota = c_("iota")
                for i in range(nt):
                    if i >= 2:
                        dve.wait_ge(ms["h_out"], 16 * (sum(len(tiles_of(a)) for a in range(l)) + i - 1))
                        dve.wait_ge(hT_sum, seen(hT_sum))
                    s = i // NL
                    norm_tile(i, mbc[:, 2 * s, :], mbc[:, 2 * s + 1, :], mh[:, i % 2, :], mtmp).then_inc(h_ready, 1)
                    dve.wait_ge(h_ready, sent(h_ready))
                    dve.wait_ge(ms["ex_ready"], seen(ms["ex_ready"]))
                    step(V.tensor_scalar(sc_, ex, 1.0, None, ALU.add))
                    step(V.reciprocal(sc_, sc_))
                    step(V.tensor_tensor(sel, sc_, rbias, ALU.add))
                    for g in range(NG):
                        last = V.max(g8[:, g, :], sel[:, g * EG:(g + 1) * EG])
                    step(last)
                    step(V.tensor_tensor(small8[:, 0, :], g8[:, :, 0], g8[:, :, 1], ALU.add))
                    step(V.max(small8[:, 1, :], small8[:, 0, :]))
                    step(V.max_index(idx8, small8[:, 1, :], small8[:, 0, :]))
                    step(V.tensor_copy(small8[:, 2, :], idx8))

                    def chosen(dst, n, count):
                        q = eq[:, 0:n * count].rearrange("p (n k) -> p n k", n=n)
                        step(V.tensor_tensor(q, iota[:, 0:n].rearrange("p (n a) -> p n a", a=1).broadcast_to([P, n, count]),
                                             small8[:, 2:3, 0:count].broadcast_to([P, n, count]), ALU.is_equal))
                        step(V.tensor_reduce(dst, q, AX.X, ALU.add))

                    chosen(small8[:, 3, :], NG, TG)
                    step(V.tensor_scalar(small8[:, 3, :], small8[:, 3, :], -1.0, 1e30, ALU.add, ALU.mult))
                    step(V.tensor_tensor(sel.rearrange("p (g n) -> p g n", g=NG), sel.rearrange("p (g n) -> p g n", g=NG),
                                         small8[:, 3, :].rearrange("p (g a) -> p g a", a=1).broadcast_to([P, NG, EG]), ALU.add))
                    step(V.max(small8[:, 1, :], sel))
                    step(V.max_index(idx8, small8[:, 1, :], sel))
                    step(V.tensor_copy(small8[:, 2, :], idx8))
                    chosen(mask[:, i, :], E, TOPK)
                    step(V.tensor_tensor(gates, sc_, mask[:, i, :], ALU.mult))
                    step(V.tensor_reduce(small8[:, 4, 0:1], gates, AX.X, ALU.add))
                    step(V.reciprocal(small8[:, 4, 0:1], small8[:, 4, 0:1]))
                    step(V.tensor_scalar(gates, gates, small8[:, 4, 0:1], ROUTED, ALU.mult, ALU.mult))
                    step(V.tensor_tensor_scan(incl, mask[:, i, :], zero64, 0.0, ALU.add, ALU.add))
                    step(V.tensor_tensor(incl, incl, mask[:, i, :], ALU.mult))
                    q = eq[:, 0:TOPK * E].rearrange("p (k n) -> p k n", k=TOPK)
                    step(V.tensor_tensor(q, incl.rearrange("p (a n) -> p a n", a=1).broadcast_to([P, TOPK, E]),
                                         iota[:, 1:TOPK + 1].rearrange("p (k a) -> p k a", a=1).broadcast_to([P, TOPK, E]), ALU.is_equal))
                    step(V.tensor_tensor(q, q, gates.rearrange("p (a n) -> p a n", a=1).broadcast_to([P, TOPK, E]), ALU.mult))
                    step(V.tensor_reduce(gk[:, i, 0:TOPK], q, AX.X, ALU.add))
                    V.tensor_copy(meta[:, i, :, 0], c_("tok").broadcast_to([P, E]))
                    V.memset(meta[:, i, :, 1], float(i))
                    V.tensor_scalar(meta[:, i, :, 2], incl, -1.0, None, ALU.add)
                    V.memset(meta[:, i, :, 3], 1.0)
                    step(V.tensor_copy(mask_bf[:, i, :], mask[:, i, :]))
                    dve.wait_ge(ms["shg_ready"], seen(ms["shg_ready"]))
                    V.tensor_tensor(sh_act.rearrange("p (k q) -> p q k", k=2), sh_sg.rearrange("p (q k) -> p q k", k=2),
                                    pb[:, 5, FF:2 * FF].rearrange("p (q k) -> p q k", k=2), ALU.mult).then_inc(ms["act_ready"], 1)
                    dve.wait_ge(ms["act_ready"], sent(ms["act_ready"]))
                    V.tensor_copy(small8[:, 5, 0:1], small8[:, 4, 0:1]).then_inc(ms["mask_ready"], 1)
                    dve.wait_ge(ms["mask_ready"], sent(ms["mask_ready"]))
                seen(hT_sum, 2)
                dve.wait_ge(ms["pos_sum"], seen(ms["pos_sum"]))
                step(V.scalar_tensor_tensor(posm[:, 0:nt, :], pb[:, 0, 0:nt * E].rearrange("p (i e) -> p i e", i=nt), 1.0, mask[:, 0:nt, :], ALU.add, ALU.mult))
                step(V.tensor_scalar(posm[:, 0:nt, :], posm[:, 0:nt, :], -1.0, None, ALU.add))
                step(V.tensor_reduce(cntf, pb[:, 0, nt * E:(nt + 1) * E], AX.X, ALU.max))
                V.tensor_copy(cnti, cntf).then_inc(ms["count_ready"], 1)
                end_phase(dve, "dve")

                def slots(b, ready, step):
                    step(V.tensor_scalar(posb[:, 0:nt, :], posm[:, 0:nt, :], -float(b * CAP), None, ALU.add))
                    for i in range(nt):
                        last = V.tensor_tensor(onehot[:, i], iota[:, 0:CAP].rearrange("p (a s) -> p a s", a=1).broadcast_to([P, E, CAP]),
                                               posb[:, i, :].rearrange("p (e a) -> p e a", a=1).broadcast_to([P, E, CAP]), ALU.is_equal)
                    last.then_inc(ready, 1)

                def index_tables(step):
                    t = pb[:, 0, 0:4 * E].rearrange("p (e c) -> p e c", c=4)
                    V.tensor_scalar(tabf[:, 0, :], t[:, :, 1], float(P), None, ALU.mult)
                    step(V.tensor_scalar(tabf[:, 1, :], t[:, :, 3], -OUT_OF_RANGE, OUT_OF_RANGE, ALU.mult, ALU.add))
                    step(V.tensor_tensor(tabf[:, 0, :], t[:, :, 0], tabf[:, 0, :], ALU.add))
                    step(V.scalar_tensor_tensor(tabf[:, 2, :], tabf[:, 0, :], float(TOPK), tabf[:, 1, :], ALU.mult, ALU.add))
                    step(V.tensor_tensor(tabf[:, 2, :], t[:, :, 2], tabf[:, 2, :], ALU.add))
                    step(V.tensor_tensor(tabf[:, 0, :], tabf[:, 0, :], tabf[:, 1, :], ALU.add))
                    V.tensor_copy(gi, tabf[:, 0, :])
                    return V.tensor_copy(si, tabf[:, 2, :])

                slots(0, ms["onehot_ready"], step)
                dve.wait_ge(ms["tab_sum"], seen(ms["tab_sum"]))
                V.memset(gx, 0.0)
                step(index_tables(step))
                end_phase(dve, "dve")

                def dve_walk(S, base):
                    def rows(it, j, n, waits):
                        dve.wait_ge(S.dn_sum, n + 1)
                        if waits:
                            dve.wait_ge(S.y_out[j % 4], 16 * (it + base // 4 + j // 4))
                        V.tensor_copy(yx[:, j % 4], pb[:, 5:7, :].rearrange("p b n -> p (b n)")).then_inc(S.y_ready, 1)

                    def body(it, first, last_):
                        for j in range(4):
                            n = it * 4 + j + base
                            dve.wait_ge(S.sg_ready, n + 1)
                            if not (first and j < 2):
                                dve.wait_ge(S.aT_sum, n - 1)
                            V.tensor_tensor(actx[:, j % 2].rearrange("p (k q) -> p q k", k=2), sg[:, j % 2].rearrange("p (q k) -> p q k", k=2),
                                            pb[:, 2 + j % 2, FF:2 * FF].rearrange("p (q k) -> p q k", k=2), ALU.mult).then_inc(S.act_ready, 1)
                            if not (first and j == 0):
                                rows(it, j - 1, n - 1, not first)
                            dve.wait_ge(S.aT_sum, n + 1)
                            if not (first and j < 2):
                                dve.wait_ge(S.dn_sum, n - 1)
                            V.tensor_copy(aT[:, j % 2].rearrange("p k t -> p (k t)"), pb[:, 4, 0:2 * P]).then_inc(S.aT_ready, 1)
                    walk(dve, body)
                    rows(E // 4 - 1, 3, base + E - 1, True)

                dve_walk(main, E * l)
                end_phase(dve, "dve")
                dve.wait_ge(ms["count_ready"], l + 1)
                most = dve.value_load(cnti[0:1, 0:1], min_val=0, max_val=NT * P)
                with dve.If(most > CAP):
                    xstep = lambda ins: link(dve, ins, x_step[l])
                    for b in range(1, nt):
                        if b > 1:
                            dve.wait_ge(x_chain[l], x_at(b, 0) - X_TAB)
                        slots(b, x_chain[l], xstep)
                        dve.wait_ge(x_chain[l], x_at(b, 0) - 1)
                        xstep(index_tables(xstep))
                        dve.engine_nop().then_inc(x_chain[l], 1)
                        with dve.Fori(0, E) as e:
                            dve.wait_ge(x_chain[l], x_at(b, e, X_SILU))
                            V.tensor_tensor(actx[:, 0].rearrange("p (k q) -> p q k", k=2), sg[:, 0].rearrange("p (q k) -> p q k", k=2),
                                            pb[:, 2, FF:2 * FF].rearrange("p (q k) -> p q k", k=2), ALU.mult).then_inc(x_chain[l], 1)
                            dve.wait_ge(x_chain[l], x_at(b, e, X_AT))
                            V.tensor_copy(aT[:, 0].rearrange("p k t -> p (k t)"), pb[:, 4, 0:2 * P]).then_inc(x_chain[l], 1)
                            dve.wait_ge(x_chain[l], x_at(b, e, X_DN))
                            V.tensor_copy(yx[:, 0], pb[:, 5:7, :].rearrange("p b n -> p (b n)")).then_inc(x_chain[l], 1)
                end_phase(dve, "dve")
                if l == DEPTH - 1:
                    dve.wait_ge(ms["f_in"], seen(ms["f_in"], 16 * (nt // 2)))
                    for i in range(nt):
                        combine(l, i)
                    end_phase(dve, "dve")

        @block.gpsimd
        def _(pool):
            seen = Seen()

            def roots(n):
                for _ in range(n):
                    pool.wait_ge(root_in, seen(root_in))
                    nc.gpsimd.tensor_tensor(root, root, minus_half, ALU.pow).then_inc(root_out, 1)

            end_phase(pool, "pool")
            for l in range(DEPTH):
                for k in range(1, 6):
                    if k == 2:
                        nc.gpsimd.memset(rb["loraW"], 0.0).then_inc(rs["zero"], 1)
                    nt = len(tiles_of(l))
                    roots({1: NT, 2: NT, 3: 0, 4: NT + nt, 5: nt}[k])
                    end_phase(pool, "pool")
                roots(len(tiles_of(l)))
                end_phase(pool, "pool")
                end_phase(pool, "pool")

                def row_walk(S, base):
                    def gather(e, n, j):
                        nc.gpsimd.tensor_copy(idx_now[:, j:j + 1], gi[:, bass.ds(e, 1)]).then_inc(S.gather_idx, 1)
                        pool.wait_ge(S.gather_idx, n + 1)
                        pool.sem_inc(wait_held, 1)
                        nc.gpsimd.indirect_dma_start(gx[:, j, :], None, h_dram, bass.IndirectOffsetOnAxis(ap=idx_now[:, j:j + 1], axis=0),
                                                     bounds_check=NT * P - 1, oob_is_err=False).then_inc(S.g_in[j], 16)

                    def body(it, first, last_):
                        if first:
                            for a in range(4):
                                gather(a, base + a, a)
                        for j in range(4):
                            e = it * 4 + j
                            n = e + base
                            if not last_:
                                pool.wait_ge(S.gT_sum, n + 1)
                                gather(e + 4, n + 4, j)
                            pool.wait_ge(S.y_ready, n + 1)
                            sl = idx_now[:, 4 + j:5 + j]
                            if not first:
                                pool.wait_ge(S.y_out[j], 16 * (base // 4 + it))
                            nc.gpsimd.tensor_copy(sl, si[:, bass.ds(e, 1)]).then_inc(S.scatter_idx, 1)
                            pool.wait_ge(S.scatter_idx, n + 1)
                            pool.sem_inc(wait_held, 1)
                            nc.gpsimd.indirect_dma_start(y_dram, bass.IndirectOffsetOnAxis(ap=sl, axis=0), yx[:, j, :], None,
                                                         bounds_check=NT * P * TOPK - 1, oob_is_err=False).then_inc(S.y_out[j], 16)
                    walk(pool, body)
                    for j in range(4):
                        pool.wait_ge(S.y_out[j], 16 * (base // 4 + E // 4))

                row_walk(main, E * l)
                end_phase(pool, "pool")
                pool.wait_ge(ms["count_ready"], l + 1)
                most = pool.value_load(cnti[0:1, 0:1], min_val=0, max_val=NT * P)
                with pool.If(most > CAP):
                    for b in range(1, len(tiles_of(l))):
                        with pool.Fori(0, E) as e:
                            pool.wait_ge(x_chain[l], x_at(b, e))
                            nc.gpsimd.tensor_copy(idx_now[:, 0:1], gi[:, bass.ds(e, 1)]).then_inc(x_chain[l], 1)
                            pool.wait_ge(x_chain[l], x_at(b, e, X_IDX))
                            pool.sem_inc(wait_held, 1)
                            nc.gpsimd.indirect_dma_start(gx[:, 0, :], None, h_dram, bass.IndirectOffsetOnAxis(ap=idx_now[:, 0:1], axis=0),
                                                         bounds_check=NT * P - 1, oob_is_err=False).then_inc(x_rows[l], 16)
                            pool.wait_ge(x_chain[l], x_at(b, e, X_Y))
                            nc.gpsimd.tensor_copy(idx_now[:, 1:2], si[:, bass.ds(e, 1)]).then_inc(x_chain[l], 1)
                            pool.wait_ge(x_chain[l], x_at(b, e, X_SIDX))
                            pool.sem_inc(wait_held, 1)
                            nc.gpsimd.indirect_dma_start(y_dram, bass.IndirectOffsetOnAxis(ap=idx_now[:, 1:2], axis=0), yx[:, 0, :], None,
                                                         bounds_check=NT * P * TOPK - 1, oob_is_err=False).then_inc(x_out[l], 16)
                            pool.wait_ge(x_out[l], 16 * ((b - 1) * E + e + 1))
                            pool.sem_inc(x_chain[l], 1)
                end_phase(pool, "pool")
                roots(len(tiles_of(l)))
                if l == DEPTH - 1:
                    end_phase(pool, "pool")



_INS = ['x', 'c', 'ctx', 'c_ctx', 'ada_w', 'ada_b', 'pre_mix_g', 'post_mix_g', 'pre_ffn_g', 'post_ffn_g', 'w_in', 'w_out',
        'mla_q_norm', 'mla_w_q_b', 'mla_kv_norm', 'mla_w_kv_b', 'pool_w', 'pool_scale', 'rwkv_mu', 'rwkv_w0', 'rwkv_w2',
        'rwkv_a0', 'rwkv_a2', 'rwkv_g2', 'rwkv_k_k', 'rwkv_k_a', 'rwkv_r_k', 'rwkv_ln_w', 'rwkv_ln_b', 'router_w',
        'router_bias', 'exp_w_gate', 'exp_w_up', 'exp_w_down', 'sh_w_gate', 'sh_w_up', 'sh_w_down']


def kernel(**inputs):
    import numpy as _np
    import concourse.bacc as _bacc
    from concourse import mybir as _mybir
    from concourse.bass_utils import run_bass_kernel_spmd as _run

    nc = _bacc.Bacc("TRN2", target_bir_lowering=False, num_devices=1)
    arrays, args = {}, {}
    const, _, pool = lay_constants()
    for name, a in [(n, inputs[n]) for n in _INS] + [("shape_consts", const), ("pool_matrix", pool)]:
        a = _np.ascontiguousarray(a)
        arrays[f"in_{name}_dram"] = a
        args[name] = nc.dram_tensor(f"in_{name}_dram", a.shape, _mybir.dt.from_np(a.dtype), kind="ExternalInput").ap()
    out = nc.dram_tensor("out_0_dram", (1, SEQ, D), _mybir.dt.float32, kind="ExternalOutput").ap()
    trunk_kernel(nc, args, out)
    r = _run(nc, [arrays], core_ids=[0])
    return r.results[0]["out_0_dram"]
```

```python
from contextlib import ExitStack

import numpy as np
import concourse.bass as bass
from concourse import mybir

ALU = mybir.AluOpType
ACT = mybir.ActivationFunctionType
AX = mybir.AxisListType
F32 = mybir.dt.float32
BF16 = mybir.dt.bfloat16
I32 = mybir.dt.int32
U32 = mybir.dt.uint32

P = 128
D = 1024
KD = D // P
SEQ, CTX = 256, 256
NT = (SEQ + CTX) // P
NL = SEQ // P
DEPTH = 2
GRID_W = 64
EPS = 1e-6
H, NOPE, ROPE, VH = 8, 64, 32, 64
QK = NOPE + ROPE
QL, KVL = 384, 256
MLA_IN = QL + KVL + ROPE
MLA_SCALE = QK ** -0.5
WINDOWS = (2, 4, 8, 16)
PG, PC = 4, 64
PW = PG * PC
RH, RD = 4, 64
RW = RH * RD
LORA, GLORA = 32, 64
RIN = 3 * RW + 4 * LORA + GLORA
INW = MLA_IN + PW + RIN
GN_EPS = 64e-5
C = 64
NPAIR = RH // 2
E, TOPK, FF, NG, TG = 64, 6, 256, 8, 4
EG = E // NG
ROUTED = 2.5
CAP = 128
ROWS = (128, 96)
OUT_OF_RANGE = 65536.0
DECAY = -float(np.exp(-0.5))


def lay_constants():
    t = np.arange(P)
    same = (t[:, None] // C) == (t[None, :] // C)
    parts = {}
    parts["ident"] = np.eye(P)
    strict = (t[:, None] < t[None, :]) & same
    incl = (t[:, None] <= t[None, :]) & same
    parts["mask_st"] = np.concatenate([strict, incl, strict.T, incl.T], 1)
    parts["cum"] = np.concatenate([incl, incl.T], 1)
    lv = []
    for d in range(2):
        for s in [1, 2, 4, 8, 16, 32]:
            blk = (t[:, None] // (2 * s)) == (t[None, :] // (2 * s))
            m = blk & ((t[:, None] // s) % 2 == 1) & ((t[None, :] // s) % 2 == 0)
            lv.append(-(m if d == 0 else m.T).astype(np.float64))
    parts["levels"] = np.concatenate(lv, 1)
    parts["chunk_of"] = np.stack([t < C, t >= C], 1)
    tt = np.arange(SEQ)
    sh = 0.5 * (np.abs(tt[:, None] - tt[None, :]) == 1) - np.eye(SEQ)
    parts["shift"] = np.concatenate([sh[0:P], sh[P:SEQ]], 1)
    row, col = tt // GRID_W, tt % GRID_W
    inv = np.float32(10000.0) ** (-np.arange(ROPE // 4, dtype=np.float32) / np.float32(ROPE // 4))
    ang = np.concatenate([row[:, None].astype(np.float32) * inv, col[:, None].astype(np.float32) * inv], 1)
    for nm, f in (("cos", np.cos), ("sin", np.sin)):
        v = f(ang.astype(np.float32))
        parts[nm] = np.concatenate([v[0:P], v[P:SEQ]], 1)
    parts["iota"] = np.broadcast_to(np.arange(P)[None, :], (P, P))
    parts["before"] = t[:, None] < t[None, :]
    parts["tok"] = t[:, None]
    parts["eye2"] = np.tile(np.eye(C), (2, 1))
    parts["ones"] = np.ones((P, P))
    at, cols, n = {}, [], 0
    for k, v in parts.items():
        v = np.asarray(v, np.float32)
        at[k] = (n, n + v.shape[1])
        n += v.shape[1]
        cols.append(v)
    pool = []
    for w in WINDOWS:
        lo, hi = np.clip(tt - w // 2, 0, SEQ), np.clip(tt + w // 2, 0, SEQ)
        m = ((tt[None, :] >= lo[:, None]) & (tt[None, :] < hi[:, None])) / (hi - lo)[:, None] - np.eye(SEQ)
        pool.append(m.T)
    pool = np.stack(pool, 0).reshape(PG, 2, P, SEQ).transpose(2, 1, 0, 3).reshape(P, 2 * PG * SEQ)
    return np.ascontiguousarray(np.concatenate(cols, 1)), at, np.ascontiguousarray(pool, np.float32)


class Seen:

    def __init__(self):
        self.n = {}

    def __call__(self, sem, by=1):
        self.n[id(sem)] = self.n.get(id(sem), 0) + by
        return self.n[id(sem)]


class Region:

    def __init__(self, arena, start, end):
        self.arena, self.at, self.end = arena, start, end

    def take(self, n, dt=F32):
        a = self.arena[:, self.at:self.at + n]
        self.at += n
        assert self.at <= self.end, (self.at, self.end)
        return a if dt == F32 else a.bitcast(dt)


def trunk_kernel(nc, A, out):
    const_cols, at, _ = lay_constants()
    NCONST = const_cols.shape[1]
    ctx = ExitStack()
    with ctx:
        def sem(name):
            return ctx.enter_context(nc.semaphore(name))

        mod_dram = nc.dram_tensor("mod_rows", [DEPTH, 2, 6 * D], F32).ap()
        h_dram = nc.dram_tensor("h_rows", [NT * P, D], F32).ap()
        y_dram = nc.dram_tensor("y_rows", [NT * P * TOPK, D], F32).ap()

        AR = 53100
        arena = ctx.enter_context(nc.sbuf_tensor("arena", [P, AR], F32))
        pb = ctx.enter_context(nc.psum_tensor("pb", [P, 8, 512], F32))

        fixed = Region(arena, 0, AR)
        x = fixed.take(NT * D).rearrange("p (i d) -> p i d", i=NT)
        cst = fixed.take(NCONST)
        small = fixed.take(128)
        ones_bf = fixed.take(64, BF16)
        before_bf = fixed.take(64, BF16)
        R0 = fixed.at

        def c_(name):
            return cst[:, at[name][0]:at[name][1]]

        ident = c_("ident")
        masks = c_("mask_st").rearrange("p (d m t) -> p d m t", d=2, m=2)
        cum = c_("cum").rearrange("p (d t) -> p d t", d=2)
        levels = c_("levels").rearrange("p (d l t) -> p d l t", d=2, l=6)
        shift = c_("shift").rearrange("p (k t) -> p k t", k=2)
        cos = c_("cos").rearrange("p (i f) -> p i f", i=NL)
        sin = c_("sin").rearrange("p (i f) -> p i f", i=NL)

        sreg = Region(small, 0, 128)
        cs = sreg.take(2 * KD).rearrange("p (k s) -> p k s", s=2)
        craw = sreg.take(2 * KD).rearrange("p (s k) -> p s k", s=2)
        ssq = sreg.take(16)
        root = sreg.take(16)
        minus_half = sreg.take(16)
        qcol = sreg.take(QL // P)
        kvcol = sreg.take(KVL // P)
        gk = sreg.take(NT * 8).rearrange("p (i k) -> p i k", i=NT)

        phase_end = sem("phase_end")
        phases = {}

        def end_phase(eng, name):
            phases[name] = phases.get(name, 0) + 1
            eng.drain().then_inc(phase_end, 1)
            eng.wait_ge(phase_end, 5 * phases[name])

        start_in = sem("start_in")
        c_in = sem("c_in")
        ada_in = [sem(f"ada_in{j}") for j in range(3)]
        ada_rows_in = sem("ada_rows_in")
        silu_c = sem("silu_c")
        ada_sum = sem("ada_sum")
        ada_row = sem("ada_row")
        mod_rows = sem("mod_rows_ready")
        mod_out = sem("mod_out")
        bc_in = [sem(f"bc_in{s}") for s in range(2)]
        h_ready = sem("h_ready")
        hT_sum = sem("hT_sum")
        hT_ready = sem("hT_ready")
        w_in_in = [sem(f"w_in_in{c}") for c in range(4)]
        z_sum = sem("z_sum")
        z_ready = sem("z_ready")
        mla_in = sem("mla_in")
        zn_ready = sem("zn_ready")
        znT_sum = sem("znT_sum")
        znT_ready = sem("znT_ready")
        qkv_sum = sem("qkv_sum")
        qkv_raw = sem("qkv_raw")
        qk_ready = sem("qk_ready")
        qkT_sum = sem("qkT_sum")
        qkT_ready = sem("qkT_ready")
        score_sum = sem("score_sum")
        max_ready = sem("max_ready")
        probs_ready = sem("probs_ready")
        probsT_sum = sem("probsT_sum")
        probsT_ready = sem("probsT_ready")
        att_sum = sem("att_sum")
        att_ready = sem("att_ready")
        pool_in = sem("pool_in")
        diff_sum = sem("diff_sum")
        diff_ready = sem("diff_ready")
        pool_sum = sem("pool_sum")
        pool_ready = sem("pool_ready")
        w_out_in = sem("w_out_in")
        mixT_sum = sem("mixT_sum")
        mixT_ready = sem("mixT_ready")
        y_sum = sem("y_sum")
        y_sq = sem("y_sq")
        y_used = sem("y_used")

        root_in = sem("root_in")
        root_out = sem("root_out")
        dve_step = sem("dve_step")
        act_step = sem("act_step")
        steps = {}

        def link(eng, ins, s):
            steps[id(s)] = steps.get(id(s), 0) + 1
            ins.then_inc(s, 1)
            eng.wait_ge(s, steps[id(s)])

        r = Region(arena, R0, AR - KD * INW)
        hT = r.take(KD * NT * P).rearrange("p (k t) -> p k t", k=KD)
        mix = r.take(NT * D).rearrange("p (i d) -> p i d", i=NT)
        R_ZR = r.at
        zr = r.take(NT * RIN).rearrange("p (i n) -> p i n", i=NT)
        R_RWKV = r.at
        za = r.take(NT * (INW - RIN)).rearrange("p (i n) -> p i n", i=NT)
        R1 = r.at
        htmp = r.take(D)
        hbuf = r.take(2 * D).rearrange("p (j d) -> p j d", j=2)
        bc = r.take(4 * D).rearrange("p (j d) -> p j d", j=4)
        R2 = r.at
        NY = 5
        ybuf = r.take(NY * D).rearrange("p (j d) -> p j d", j=NY)
        fbc = r.take(2 * D).rearrange("p (s d) -> p s d", s=2)
        w_in = Region(arena, AR - KD * INW, AR).take(KD * INW).rearrange("p (k n) -> p k n", k=KD)
        ZA = INW - RIN
        NA = 3
        ada_ring = Region(arena, R0, R1).take(NA * KD * 512).rearrange("p (j k n) -> p j k n", j=NA, k=KD)
        r = Region(arena, R0 + NA * KD * 512, R1)
        post_mix_row, pre_ffn_row, post_ffn_row = (r.take(D) for _ in range(3))
        r = Region(arena, R2, AR - KD * INW)
        modrow = r.take(6 * D)
        pre_mix_row = r.take(D)
        r = Region(arena, R2, AR - KD * INW)
        w_q = r.take(3 * H * QK).rearrange("p (k n) -> p k n", k=3)
        w_kv = r.take(2 * H * (NOPE + VH)).rearrange("p (k n) -> p k n", k=2)
        R3 = r.at
        r = Region(arena, R1, R2)
        zn = r.take(2 * (QL + KVL)).rearrange("p (j n) -> p j n", j=2)
        znT = r.take(2 * (QL + KVL)).rearrange("p (j k t) -> p j k t", j=2, k=5)
        qraw = r.take(2 * H * QK).rearrange("p (j h n) -> p j h n", j=2, h=H)
        kk_ = r.take(2 * H * QK).rearrange("p (j h n) -> p j h n", j=2, h=H)
        rtmp = r.take(2 * H * ROPE // 2).rearrange("p (j h n) -> p j h n", j=2, h=H)
        probs = r.take(2 * 512).rearrange("p (j t) -> p j t", j=2)
        mrow = r.take(2)
        rsum = r.take(NT * H).rearrange("p (i h) -> p i h", i=NT)
        rinv = r.take(NT * H).rearrange("p (i h) -> p i h", i=NT)
        NPAR = 10 * RW + RIN + 4 * RW
        r = Region(arena, R3, AR - NPAR)
        qT = r.take(H * NT * P).rearrange("p (h t) -> p h t", h=H)
        kT = r.take(H * NT * P).rearrange("p (h t) -> p h t", h=H)
        vv = r.take(NT * H * VH).rearrange("p (i n) -> p i n", i=NT)
        probsT = r.take(2 * 512).rearrange("p (j k t) -> p j k t", j=2, k=4)
        r = Region(arena, R0, R0 + KD * NT * P)
        poolm = r.take(2 * PG * SEQ).rearrange("p (k g t) -> p k g t", k=2, g=PG)
        pool_w = r.take(PG * PC).rearrange("p (g n) -> p g n", g=PG)
        pool_s = r.take(PW)
        diffT = r.take(2 * SEQ).rearrange("p (j t) -> p j t", j=2)

        r = Region(arena, R_RWKV, AR - NPAR)
        rb = {}
        NC = NT * 2
        hr = Region(arena, R0, R0 + KD * NT * P)
        rb["TT"] = hr.take(2 * NPAIR * NC * C).rearrange("p (d q c k) -> p d q c k", d=2, q=NPAIR, c=NC)
        rb["W"] = hr.take(2 * NPAIR * NC * C).rearrange("p (d q c k) -> p d q c k", d=2, q=NPAIR, c=NC)
        rb["Z"] = r.take(2 * NPAIR * NC * C).rearrange("p (d q c k) -> p d q c k", d=2, q=NPAIR, c=NC)
        rb["RQT"] = r.take(2 * NPAIR * NT * P).rearrange("p (d q t) -> p d q t", d=2, q=NPAIR)
        rb["AC"] = r.take(2 * NPAIR * NC).rearrange("p (d q c) -> p d q c", d=2, q=NPAIR)
        rb["YV"] = r.take(NT * RW).rearrange("p (i n) -> p i n", i=NT)
        rb["g"] = r.take(NT * RW).rearrange("p (i n) -> p i n", i=NT)
        rb["bonus"] = r.take(NT * RW).rearrange("p (i n) -> p i n", i=NT)
        rp = Region(arena, AR - NPAR, AR)
        rb["loraW"] = rp.take(4 * RW)
        rb["g2"] = rp.take(RW)
        rb["mu"] = rp.take(RIN)
        rb["wbias"] = rp.take(4 * RW)
        for nm in ("k_k", "k_a", "r_k", "ln_w", "ln_b"):
            rb[nm] = rp.take(RW)
        rb["zs2"] = r.take(2 * RIN).rearrange("p (j n) -> p j n", j=2)
        rb["lo"] = r.take(4 * LORA + GLORA)
        rb["loT"] = r.take(2 * P).rearrange("p (j t) -> p j t", j=2)
        rb["xwa"] = r.take(4 * RW).rearrange("p (a d n) -> p a d n", a=2, d=2)
        rb["kk"] = r.take(RW)
        rb["s1"] = r.take(2 * RW).rearrange("p (d n) -> p d n", d=2)
        rb["s2"] = r.take(2 * RW).rearrange("p (d n) -> p d n", d=2)
        R_DEAD = r.at
        rb["arr2"] = r.take(2 * 4 * 2 * RW).rearrange("p (j a d n) -> p j a d n", j=2, a=4, d=2)
        rb["arrT"] = r.take(4 * 2 * RW).rearrange("p (d q a t) -> p d q a t", d=2, q=NPAIR, a=4)
        rb["LG"] = r.take(2 * RH * 2 * P).rearrange("p (d h m t) -> p d h m t", d=2, h=RH, m=2)
        rb["MG"] = r.take(2 * RH * 2 * P).rearrange("p (d h m t) -> p d h m t", d=2, h=RH, m=2)
        rb["X"] = r.take(2 * RH * P).rearrange("p (d h t) -> p d h t", d=2, h=RH)
        rb["XT"] = r.take(2 * RH * P).rearrange("p (d h t) -> p d h t", d=2, h=RH)
        rb["T1"] = r.take(2 * RH * P).rearrange("p (d h t) -> p d h t", d=2, h=RH)
        rb["KMV"] = rb["X"].rearrange("p d h (m n) -> p d h m n", m=2)
        rb["tmp"] = r.take(2 * RW).rearrange("p (j n) -> p j n", j=2)
        rb["nX"] = r.take(2 * 2 * RW).rearrange("p (d m h n) -> p d m h n", d=2, m=2, h=RH)
        rb["st"] = r.take(32)
        r = Region(arena, R_DEAD, AR - NPAR)
        w_out = r.take(KD * D).rearrange("p (k n) -> p k n", k=KD)
        gbc = r.take(2 * D).rearrange("p (s d) -> p s d", s=2)
        R_OUT = r.at
        r = Region(arena, R_ZR, R_RWKV)
        mixT = r.take(2 * KD * P).rearrange("p (j k t) -> p j k t", j=2, k=KD)
        ytmp = r.take(D)

        rs = {n: sem("r_" + n) for n in (
            "in", "zero", "shift_sum", "zs_ready", "lo_ready", "loT_sum", "loT_ready", "lora_sum", "xwa_ready",
            "th_ready", "lw_ready", "cum_sum", "eL_ready", "Lx_ready", "eLx_ready", "arr_ready", "arrT_sum",
            "arrT_ready", "mats_sum", "mats_used", "mats_ready", "mv_sum", "kmv_ready", "t1_sum", "t1_ready", "x_sum",
            "x_ready", "nx_sum", "nx_ready", "fin_sum", "fin_ready", "chain_sum", "chain_ready", "inter_sum",
            "mix_ready")}
        ORDER = [list(range(2 * NL, NC)) + list(range(2 * NL)), list(range(NC - 1, 2 * NL - 1, -1)) + list(range(2 * NL - 1, -1, -1))]
        r = Region(arena, R0 + 2 * KD * NT * P, AR)
        acc = mix
        ring = r.take(4 * 6 * D).rearrange("p (j n) -> p j n", j=4)
        ring_gu = ring[:, :, 0:4 * D].rearrange("p j (m k n) -> p j m k n", m=2, k=KD)
        ring_dn = ring[:, :, 4 * D:6 * D].rearrange("p j (k n) -> p j k n", k=2)
        gT = r.take(2 * D).rearrange("p (j k t) -> p j k t", j=2, k=KD)
        yx = r.take(4 * D).rearrange("p (j d) -> p j d", j=4)
        sg = r.take(2 * FF).rearrange("p (j n) -> p j n", j=2)
        actx = r.take(2 * FF).rearrange("p (j n) -> p j n", j=2)
        aT = r.take(2 * 2 * P).rearrange("p (j k t) -> p j k t", j=2, k=2)
        R_WALK_TOP = r.at
        mask = r.take(NT * E).rearrange("p (i e) -> p i e", i=NT)
        gates = r.take(E)
        posm = r.take(NT * E).rearrange("p (i e) -> p i e", i=NT)
        mask_bf = r.take(NT * E // 2, BF16).rearrange("p (i e) -> p i e", i=NT)
        meta = r.take(NT * E * 4 // 2, BF16).rearrange("p (i e c) -> p i e c", i=NT, e=E)
        gi = r.take(E, U32)
        si = r.take(E, U32)
        idx_now = r.take(8, U32)
        cntf = r.take(1)
        cnti = r.take(1, I32)
        posb_bf = r.take(NT * E // 2, BF16).rearrange("p (i e) -> p i e", i=NT)
        mtmp = r.take(D)
        mh = r.take(2 * D).rearrange("p (j d) -> p j d", j=2)
        r2 = Region(arena, R_RWKV, R_DEAD)
        mbc = r2.take(4 * D).rearrange("p (j d) -> p j d", j=4)
        rw = r2.take(KD * E).rearrange("p (k e) -> p k e", k=KD)
        sh_gu = r2.take(4 * D).rearrange("p (m k n) -> p m k n", m=2, k=KD)
        sh_dn = r2.take(2 * D).rearrange("p (k n) -> p k n", k=2)
        rbias = r2.take(E)
        r2 = Region(arena, R_OUT, R_WALK_TOP)
        iota_e = r2.take(CAP * E // 2, BF16).rearrange("p (s e) -> p s e", e=E)
        sh_sg = r2.take(FF)
        sh_act = r2.take(FF)
        sh_aT = r2.take(2 * P).rearrange("p (k t) -> p k t", k=2)
        sc_ = r2.take(E)
        ex = r2.take(E)
        sel = r2.take(E)
        incl = r2.take(E)
        zero64 = r2.take(E)
        g8 = r2.take(NG * 8).rearrange("p (g n) -> p g n", g=NG)
        small8 = r2.take(64).rearrange("p (a n) -> p a n", n=8)
        idx8 = r2.take(8, U32)
        eq = r2.take(8 * E)
        r3 = Region(arena, R0 + 2 * KD * NT * P + 6 * D, R_OUT)
        tabf = r3.take(4 * E).rearrange("p (a e) -> p a e", a=4)
        posb = r3.take(NT * E).rearrange("p (i e) -> p i e", i=NT)
        onehot = r3.take(NT * E * CAP // 2, BF16).rearrange("p (i s e) -> p i s e", i=NT, e=E)
        gx = arena[:, R0:R0 + 4 * D].rearrange("p (j d) -> p j d", j=4)
        ms = {n: sem("m_" + n) for n in ("in", "h_out", "logit_sum", "shgu_sum", "ex_ready", "shg_ready", "act_ready", "aT_sum",
                                         "aT_ready", "dn_sum", "sh_ready", "mask_ready", "pos_sum", "count_ready", "iota_ready",
                                         "onehot_ready", "tab_sum", "y_used", "out_done")}
        f_in = [sem(f"f_in{s}") for s in range(2)]
        y_in = [sem(f"y_in{j}") for j in range(NY)]

        class Pass:

            def __init__(self, tag):
                self.gT_sum = sem(f"{tag}_gT_sum")
                self.gT_ready = sem(f"{tag}_gT_ready")
                self.gu_sum = sem(f"{tag}_gu_sum")
                self.sg_ready = sem(f"{tag}_sg_ready")
                self.act_ready = sem(f"{tag}_act_ready")
                self.aT_sum = sem(f"{tag}_aT_sum")
                self.aT_ready = sem(f"{tag}_aT_ready")
                self.dn_sum = sem(f"{tag}_dn_sum")
                self.y_ready = sem(f"{tag}_y_ready")
                self.gather_idx = sem(f"{tag}_gather_idx")
                self.scatter_idx = sem(f"{tag}_scatter_idx")
                self.w_in = [sem(f"{tag}_w_in{j}") for j in range(4)]
                self.g_in = [sem(f"{tag}_g_in{j}") for j in range(4)]
                self.y_out = [sem(f"{tag}_y_out{j}") for j in range(4)]

        main = Pass("main")
        x_chain = [sem(f"extra{l}_chain") for l in range(DEPTH)]
        x_in = [sem(f"extra{l}_in") for l in range(DEPTH)]
        x_rows = [sem(f"extra{l}_rows") for l in range(DEPTH)]
        x_out = [sem(f"extra{l}_out") for l in range(DEPTH)]
        x_step = [sem(f"extra{l}_step") for l in range(DEPTH)]
        X_TAB = 3
        (X_IDX, X_TURN, X_TURNED, X_GU, X_SILU, X_ACT, X_AT, X_ATC, X_DN, X_Y, X_SIDX, X_OUT) = range(1, 13)

        wait_held = sem("wait_held")

        def x_at(b, e, s=0):
            return (b - 1) * (X_TAB + E * X_OUT) + X_TAB + e * X_OUT + s

        def walk(eng, body):
            n = E // 4
            body(0, True, False)
            with eng.Fori(1, n - 1) as it:
                body(it, False, False)
            body(n - 1, False, True)

        block = ctx.enter_context(nc.Block())

        def tiles_of(l):
            return range(NT if l < DEPTH - 1 else NL)

        SCORE_BANK = (0, 1, 6)
        Y_BANK = (2, 6)

        def turned_before(l, i):
            return min(2 * i, i + len(tiles_of(l)))

        def z_part(c):
            return (c * ZA // 2, ZA // 2) if c < 2 else (ZA + (c - 2) * RIN // 2, RIN // 2)

        def blocks(l):
            return -(-len(tiles_of(l)) * P // ROWS[l])

        def head_rows(h):
            return (h % 2) * RD, (h % 2) * RD + RD

        @block.sync
        def _(sp):
            seen = Seen()
            sp.dma_start(craw[:, 0, :], A["c"].rearrange("a (p k) -> p (a k)", p=P)).then_inc(c_in, 16)
            sp.dma_start(craw[:, 1, :], A["c_ctx"].rearrange("(p k) -> p k", p=P)).then_inc(c_in, 16)

            def mod_inputs(l):
                sp.dma_start(modrow[0:2, :], A["ada_b"][l:l + 1, :].broadcast_to([2, 6 * D])).then_inc(ada_rows_in, 16)
                for nm, dst in (("pre_mix_g", pre_mix_row), ("post_mix_g", post_mix_row), ("pre_ffn_g", pre_ffn_row), ("post_ffn_g", post_ffn_row)):
                    sp.dma_start(dst[0:2, :], A[nm][l:l + 1, :].broadcast_to([2, D])).then_inc(ada_rows_in, 16)

            def mod_store(l):
                sp.wait_ge(mod_rows, l + 1)
                sp.dma_start(mod_dram[l], modrow[0:2, :]).then_inc(mod_out, 16)
                sp.wait_ge(mod_out, 16 * (l + 1))

            def load_w_in(l, c):
                w0, wn = z_part(c)
                sp.dma_start(w_in[:, :, w0:w0 + wn], A["w_in"][l].rearrange("(p k) n -> p k n", p=P)[:, :, w0:w0 + wn]).then_inc(w_in_in[c], 16)

            def row(l, s, j):
                return mod_dram[l][s:s + 1, j * D:(j + 1) * D].broadcast_to([P, D])

            def load_bc(l, s):
                sp.dma_start(bc[:, 2 * s, :], row(l, s, 1)).then_inc(bc_in[s], 16)
                sp.dma_start(bc[:, 2 * s + 1, :], row(l, s, 0)).then_inc(bc_in[s], 16)

            def load_mla(l):
                sp.dma_start(w_q, A["mla_w_q_b"][l].rearrange("(k p) n -> p k n", p=P)).then_inc(mla_in, 16)
                sp.dma_start(w_kv, A["mla_w_kv_b"][l].rearrange("(k p) n -> p k n", p=P)).then_inc(mla_in, 16)
                sp.dma_start(qcol, A["mla_q_norm"][l].rearrange("(k p) -> p k", p=P), allow_slow_non_contiguous=True).then_inc(mla_in, 16)
                sp.dma_start(kvcol, A["mla_kv_norm"][l].rearrange("(k p) -> p k", p=P), allow_slow_non_contiguous=True).then_inc(mla_in, 16)

            for n in range(12 * DEPTH):
                l, c = n // 12, n % 12
                if n >= NA:
                    sp.wait_ge(ada_sum, n + 1 - NA)
                sp.dma_start(ada_ring[:, n % NA], A["ada_w"][l].rearrange("(p k) n -> p k n", p=P)[:, :, c * 512:(c + 1) * 512]
                             ).then_inc(ada_in[n % NA], 16)
                if n == 0:
                    mod_inputs(0)
                if n == 3:
                    sp.dma_start(cst, A["shape_consts"]).then_inc(start_in, 16)
                    sp.dma_start(x[:, 0:NL, :], A["x"].rearrange("a (i p) d -> p (a i) d", p=P)).then_inc(start_in, 16)
                    sp.dma_start(x[:, NL:NT, :], A["ctx"].rearrange("a (i p) d -> p (a i) d", p=P)).then_inc(start_in, 16)
                if c == 3 and l > 0:
                    mod_store(l - 1)
                    mod_inputs(l)
                    if l == 1:
                        load_bc(0, 0)
                        load_bc(0, 1)
            for c in range(4):
                load_w_in(0, c)
            mod_store(DEPTH - 1)

            for l in range(DEPTH):
                load_mla(l)
                end_phase(sp, "sp")
                sp.dma_start(poolm, A["pool_matrix"].rearrange("p (k g t) -> p k g t", k=2, g=PG)).then_inc(pool_in, 16)
                sp.dma_start(pool_w[0:PC], A["pool_w"][l].rearrange("g c n -> c g n")).then_inc(pool_in, 16)
                sp.dma_start(pool_s, A["pool_scale"][l:l + 1, :].broadcast_to([P, PW])).then_inc(pool_in, 16)
                for nm, src, n in (("mu", A["rwkv_mu"][l:l + 1, :], RIN), ("k_k", A["rwkv_k_k"][l:l + 1, :], RW),
                                   ("k_a", A["rwkv_k_a"][l:l + 1, :], RW), ("r_k", A["rwkv_r_k"][l:l + 1].rearrange("a h n -> a (h n)"), RW),
                                   ("ln_w", A["rwkv_ln_w"][l:l + 1, :], RW), ("ln_b", A["rwkv_ln_b"][l:l + 1, :], RW)):
                    sp.dma_start(rb[nm], src.broadcast_to([P, n])).then_inc(rs["in"], 16)
                for a, nm in enumerate(("rwkv_w0", "rwkv_a0")):
                    sp.dma_start(rb["wbias"][:, a * 2 * RW:(a + 1) * 2 * RW], A[nm][l:l + 1].rearrange("a d n -> a (d n)").broadcast_to([P, 2 * RW])
                                 ).then_inc(rs["in"], 16)
                sp.dma_start(rb["g2"][0:GLORA], A["rwkv_g2"][l]).then_inc(rs["in"], 16)
                sp.wait_ge(rs["zero"], l + 1)
                for a, nm in enumerate(("rwkv_w2", "rwkv_a2")):
                    for d in range(2):
                        j = 2 * a + d
                        sp.dma_start(rb["loraW"][j * LORA:(j + 1) * LORA, j * RW:(j + 1) * RW], A[nm][l, d]).then_inc(rs["in"], 16)
                end_phase(sp, "sp")
                sp.wait_ge(rs["fin_ready"], NT * (l + 1))
                for k in range(4):
                    sp.dma_start(w_out[:, 2 * k:2 * k + 2, :], A["w_out"][l].rearrange("(k p) n -> p k n", p=P)[:, 2 * k:2 * k + 2, :]
                                 ).then_inc(w_out_in, 16)
                for s in range(2):
                    sp.dma_start(gbc[:, s, :], row(l, s, 2)).then_inc(w_out_in, 16)
                sp.wait_ge(rs["mix_ready"], l + 1)
                for s in range(2 if l < DEPTH - 1 else 1):
                    sp.dma_start(mbc[:, 2 * s, :], row(l, s, 4)).then_inc(ms["in"], 16)
                    sp.dma_start(mbc[:, 2 * s + 1, :], row(l, s, 3)).then_inc(ms["in"], 16)
                sp.dma_start(rw, A["router_w"][l].rearrange("(p k) e -> p k e", p=P)).then_inc(ms["in"], 16)
                sp.dma_start(rbias, A["router_bias"][l:l + 1, :].broadcast_to([P, E])).then_inc(ms["in"], 16)
                for m, nm in enumerate(("sh_w_gate", "sh_w_up")):
                    sp.dma_start(sh_gu[:, m], A[nm][l].rearrange("(p k) n -> p k n", p=P)).then_inc(ms["in"], 16)
                sp.dma_start(sh_dn, A["sh_w_down"][l].rearrange("(p k) n -> p k n", p=P)).then_inc(ms["in"], 16)
                for i in tiles_of(l):
                    sp.wait_ge(h_ready, NT * (l + 1) + sum(len(tiles_of(a)) for a in range(l)) + i + 1)
                    sp.dma_start(h_dram[i * P:(i + 1) * P, :], mh[:, i % 2, :]).then_inc(ms["h_out"], 16)
                    sp.wait_ge(ms["h_out"], seen(ms["h_out"], 16))
                end_phase(sp, "sp")

                def load_expert(S, e, j):
                    for m, nm in enumerate(("exp_w_gate", "exp_w_up")):
                        sp.dma_start(ring_gu[:, j, m], A[nm][l, bass.ds(e, 1)].rearrange("a (p k) n -> p (a k) n", p=P)).then_inc(S.w_in[j], 16)
                    sp.dma_start(ring_dn[:, j], A["exp_w_down"][l, bass.ds(e, 1)].rearrange("a (p k) n -> p (a k) n", p=P)).then_inc(S.w_in[j], 16)

                def load_walk(S, base):
                    def body(it, first, last):
                        for j in range(4):
                            e = it * 4 + j
                            if first and j == 0:
                                load_expert(S, 0, 0)
                                end_phase(sp, "sp")
                                sp.wait_ge(S.g_in[0], 16 * (base // 4 + 1))
                                continue
                            if not first:
                                sp.wait_ge(S.dn_sum, base + e - 3)
                            load_expert(S, e, j)
                    walk(sp, body)

                load_walk(main, E * l)
                end_phase(sp, "sp")
                sp.wait_ge(ms["count_ready"], l + 1)
                most = sp.value_load(cnti[0:1, 0:1], min_val=0, max_val=NT * P)
                with sp.If(most > ROWS[l]):
                    for b in range(1, blocks(l)):
                        with sp.Fori(0, E) as e:
                            sp.wait_ge(x_chain[l], x_at(b, e))
                            for m, nm in enumerate(("exp_w_gate", "exp_w_up")):
                                sp.dma_start(ring_gu[:, 0, m], A[nm][l, bass.ds(e, 1)].rearrange("a (p k) n -> p (a k) n", p=P)).then_inc(x_in[l], 16)
                            sp.dma_start(ring_dn[:, 0], A["exp_w_down"][l, bass.ds(e, 1)].rearrange("a (p k) n -> p (a k) n", p=P)).then_inc(x_in[l], 16)
                end_phase(sp, "sp")
                def load_stream(s):
                    sp.dma_start(fbc[:, s, :], row(l, s, 5)).then_inc(f_in[s], 16)
                    if l < DEPTH - 1:
                        load_bc(l + 1, s)

                before = sum(len(tiles_of(a)) for a in range(l))
                for n in range(TOPK * len(tiles_of(l))):
                    i, k, m = n // TOPK, n % TOPK, n + TOPK * before
                    if n >= NY:
                        sp.wait_ge(ms["y_used"], m + 1 - NY)
                    sp.dma_start(ybuf[:, m % NY], y_dram[i * P * TOPK:(i + 1) * P * TOPK, :].rearrange("(p k) d -> p k d", k=TOPK)[:, k, :]
                                 ).then_inc(y_in[m % NY], 16)
                    if n == NY - 1:
                        load_stream(0)
                    if n == TOPK - 1 and l < DEPTH - 1:
                        load_w_in(l + 1, 0)
                    if n == 2 * TOPK - 2 and l < DEPTH - 1:
                        load_w_in(l + 1, 1)
                    if n == 2 * TOPK - 1 and l < DEPTH - 1:
                        for c in range(2, 4):
                            load_w_in(l + 1, c)
                        load_stream(1)
                if l < DEPTH - 1:
                    sp.wait_ge(h_ready, NT * (l + 2) + before + len(tiles_of(l)))
                if l == DEPTH - 1:
                    end_phase(sp, "sp")
                    sp.dma_start(out[0].rearrange("(i p) d -> p i d", p=P), x[:, 0:NL, :]).then_inc(ms["out_done"], 16)
                    sp.wait_ge(ms["out_done"], 16)

        @block.tensor
        def _(pe):
            seen = Seen()
            mm = nc.tensor.matmul
            tr = nc.tensor.transpose
            pe.wait_ge(silu_c, 1)
            for n in range(12 * DEPTH):
                pe.wait_ge(ada_in[n % NA], 16 * (n // NA + 1))
                if n >= 8:
                    pe.wait_ge(ada_row, n - 7)
                for k in range(KD):
                    last = mm(pb[0:2, n % 8, :], cs[:, k, :], ada_ring[:, n % NA, k, :], start=(k == 0), stop=(k == KD - 1))
                last.then_inc(ada_sum, 1)
            pe.wait_ge(start_in, 48)
            pe.wait_ge(ada_row, 12 * DEPTH)

            def turn_tile(src, first_bank):
                for k in range(KD):
                    last = tr(pb[:, first_bank + k // 4, (k % 4) * P:(k % 4 + 1) * P], src[:, k * P:(k + 1) * P], ident)
                return last

            for l in range(DEPTH):
                turned = seen(hT_ready, 0)

                def h_turn(i):
                    pe.wait_ge(h_ready, seen(h_ready))
                    turn_tile(hbuf[:, i % 2, :], 2 * (i % 2)).then_inc(hT_sum, 1)

                h_turn(0)
                n = 0
                for i in range(NT):
                    pe.wait_ge(hT_ready, turned + i + 1)
                    for c in range(4):
                        if i == 0:
                            pe.wait_ge(w_in_in[c], 16 * (l + 1))
                        if n >= 4:
                            pe.wait_ge(z_ready, seen(z_ready))
                        w0, wn = z_part(c)
                        for k in range(KD):
                            last = mm(pb[:, 4 + n % 4, 0:wn], hT[:, k, i * P:(i + 1) * P], w_in[:, k, w0:w0 + wn],
                                      start=(k == 0), stop=(k == KD - 1))
                        last.then_inc(z_sum, 1)
                        n += 1
                        if c == 2 and i + 1 < NT:
                            h_turn(i + 1)
                seen(z_ready, 4)
                seen(hT_ready, NT)
                end_phase(pe, "pe")

                pe.wait_ge(mla_in, seen(mla_in, 64))
                turned, qk_copied = seen(znT_ready, 0), seen(qkT_ready, 0)

                def turn_latents(i):
                    pe.wait_ge(zn_ready, seen(zn_ready))
                    for k in range(5):
                        last = tr(pb[:, k // 4, (k % 4) * P:(k % 4 + 1) * P], zn[:, i % 2, k * P:(k + 1) * P], ident)
                    last.then_inc(znT_sum, 1)

                def project(i):
                    pe.wait_ge(znT_ready, turned + i + 1)
                    if i >= 1:
                        pe.wait_ge(qkv_raw, seen(qkv_raw))
                    for c in range(2 if i in tiles_of(l) else 0):
                        for k in range(3):
                            mm(pb[:, 2 + c, 0:384], znT[:, i % 2, k, :], w_q[:, k, c * 384:(c + 1) * 384], start=(k == 0), stop=(k == 2))
                    for c in range(2):
                        for k in range(2):
                            last = mm(pb[:, 4 + c, :], znT[:, i % 2, 3 + k, :], w_kv[:, k, c * 512:(c + 1) * 512], start=(k == 0), stop=(k == 1))
                    last.then_inc(qkv_sum, 1)

                turn_latents(0)
                project(0)
                turn_latents(1)
                for i in range(NT):
                    if i + 1 < NT:
                        project(i + 1)
                    pe.wait_ge(qk_ready, seen(qk_ready))
                    for m, src in enumerate((qraw, kk_) if i in tiles_of(l) else (kk_,)):
                        if i >= 1 or m == 1:
                            pe.wait_ge(qkT_ready, qk_copied + turned_before(l, i) + m)
                        for h in range(H):
                            last = tr(pb[0:QK, 6 + h // 4, (h % 4) * P:(h % 4 + 1) * P], src[:, i % 2, h, :], ident)
                        last.then_inc(qkT_sum, 1)
                        if m == 0 and i + 2 < NT:
                            turn_latents(i + 2)
                seen(znT_ready, NT)
                seen(qkT_ready, turned_before(l, NT) - 1)
                pe.wait_ge(qkT_ready, seen(qkT_ready))
                seen(qkv_raw)

                units = [(i, h) for i in tiles_of(l) for h in range(H)]
                keys = lambda i: (0, NT) if i < NL else (NL, NT)
                exped, copied = seen(probs_ready, 0), seen(probsT_ready, 0)

                def score(u):
                    i, h = units[u]
                    a, b = keys(i)
                    mm(pb[:, SCORE_BANK[u % 3], 0:(b - a) * P], qT[0:QK, h, i * P:(i + 1) * P], kT[0:QK, h, a * P:b * P],
                       start=True, stop=True).then_inc(score_sum, 1)

                def attend(u):
                    i, h = units[u]
                    a, b = keys(i)
                    pe.wait_ge(probsT_ready, copied + u + 1)
                    if h == 0 and i >= 2:
                        pe.wait_ge(att_ready, seen(att_ready))
                    for k in range(a, b):
                        last = mm(pb[:, 4 + i % 2, h * VH:(h + 1) * VH], probsT[:, u % 2, k - a, :], vv[:, k, h * VH:(h + 1) * VH],
                                  start=(k == a), stop=(k == b - 1))
                    last.then_inc(att_sum, 1)

                score(0)
                score(1)
                for u, (i, h) in enumerate(units):
                    a, b = keys(i)
                    pe.wait_ge(probs_ready, exped + u + 1)
                    for k in range(b - a):
                        last = tr(pb[:, 2 + u % 2, k * P:(k + 1) * P], probs[:, u % 2, k * P:(k + 1) * P], ident)
                    last.then_inc(probsT_sum, 1)
                    if u + 2 < len(units):
                        score(u + 2)
                    if u >= 1:
                        attend(u - 1)
                attend(len(units) - 1)
                seen(probs_ready, len(units))
                seen(probsT_ready, len(units))
                pe.wait_ge(att_ready, seen(att_ready, 2))
                end_phase(pe, "pe")

                pe.wait_ge(pool_in, seen(pool_in, 48))
                groups = [(s, g) for s in range(len(tiles_of(l)) // 2) for g in range(PG)]

                def pooled():
                    def times_weights(u):
                        s, g = groups[u]
                        pe.wait_ge(diff_ready, seen(diff_ready))
                        for t in range(2):
                            last = mm(pb[:, 2 + 2 * s + t, g * PC:(g + 1) * PC], diffT[0:PC, u % 2, t * P:(t + 1) * P], pool_w[0:PC, g, :],
                                      start=True, stop=True)
                        last.then_inc(pool_sum, 1)

                    for u, (s, g) in enumerate(groups):
                        for k in range(2):
                            last = mm(pb[0:PC, u % 2, 0:SEQ], za[:, 2 * s + k, MLA_IN + g * PC:MLA_IN + (g + 1) * PC], poolm[:, k, g, :],
                                      start=(k == 0), stop=(k == 1))
                        last.then_inc(diff_sum, 1)
                        if u >= 1:
                            times_weights(u - 1)
                        if u == len(groups) - 1:
                            times_weights(u)
                        yield

                R = rs
                pe.wait_ge(R["in"], seen(R["in"], 16 * 13))

                def front(i):
                    s = i // 2
                    for c in range(2):
                        for k in range(2):
                            last = mm(pb[:, 6 + c, 0:RIN // 2], shift[:, k, (i % 2) * P:(i % 2 + 1) * P],
                                      zr[:, 2 * s + k, c * RIN // 2:(c + 1) * RIN // 2], start=(k == 0), stop=(k == 1))
                    last.then_inc(R["shift_sum"], 1)
                    yield
                    pe.wait_ge(R["lo_ready"], seen(R["lo_ready"]))
                    tr(pb[:, 6, 0:P], rb["lo"][:, 0:P], ident)
                    tr(pb[0:GLORA, 6, P:2 * P], rb["lo"][:, P:P + GLORA], ident).then_inc(R["loT_sum"], 1)
                    yield
                    pe.wait_ge(R["loT_ready"], seen(R["loT_ready"]))
                    for c in range(2):
                        last = mm(pb[:, 6 + c, :], rb["loT"][:, 0, :], rb["loraW"][:, c * 512:(c + 1) * 512], start=True, stop=True)
                    last.then_inc(R["lora_sum"], 1)
                    yield
                    pe.wait_ge(R["lw_ready"], seen(R["lw_ready"]))
                    for d in range(2):
                        mm(pb[:, 6, d * RW:(d + 1) * RW], cum[:, d, :], rb["xwa"][:, 0, d, :], start=True, stop=True)
                    if i in tiles_of(l):
                        mm(pb[:, 7, 8:8 + RW], rb["loT"][0:GLORA, 1, :], rb["g2"][0:GLORA], start=True, stop=True)
                    for d in range(2):
                        for q in range(NPAIR):
                            last = mm(pb[:, 7, (2 * d + q) * 2:(2 * d + q) * 2 + 2], rb["xwa"][:, 0, d, q * P:(q + 1) * P], c_("chunk_of"),
                                      start=True, stop=True)
                    last.then_inc(R["cum_sum"], 1)
                    yield
                    for d in range(2):
                        if d == 0:
                            pe.wait_ge(R["arr_ready"], seen(R["arr_ready"]))
                        else:
                            pe.wait_ge(R["arrT_ready"], NT * 2 * l + 2 * i + 1)
                        for q in range(NPAIR):
                            for a in range(4):
                                last = tr(pb[:, 6 + q, a * P:(a + 1) * P], rb["arr2"][:, i % 2, a, d, q * P:(q + 1) * P], ident)
                        last.then_inc(R["arrT_sum"], 1)
                        yield

                ahead = front(0)
                pooling = pooled()
                for stage in range(5):
                    next(ahead)
                    if stage < 4:
                        for _ in range(2):
                            next(pooling, None)
                for _ in pooling:
                    pass
                pe.wait_ge(pool_ready, seen(pool_ready, len(groups) // PG))
                turned = seen(R["arrT_ready"], 0)
                for i in range(NT):
                    arr = rb["arr2"][:, i % 2]
                    zs = rb["zs2"][:, i % 2]
                    mine = ahead
                    v_ = lambda h: zs[:, 2 * RW + h * RD:2 * RW + (h + 1) * RD]
                    ahead = front(i + 1) if i + 1 < NT else iter(())
                    used, ready = seen(R["mats_used"], 0), seen(R["mats_ready"], 0)
                    for d in range(2):
                        pe.wait_ge(R["arrT_ready"], turned + 2 * i + d + 1)
                        if d == 0 and i >= 1:
                            pe.wait_ge(R["fin_ready"], seen(R["fin_ready"]))
                        for r in range(2):
                            if d == 1:
                                pe.wait_ge(R["mats_used"], used + r + 1)
                            for q in range(NPAIR):
                                T = rb["arrT"][r * RD:(r + 1) * RD, d, q]
                                mm(pb[:, 4 + r, q * P:(q + 1) * P], T[:, 0, :], T[:, 2, :], start=True, stop=True)
                                kr = T[:, 0:2, :].rearrange("p a t -> p (a t)")
                                mm(pb[:, r, q * 256:(q + 1) * 256], T[:, 2, :], kr, start=True, stop=True)
                                last = mm(pb[:, 2 + r, q * 256:(q + 1) * 256], T[:, 3, :], kr, start=True, stop=True)
                            last.then_inc(R["mats_sum"], 1)
                        if d == 0:
                            next(mine)
                    for lv in range(1, 6):
                        for d in range(2):
                            if lv > 1:
                                pe.wait_ge(R["x_ready"], seen(R["x_ready"]))
                            else:
                                pe.wait_ge(R["mats_ready"], ready + 2 * (d + 1))
                                pe.wait_ge(R["mats_used"], used + 3 + d)
                            for h in range(RH):
                                last = mm(pb[:, 4 + d, h * P:(h + 1) * P], rb["LG"][:, d, h, 0, :], rb["X"][:, d, h, :], start=True, stop=True)
                            last.then_inc(R["t1_sum"], 1)
                        if lv in (1, 3, 5):
                            next(ahead, None)
                        if lv == 5:
                            for d in range(2):
                                for h in range(RH):
                                    last = mm(pb[:, d, h * RD:(h + 1) * RD], rb["MG"][:, d, h, 0, :], v_(h), start=True, stop=True)
                                last.then_inc(R["mv_sum"], 1)
                        for d in range(2):
                            pe.wait_ge(R["t1_ready"], seen(R["t1_ready"]))
                            for h in range(RH):
                                if lv < 5:
                                    mm(pb[:, d, h * P:(h + 1) * P], rb["XT"][:, d, h, :], rb["T1"][:, d, h, :], start=True, stop=True)
                                last = mm(pb[:, 2 + d, h * P:(h + 1) * P], rb["T1"][:, d, h, :], rb["XT"][:, d, h, :], start=True, stop=True)
                            last.then_inc(R["x_sum"], 1)
                        if lv == 2:
                            next(ahead, None)
                    seen(R["mats_used"], 4)
                    seen(R["mats_ready"], 4)
                    for d in range(2):
                        pe.wait_ge(R["x_ready"], seen(R["x_ready"]))
                        pe.wait_ge(R["kmv_ready"], seen(R["kmv_ready"]))
                        for h in range(RH):
                            last = mm(pb[:, 4 + d, h * P:(h + 1) * P], rb["XT"][:, d, h, :], rb["KMV"][:, d, h].rearrange("p m n -> p (m n)"),
                                      start=True, stop=True)
                        last.then_inc(R["nx_sum"], 1)
                    pe.wait_ge(R["nx_ready"], seen(R["nx_ready"], 2))
                    for h in range(RH if i in tiles_of(l) else 0):
                        for d in range(2):
                            mm(pb[:, 0, h * RD:(h + 1) * RD], rb["MG"][:, d, h, 1, :], v_(h), start=(d == 0), stop=False)
                            mm(pb[:, 0, h * RD:(h + 1) * RD], rb["LG"][:, d, h, 1, :], rb["nX"][:, d, 1, h, :], start=False, stop=(d == 1))
                    for d in range(2):
                        for h in range(RH):
                            a, b = head_rows(h)
                            dq = 2 * d + h // 2
                            if i in tiles_of(l):
                                mm(pb[a:b, 1, dq * P:(dq + 1) * P], rb["nX"][:, d, 0, h, :], rb["LG"][:, d, h, 1, :], start=True, stop=True)
                            for c in range(2):
                                ca, cb = c * C, (c + 1) * C
                                o = dq * C
                                beta = arr[ca:cb, 2, d, h * RD:(h + 1) * RD]
                                khat = arr[ca:cb, 3, d, h * RD:(h + 1) * RD]
                                mm(pb[a:b, 2 + 2 * c, o:o + C], rb["nX"][ca:cb, d, 0, h, :], beta, start=True, stop=True)
                                mm(pb[a:b, 3 + 2 * c, o:o + C], khat, zs[ca:cb, 2 * RW + h * RD:2 * RW + (h + 1) * RD], start=True, stop=False)
                                last = mm(pb[a:b, 3 + 2 * c, o:o + C], beta, rb["nX"][ca:cb, d, 1, h, :], start=False, stop=True)
                    last.then_inc(R["fin_sum"], 1)
                    next(ahead, None)
                pe.wait_ge(R["fin_ready"], seen(R["fin_ready"]))
                seen(R["arrT_ready"], 2 * NT)
                for n in range(1, NC - 1):
                    for d in range(2):
                        pe.wait_ge(R["chain_ready"], seen(R["chain_ready"]))
                        cp = ORDER[d][n]
                        for h in range(RH):
                            a, b = head_rows(h)
                            last = mm(pb[a:b, d, (h // 2) * RD:(h // 2 + 1) * RD], rb["TT"][a:b, d, h // 2, cp, :], rb["Z"][a:b, d, h // 2, cp, :],
                                      start=True, stop=True)
                        last.then_inc(R["chain_sum"], 1)
                pe.wait_ge(R["chain_ready"], seen(R["chain_ready"], 2))
                for i in tiles_of(l):
                    for h in range(RH):
                        a, b = head_rows(h)
                        for j in range(2):
                            c = 2 * i + j
                            ds = [d for d in range(2) if c != ORDER[d][0]]
                            for d in ds:
                                last = mm(pb[j * C:(j + 1) * C, 4 + h % 2, i * P + (h // 2) * RD:i * P + (h // 2 + 1) * RD], rb["RQT"][a:b, d, h // 2, c * C:(c + 1) * C],
                                          rb["Z"][a:b, d, h // 2, c, :], start=(d == ds[0]), stop=(d == ds[-1]))
                last.then_inc(R["inter_sum"], 1)
                pe.wait_ge(w_out_in, seen(w_out_in, 96))
                copied, used = seen(mixT_ready, 0), seen(y_used, 0)
                nt = len(tiles_of(l))

                def turn_mix(i, ks, bank):
                    for n, k in enumerate(ks):
                        last = tr(pb[:, bank + n // 4, (n % 4) * P:(n % 4 + 1) * P], mix[:, i, k * P:(k + 1) * P], ident)
                    last.then_inc(mixT_sum, 1)

                def out_product(i, c, ks):
                    for k in ks:
                        last = mm(pb[:, Y_BANK[i % 2] + c, :], mixT[:, i % 2, k, :], w_out[:, k, c * 512:(c + 1) * 512],
                                  start=(k == 0), stop=(k == KD - 1))
                    return last

                EARLY, LATE = range(6), range(6, KD)
                turn_mix(0, EARLY, 0)
                for i0 in range(0, nt, 2):
                    pe.wait_ge(mixT_ready, copied + 2 * i0 + 1)
                    if i0 > 0:
                        pe.wait_ge(y_used, used + i0 - 1)
                    out_product(i0, 0, EARLY)
                    turn_mix(i0 + 1, EARLY, 0)
                    out_product(i0, 1, EARLY)
                    pe.wait_ge(mixT_ready, copied + 2 * i0 + 2)
                    if i0 > 0:
                        pe.wait_ge(y_used, used + i0)
                    for c in range(2):
                        out_product(i0 + 1, c, EARLY)
                    if i0 == 0:
                        pe.wait_ge(R["mix_ready"], seen(R["mix_ready"]))
                    for j in range(2):
                        turn_mix(i0 + j, LATE, 4 + j)
                    if i0 + 2 < nt:
                        turn_mix(i0 + 2, EARLY, 0)
                    for j in range(2):
                        pe.wait_ge(mixT_ready, copied + 2 * i0 + 3 + j)
                        for c in range(2):
                            last = out_product(i0 + j, c, LATE)
                        last.then_inc(y_sum, 1)
                seen(mixT_ready, 2 * nt)
                pe.wait_ge(ms["in"], seen(ms["in"], 16 * (5 + 2 * (len(tiles_of(l)) // 2))))
                turned = seen(hT_ready, 0)
                nt = len(tiles_of(l))

                def h_turn(i):
                    pe.wait_ge(h_ready, seen(h_ready))
                    turn_tile(mh[:, i % 2, :], 2 * (i % 2)).then_inc(hT_sum, 1)

                h_turn(0)
                for i in range(nt):
                    pe.wait_ge(hT_ready, turned + i + 1)
                    own = slice(i * P, (i + 1) * P)
                    for k in range(KD):
                        last = mm(pb[:, 4, 0:E], hT[:, k, own], rw[:, k, :], start=(k == 0), stop=(k == KD - 1))
                    last.then_inc(ms["logit_sum"], 1)
                    for k in range(KD):
                        last = mm(pb[:, 5, :], hT[:, k, own], sh_gu[:, :, k, :], start=(k == 0), stop=(k == KD - 1))
                    last.then_inc(ms["shgu_sum"], 1)
                    if i == 0:
                        pe.wait_ge(y_used, seen(y_used, nt))
                    if i + 1 < nt:
                        h_turn(i + 1)
                    pe.wait_ge(ms["act_ready"], seen(ms["act_ready"]))
                    for k in range(2):
                        last = tr(pb[:, 4, k * P:(k + 1) * P], sh_act[:, k * P:(k + 1) * P], ident)
                    last.then_inc(ms["aT_sum"], 1)
                    pe.wait_ge(ms["aT_ready"], seen(ms["aT_ready"]))
                    if i >= 1:
                        pe.wait_ge(ms["sh_ready"], seen(ms["sh_ready"]))
                    for c in range(2):
                        for k in range(2):
                            last = mm(pb[:, 6 + c, :], sh_aT[:, k, :], sh_dn[:, k, c * 512:(c + 1) * 512], start=(k == 0), stop=(k == 1))
                    last.then_inc(ms["dn_sum"], 1)
                seen(hT_ready, nt)
                pe.wait_ge(ms["sh_ready"], seen(ms["sh_ready"]))
                pe.wait_ge(ms["mask_ready"], seen(ms["mask_ready"], nt))
                for i in range(nt):
                    for j in range(i + 1):
                        mm(pb[:, 0, i * E:(i + 1) * E], before_bf if j == i else ones_bf, mask_bf[:, j, :], start=(j == 0), stop=(j == i))
                for j in range(nt):
                    last = mm(pb[:, 0, nt * E:(nt + 1) * E], ones_bf, mask_bf[:, j, :], start=(j == 0), stop=(j == nt - 1))
                last.then_inc(ms["pos_sum"], 1)
                end_phase(pe, "pe")

                def tables(done):
                    for e in range(E):
                        for i in range(nt):
                            last = mm(pb[:, 0, 4 * e:4 * e + 4], onehot[:, i, :, e], meta[:, i, e, :], start=(i == 0), stop=(i == nt - 1))
                    last.then_inc(done, 1)

                pe.wait_ge(ms["onehot_ready"], seen(ms["onehot_ready"]))
                tables(ms["tab_sum"])
                end_phase(pe, "pe")

                def ffn_walk(S, base):
                    def turn(m, j):
                        pe.wait_ge(S.g_in[j], m)
                        turn_tile(gx[:, j, :], 0).then_inc(S.gT_sum, 1)

                    def down(n, j, waits):
                        pe.wait_ge(S.aT_ready, n + 1)
                        if waits:
                            pe.wait_ge(S.y_ready, n)
                        for c in range(2):
                            for k in range(2):
                                last = mm(pb[:, 5 + c, :], aT[:, j % 2, k, :], ring_dn[:, j % 4, k, c * 512:(c + 1) * 512], start=(k == 0), stop=(k == 1))
                        last.then_inc(S.dn_sum, 1)

                    def gathered(it, j):
                        return 16 * (base // 4 + it + 1)

                    def body(it, first, last_):
                        for j in range(4):
                            n = it * 4 + j + base
                            if first and j == 0:
                                turn(gathered(0, 0), 0)
                            pe.wait_ge(S.w_in[j], 48 * (it + 1 + base // 4))
                            pe.wait_ge(S.gT_ready, n + 1)
                            if not (first and j < 2):
                                pe.wait_ge(S.act_ready, n - 1)
                            for k in range(KD):
                                last = mm(pb[:, 2 + j % 2, :], gT[:, j % 2, k, :], ring_gu[:, j, :, k, :], start=(k == 0), stop=(k == KD - 1))
                            last.then_inc(S.gu_sum, 1)
                            if not (last_ and j == 3):
                                turn(gathered(it, j + 1) if j < 3 else gathered(it + 1, 0), (j + 1) % 4)
                            if not (first and j == 0):
                                down(n - 1, j - 1, not (first and j == 1))
                            pe.wait_ge(S.act_ready, n + 1)
                            if not (first and j == 0):
                                pe.wait_ge(S.aT_ready, n)
                            for k in range(2):
                                last = tr(pb[:, 4, k * P:(k + 1) * P], actx[:, j % 2, k * P:(k + 1) * P], ident)
                            last.then_inc(S.aT_sum, 1)
                    walk(pe, body)
                    down(base + E - 1, 3, True)

                ffn_walk(main, E * l)
                end_phase(pe, "pe")
                pe.wait_ge(ms["count_ready"], l + 1)
                most = pe.value_load(cnti[0:1, 0:1], min_val=0, max_val=NT * P)
                with pe.If(most > ROWS[l]):
                    for b in range(1, blocks(l)):
                        pe.wait_ge(x_chain[l], x_at(b, 0) - 2)
                        tables(x_chain[l])
                        with pe.Fori(0, E) as e:
                            pe.wait_ge(x_in[l], 48 * ((b - 1) * E + e + 1))
                            pe.wait_ge(x_rows[l], 16 * ((b - 1) * E + e + 1))
                            turn_tile(gx[:, 0, :], 0).then_inc(x_chain[l], 1)
                            pe.wait_ge(x_chain[l], x_at(b, e, X_TURNED))
                            for k in range(KD):
                                last = mm(pb[:, 2, :], gT[:, 0, k, :], ring_gu[:, 0, :, k, :], start=(k == 0), stop=(k == KD - 1))
                            last.then_inc(x_chain[l], 1)
                            pe.wait_ge(x_chain[l], x_at(b, e, X_ACT))
                            for k in range(2):
                                last = tr(pb[:, 4, k * P:(k + 1) * P], actx[:, 0, k * P:(k + 1) * P], ident)
                            last.then_inc(x_chain[l], 1)
                            pe.wait_ge(x_chain[l], x_at(b, e, X_ATC))
                            for c in range(2):
                                for k in range(2):
                                    last = mm(pb[:, 5 + c, :], aT[:, 0, k, :], ring_dn[:, 0, k, c * 512:(c + 1) * 512], start=(k == 0), stop=(k == 1))
                            last.then_inc(x_chain[l], 1)
                end_phase(pe, "pe")
                if l == DEPTH - 1:
                    end_phase(pe, "pe")

        @block.scalar
        def _(act):
            seen = Seen()
            ac = nc.scalar.activation
            act.wait_ge(c_in, 32)
            ac(cs.rearrange("p k s -> p s k"), craw, ACT.Silu).then_inc(silu_c, 1)
            for l in range(DEPTH):
                def turned(i):
                    act.wait_ge(hT_sum, seen(hT_sum))
                    ac(hT[:, :, i * P:(i + 1) * P], pb[:, 2 * (i % 2):2 * (i % 2) + 2, :].rearrange("p b (k t) -> p (b k) t", k=4), ACT.Copy
                       ).then_inc(hT_ready, 1)

                turned(0)
                if l == 0:
                    act.wait_ge(mod_rows, DEPTH)
                for i in range(NT):
                    for c in range(4):
                        act.wait_ge(z_sum, seen(z_sum))
                        wn = ZA // 2 if c < 2 else RIN // 2
                        dst = za[:, i, c * wn:(c + 1) * wn] if c < 2 else zr[:, i, (c - 2) * wn:(c - 1) * wn]
                        ac(dst, pb[:, 4 + (4 * i + c) % 4, 0:wn], ACT.Copy).then_inc(z_ready, 1)
                        if c == 2 and i + 1 < NT:
                            turned(i + 1)
                end_phase(act, "act")
                act.wait_ge(mla_in, seen(mla_in, 64))
                def turned_latents(i):
                    act.wait_ge(znT_sum, seen(znT_sum))
                    for k in range(5):
                        col = qcol[:, k:k + 1] if k < 3 else kvcol[:, k - 3:k - 2]
                        last = ac(znT[:, i % 2, k, :], pb[:, k // 4, (k % 4) * P:(k % 4 + 1) * P], ACT.Copy, scale=col)
                    last.then_inc(znT_ready, 1)

                def projected(i):
                    act.wait_ge(qkv_sum, seen(qkv_sum))
                    if i >= 2:
                        act.wait_ge(qkT_sum, qk_turned + turned_before(l, i - 1))
                    for c in range(2):
                        if i in tiles_of(l):
                            ac(qraw[:, i % 2, 4 * c:4 * c + 4, :], pb[:, 2 + c, 0:384].rearrange("p (h n) -> p h n", h=4), ACT.Copy)
                        kv = pb[:, 4 + c, :].rearrange("p (h n) -> p h n", h=4)
                        ac(kk_[:, i % 2, 4 * c:4 * c + 4, 0:NOPE], kv[:, :, 0:NOPE], ACT.Copy)
                        last = ac(vv[:, i, 4 * c * VH:4 * (c + 1) * VH].rearrange("p (h n) -> p h n", h=4), kv[:, :, NOPE:NOPE + VH], ACT.Copy)
                    last.then_inc(qkv_raw, 1)

                qk_turned = seen(qkT_sum, 0)
                turned_latents(0)
                projected(0)
                turned_latents(1)
                for i in range(NT):
                    if i + 1 < NT:
                        projected(i + 1)
                    for m, dst in enumerate((qT, kT) if i in tiles_of(l) else (kT,)):
                        act.wait_ge(qkT_sum, qk_turned + turned_before(l, i) + m + 1)
                        ac(dst[0:QK, :, i * P:(i + 1) * P], pb[0:QK, 6:8, :].rearrange("p b (h t) -> p (b h) t", h=4), ACT.Copy
                           ).then_inc(qkT_ready, 1)
                        if m == 0 and i + 2 < NT:
                            turned_latents(i + 2)
                seen(qkT_sum, turned_before(l, NT))
                units = [(i, h) for i in tiles_of(l) for h in range(H)]
                for u, (i, h) in enumerate(units):
                    nk = (NT if i < NL else NT - NL) * P
                    act.wait_ge(max_ready, seen(max_ready))
                    if u >= 2:
                        act.wait_ge(probsT_sum, seen(probsT_sum))
                    ac(probs[:, u % 2, 0:nk], pb[:, SCORE_BANK[u % 3], 0:nk], ACT.Exp, bias=mrow[:, u % 2:u % 2 + 1], scale=MLA_SCALE,
                       accum_out=rsum[:, i, h:h + 1]).then_inc(probs_ready, 1)
                seen(probsT_sum, 2)
                end_phase(act, "act")
                def differences():
                    for u in range(len(tiles_of(l)) // 2 * PG):
                        act.wait_ge(diff_sum, seen(diff_sum))
                        if u >= 2:
                            act.wait_ge(pool_sum, seen(pool_sum))
                        ac(diffT[0:PC, u % 2, :], pb[0:PC, u % 2, 0:SEQ], ACT.Copy).then_inc(diff_ready, 1)
                        yield

                pooling = differences()
                R = rs
                for i in range(NT):
                    zs, arr = rb["zs2"][:, i % 2], rb["arr2"][:, i % 2]
                    if i == 0:
                        next(pooling)
                    act.wait_ge(R["zs_ready"], seen(R["zs_ready"]))
                    if i >= 1:
                        act.wait_ge(R["loT_sum"], NT * l + i)
                    ac(rb["lo"][:, 0:2 * LORA], zs[:, 3 * RW:3 * RW + 2 * LORA], ACT.Tanh)
                    ac(rb["lo"][:, 2 * LORA:4 * LORA], zs[:, 3 * RW + 2 * LORA:3 * RW + 4 * LORA], ACT.Copy)
                    link(act, ac(rb["lo"][:, 4 * LORA:], zs[:, 3 * RW + 4 * LORA:RIN], ACT.Tanh, scale=0.5), act_step)
                    ac(rb["lo"][:, 4 * LORA:], rb["lo"][:, 4 * LORA:], ACT.Copy, scale=0.5, bias=0.5).then_inc(R["lo_ready"], 1)
                    if i == 0:
                        next(pooling)
                    act.wait_ge(R["loT_sum"], seen(R["loT_sum"]))
                    ac(rb["loT"][:, 0, :], pb[:, 6, 0:P], ACT.Copy)
                    ac(rb["loT"][0:GLORA, 1, :], pb[0:GLORA, 6, P:2 * P], ACT.Copy).then_inc(R["loT_ready"], 1)
                    if i == 0:
                        for _ in range(2):
                            next(pooling)
                    act.wait_ge(R["xwa_ready"], seen(R["xwa_ready"]))
                    ac(rb["xwa"], rb["xwa"], ACT.Tanh, scale=0.5).then_inc(R["th_ready"], 1)
                    if i == 0:
                        for _ in range(2):
                            next(pooling, None)
                    act.wait_ge(R["cum_sum"], seen(R["cum_sum"]))
                    ac(arr[:, 1].rearrange("p d n -> p (d n)"), pb[:, 6, :], ACT.Exp)
                    ac(rb["s1"].rearrange("p d n -> p (d n)"), pb[:, 6, :], ACT.Exp, scale=-1.0)
                    ac(rb["AC"].rearrange("p d q c -> p (d q) c")[:, :, 2 * i:2 * i + 2], pb[:, 7, 0:8].rearrange("p (a c) -> p a c", c=2), ACT.Exp
                       ).then_inc(R["eL_ready"], 1)
                    act.wait_ge(R["Lx_ready"], seen(R["Lx_ready"]))
                    ac(arr[:, 0], rb["s2"], ACT.Exp).then_inc(R["eLx_ready"], 1)
                    if i == 0:
                        for _ in pooling:
                            pass
                        seen(pool_sum, 2)
                    for d in range(2):
                        act.wait_ge(R["arrT_sum"], seen(R["arrT_sum"]))
                        for q in range(NPAIR):
                            last = ac(rb["arrT"][:, d, q].rearrange("p a t -> p (a t)"), pb[:, 6 + q, :], ACT.Copy)
                            if i in tiles_of(l):
                                last = ac(rb["RQT"][:, d, q, i * P:(i + 1) * P], pb[:, 6 + q, P:2 * P], ACT.Copy)
                        last.then_inc(R["arrT_ready"], 1)
                def turned_mix(i, n, k, bank):
                    act.wait_ge(mixT_sum, seen(mixT_sum))
                    ac(mixT[:, i % 2, k:k + n, :].rearrange("p k t -> p (k t)"), pb[:, bank:bank + 2, :].rearrange("p b n -> p (b n)")[:, 0:n * P], ACT.Copy
                       ).then_inc(mixT_ready, 1)

                def squares(i):
                    act.wait_ge(y_sum, seen(y_sum))
                    if i >= 1:
                        act.wait_ge(y_used, seen(y_used))
                    ac(ytmp, pb[:, Y_BANK[i % 2]:Y_BANK[i % 2] + 2, :].rearrange("p b n -> p (b n)"), ACT.Square,
                       accum_out=ssq[:, i:i + 1]).then_inc(y_sq, 1)

                nt = len(tiles_of(l))
                turned_mix(0, 6, 0, 0)
                for i0 in range(0, nt, 2):
                    turned_mix(i0 + 1, 6, 0, 0)
                    for j in range(2):
                        turned_mix(i0 + j, 2, 6, 4 + j)
                    if i0 + 2 < nt:
                        turned_mix(i0 + 2, 6, 0, 0)
                    for j in range(2):
                        squares(i0 + j)
                seen(y_used, 1)
                def turned(i):
                    act.wait_ge(hT_sum, seen(hT_sum))
                    ac(hT[:, :, i * P:(i + 1) * P], pb[:, 2 * (i % 2):2 * (i % 2) + 2, :].rearrange("p b (k t) -> p (b k) t", k=4), ACT.Copy
                       ).then_inc(hT_ready, 1)

                turned(0)
                ac(iota_e, c_("iota")[:, 0:CAP].rearrange("p (s a) -> p s a", a=1).broadcast_to([P, CAP, E]), ACT.Copy).then_inc(ms["iota_ready"], 1)
                for i in tiles_of(l):
                    act.wait_ge(ms["logit_sum"], seen(ms["logit_sum"]))
                    if i >= 1:
                        act.wait_ge(ms["mask_ready"], seen(ms["mask_ready"]))
                    ac(ex, pb[:, 4, 0:E], ACT.Exp, scale=-1.0).then_inc(ms["ex_ready"], 1)
                    act.wait_ge(ms["shgu_sum"], seen(ms["shgu_sum"]))
                    ac(sh_sg, pb[:, 5, 0:FF], ACT.Silu).then_inc(ms["shg_ready"], 1)
                    if i + 1 < len(tiles_of(l)):
                        turned(i + 1)
                    act.wait_ge(ms["aT_sum"], seen(ms["aT_sum"]))
                    ac(sh_aT.rearrange("p k t -> p (k t)"), pb[:, 4, 0:2 * P], ACT.Copy).then_inc(ms["aT_ready"], 1)
                    act.wait_ge(ms["dn_sum"], seen(ms["dn_sum"]))
                    ac(acc[:, i, :], pb[:, 6:8, :].rearrange("p b n -> p (b n)"), ACT.Copy).then_inc(ms["sh_ready"], 1)
                seen(ms["mask_ready"])
                end_phase(act, "act")
                end_phase(act, "act")

                def act_walk(S, base):
                    def turned(n, j):
                        act.wait_ge(S.gT_sum, n + 1)
                        ac(gT[:, j % 2].rearrange("p k t -> p (k t)"), pb[:, 0:2, :].rearrange("p b n -> p (b n)"), ACT.Copy).then_inc(S.gT_ready, 1)

                    def body(it, first, last_):
                        for j in range(4):
                            n = it * 4 + j + base
                            if first and j == 0:
                                turned(n, 0)
                            act.wait_ge(S.gu_sum, n + 1)
                            if not (first and j < 2):
                                act.wait_ge(S.act_ready, n - 1)
                            ac(sg[:, j % 2], pb[:, 2 + j % 2, 0:FF], ACT.Silu).then_inc(S.sg_ready, 1)
                            if not (last_ and j == 3):
                                turned(n + 1, j + 1)
                    walk(act, body)

                act_walk(main, E * l)
                end_phase(act, "act")
                act.wait_ge(ms["count_ready"], l + 1)
                most = act.value_load(cnti[0:1, 0:1], min_val=0, max_val=NT * P)
                with act.If(most > ROWS[l]):
                    for b in range(1, blocks(l)):
                        with act.Fori(0, E) as e:
                            act.wait_ge(x_chain[l], x_at(b, e, X_TURN))
                            ac(gT[:, 0].rearrange("p k t -> p (k t)"), pb[:, 0:2, :].rearrange("p b n -> p (b n)"), ACT.Copy).then_inc(x_chain[l], 1)
                            act.wait_ge(x_chain[l], x_at(b, e, X_GU))
                            ac(sg[:, 0], pb[:, 2, 0:FF], ACT.Silu).then_inc(x_chain[l], 1)
                end_phase(act, "act")
                if l == DEPTH - 1:
                    end_phase(act, "act")

        @block.vector
        def _(dve):
            seen, sent = Seen(), Seen()
            V = nc.vector

            def step(ins):
                link(dve, ins, dve_step)

            def power(last):
                last.then_inc(root_in, 1)
                dve.wait_ge(root_out, seen(root_out))

            def inv_root(src, n, eps):
                dst = root[:, 0:src.shape[1]]
                power(V.tensor_scalar(dst, src, 1.0 / n, eps, ALU.mult, ALU.add))
                return dst

            def norm_tile(i, gain, shift_row, dst, tmp):
                step(V.tensor_tensor_reduce(tmp, x[:, i, :], x[:, i, :], 1.0, 0.0, ALU.mult, ALU.add, ssq[:, i:i + 1]))
                rstd = inv_root(ssq[:, i:i + 1], D, EPS)
                step(V.scalar_tensor_tensor(tmp, x[:, i, :], rstd, gain, ALU.mult, ALU.mult))
                return V.tensor_tensor(dst.rearrange("p (k q) -> p q k", k=KD), tmp.rearrange("p (q k) -> p q k", k=KD),
                                       shift_row.rearrange("p (q k) -> p q k", k=KD), ALU.add)

            def residual(i, y, gain, tmp):
                rstd = inv_root(ssq[:, i:i + 1], D, EPS)
                step(V.scalar_tensor_tensor(tmp, y, rstd, gain, ALU.mult, ALU.mult))
                return V.tensor_tensor(x[:, i, :], x[:, i, :], tmp, ALU.add)

            V.memset(minus_half, -0.5)
            step(V.memset(root, 1.0))
            dve.wait_ge(start_in, 48)
            V.tensor_copy(ones_bf, c_("ones"))
            V.tensor_copy(before_bf, c_("before"))
            def first_norm(i):
                s = i // NL
                norm_tile(i, bc[:, 2 * s, :], bc[:, 2 * s + 1, :], hbuf[:, i % 2, :], htmp).then_inc(h_ready, 1)
                dve.wait_ge(h_ready, sent(h_ready))

            for l in range(DEPTH):
                dve.wait_ge(ada_rows_in, 80 * (l + 1))
                for c in range(12):
                    dve.wait_ge(ada_sum, 12 * l + c + 1)
                    part = modrow[0:2, c * 512:(c + 1) * 512]
                    last = V.tensor_tensor(part, pb[0:2, (12 * l + c) % 8, :], part, ALU.add)
                    last.then_inc(ada_row, 1)
                dve.wait_ge(ada_row, 12 * (l + 1))
                def mr(j):
                    return modrow[0:2, j * D:(j + 1) * D]
                V.scalar_tensor_tensor(mr(1), mr(1), 1.0, pre_mix_row[0:2, :], ALU.add, ALU.mult)
                V.tensor_tensor(mr(2), mr(2), post_mix_row[0:2, :], ALU.mult)
                V.scalar_tensor_tensor(mr(4), mr(4), 1.0, pre_ffn_row[0:2, :], ALU.add, ALU.mult)
                V.tensor_tensor(mr(5), mr(5), post_ffn_row[0:2, :], ALU.mult).then_inc(mod_rows, 1)
                dve.wait_ge(mod_rows, sent(mod_rows))
                if l == 0:
                    for s in range(2):
                        dve.wait_ge(bc_in[s], seen(bc_in[s], 32))
                    for i in range(2):
                        first_norm(i)

            def combine(l, i):
                for k in range(TOPK):
                    n = TOPK * (i + sum(len(tiles_of(a)) for a in range(l))) + k
                    dve.wait_ge(y_in[n % NY], 16 * (n // NY + 1))
                    V.scalar_tensor_tensor(acc[:, i, :], ybuf[:, n % NY, :], gk[:, i, k:k + 1], acc[:, i, :], ALU.mult, ALU.add).then_inc(ms["y_used"], 1)
                    dve.wait_ge(ms["y_used"], sent(ms["y_used"]))
                step(V.tensor_tensor_reduce(htmp, acc[:, i, :], acc[:, i, :], 1.0, 0.0, ALU.mult, ALU.add, ssq[:, i:i + 1]))
                step(residual(i, acc[:, i, :], fbc[:, i // NL, :], htmp))

            for l in range(DEPTH):
                for i in range(NT):
                    if l > 0:
                        if i % NL == 0:
                            s = i // NL
                            dve.wait_ge(f_in[s], seen(f_in[s], 16))
                            dve.wait_ge(bc_in[s], seen(bc_in[s], 32))
                        combine(l - 1, i)
                    if i >= 2:
                        dve.wait_ge(hT_sum, seen(hT_sum))
                    if l > 0 or i >= 2:
                        first_norm(i)
                seen(hT_sum, 2)
                end_phase(dve, "dve")
                def rope(pe_, co, si, t):
                    n = ROPE // 2
                    V.tensor_tensor(t[:, 0], pe_[:, :, 0:n], si, ALU.mult)
                    step(V.tensor_tensor(t[:, 1], pe_[:, :, n:2 * n], si, ALU.mult))
                    V.tensor_tensor(pe_[:, :, 0:n], pe_[:, :, 0:n], co, ALU.mult)
                    step(V.tensor_tensor(pe_[:, :, n:2 * n], pe_[:, :, n:2 * n], co, ALU.mult))
                    V.tensor_tensor(pe_[:, :, 0:n], pe_[:, :, 0:n], t[:, 1], ALU.subtract)
                    return V.tensor_tensor(pe_[:, :, n:2 * n], pe_[:, :, n:2 * n], t[:, 0], ALU.add)

                def mla_norm(i):
                    zt, zz = za[:, i, :], zn[:, i % 2, :]
                    if i >= 2:
                        dve.wait_ge(znT_sum, NT * l + i - 1)
                    V.tensor_tensor_reduce(zz[:, 0:QL], zt[:, 0:QL], zt[:, 0:QL], 1.0, 0.0, ALU.mult, ALU.add, ssq[:, 0:1])
                    step(V.tensor_tensor_reduce(zz[:, QL:QL + KVL], zt[:, QL:QL + KVL], zt[:, QL:QL + KVL], 1.0, 0.0, ALU.mult, ALU.add, ssq[:, 1:2]))
                    V.tensor_scalar(root[:, 0:1], ssq[:, 0:1], 1.0 / QL, EPS, ALU.mult, ALU.add)
                    power(V.tensor_scalar(root[:, 1:2], ssq[:, 1:2], 1.0 / KVL, EPS, ALU.mult, ALU.add))
                    V.tensor_scalar(zz[:, 0:QL], zt[:, 0:QL], root[:, 0:1], None, ALU.mult)
                    V.tensor_scalar(zz[:, QL:QL + KVL], zt[:, QL:QL + KVL], root[:, 1:2], None, ALU.mult).then_inc(zn_ready, 1)
                    dve.wait_ge(zn_ready, sent(zn_ready))

                def mla_rotate(i):
                    zt = za[:, i, :]
                    k_pe = zt[:, QL + KVL:MLA_IN].rearrange("p (a n) -> p a n", a=1)
                    if i < NL:
                        step(rope(k_pe, cos[:, i:i + 1, :], sin[:, i:i + 1, :], rtmp[:, :, 0:1, :]))
                    dve.wait_ge(qkv_raw, seen(qkv_raw))
                    last = V.tensor_copy(kk_[:, i % 2, :, NOPE:QK], k_pe.broadcast_to([P, H, ROPE]))
                    if i < NL:
                        last = rope(qraw[:, i % 2, :, NOPE:QK], cos[:, i:i + 1, :].broadcast_to([P, H, ROPE // 2]),
                                    sin[:, i:i + 1, :].broadcast_to([P, H, ROPE // 2]), rtmp)
                    last.then_inc(qk_ready, 1)
                    dve.wait_ge(qk_ready, sent(qk_ready))

                mla_norm(0)
                mla_norm(1)
                for i in range(NT):
                    if i + 2 < NT:
                        mla_norm(i + 2)
                    mla_rotate(i)
                units = [(i, h) for i in tiles_of(l) for h in range(H)]

                attended = seen(att_sum, 0)

                def maximum(u):
                    i, h = units[u]
                    nk = (NT if i < NL else NT - NL) * P
                    dve.wait_ge(score_sum, seen(score_sum))
                    if u >= 2:
                        dve.wait_ge(probs_ready, seen(probs_ready))
                    step(V.tensor_reduce(mrow[:, u % 2:u % 2 + 1], pb[:, SCORE_BANK[u % 3], 0:nk], AX.X, ALU.max))
                    V.tensor_scalar(mrow[:, u % 2:u % 2 + 1], mrow[:, u % 2:u % 2 + 1], -MLA_SCALE, None, ALU.mult).then_inc(max_ready, 1)
                    dve.wait_ge(max_ready, sent(max_ready))

                def copy_probs(u):
                    i, h = units[u]
                    nk = (NT if i < NL else NT - NL) * P
                    dve.wait_ge(probsT_sum, seen(probsT_sum))
                    if u >= 2:
                        dve.wait_ge(att_sum, attended + u - 1)
                    V.tensor_copy(probsT[:, u % 2].rearrange("p k t -> p (k t)")[:, 0:nk], pb[:, 2 + u % 2, 0:nk]).then_inc(probsT_ready, 1)
                    dve.wait_ge(probsT_ready, sent(probsT_ready))

                def scale_out(i):
                    dve.wait_ge(att_sum, attended + (i + 1) * H)
                    step(V.reciprocal(rinv[:, i, :], rsum[:, i, :]))
                    V.tensor_tensor(mix[:, i, 0:H * VH].rearrange("p (h n) -> p h n", h=H), pb[:, 4 + i % 2, :].rearrange("p (h n) -> p h n", h=H),
                                    rinv[:, i, :].rearrange("p (h a) -> p h a", a=1).broadcast_to([P, H, VH]), ALU.mult).then_inc(att_ready, 1)
                    dve.wait_ge(att_ready, sent(att_ready))

                maximum(0)
                maximum(1)
                for u, (i, h) in enumerate(units):
                    copy_probs(u)
                    if u + 2 < len(units):
                        maximum(u + 2)
                    if h == 2 and i >= 1:
                        scale_out(i - 1)
                scale_out(i)
                seen(att_sum, len(units))
                seen(probs_ready, 2)
                end_phase(dve, "dve")
                def pool_out(s):
                    dve.wait_ge(pool_sum, seen(pool_sum, PG))
                    for t in range(2):
                        last = V.tensor_tensor(mix[:, 2 * s + t, H * VH:H * VH + PW], pb[:, 2 + 2 * s + t, 0:PW], pool_s, ALU.mult)
                    last.then_inc(pool_ready, 1)

                dve.wait_ge(pool_in, seen(pool_in, 48))
                R = rs
                dve.wait_ge(R["in"], seen(R["in"], 16 * 13))
                heads = lambda ap: ap.rearrange("p (h n) -> p h n", h=RH)
                over_heads = lambda ap: ap.rearrange("p (h a) -> p h a", a=1).broadcast_to([P, RH, RD])
                over_dirs = lambda ap: ap.rearrange("p (a n) -> p a n", a=1).broadcast_to([P, 2, RW])
                xwa, st, kk, tmp = rb["xwa"], rb["st"], rb["kk"], rb["tmp"]

                def front(i):
                    zs, arr = rb["zs2"][:, i % 2], rb["arr2"][:, i % 2]
                    r_, k_, v_ = zs[:, 0:RW], zs[:, RW:2 * RW], zs[:, 2 * RW:3 * RW]
                    dve.wait_ge(R["shift_sum"], seen(R["shift_sum"]))
                    part = RIN // 2
                    V.tensor_tensor(zs[:, 0:part], pb[:, 6, 0:part], rb["mu"][:, 0:part], ALU.mult)
                    step(V.tensor_tensor(zs[:, part:RIN], pb[:, 7, 0:part], rb["mu"][:, part:RIN], ALU.mult))
                    V.tensor_tensor(zs, zs, zr[:, i, :], ALU.add).then_inc(R["zs_ready"], 1)
                    dve.wait_ge(R["zs_ready"], sent(R["zs_ready"]))
                    yield
                    step(V.tensor_tensor(kk, k_, rb["k_k"], ALU.mult))
                    step(V.tensor_tensor(tmp[:, 0], kk, kk, ALU.mult))
                    step(V.tensor_reduce(st[:, 0:RH], heads(tmp[:, 0]), AX.X, ALU.add))
                    V.tensor_scalar(root[:, 0:RH], st[:, 0:RH], 1e-24, None, ALU.max).then_inc(root_in, 1)
                    yield
                    dve.wait_ge(root_out, seen(root_out))
                    V.tensor_tensor(heads(kk), heads(kk), over_heads(root[:, 0:RH]), ALU.mult)
                    step(V.tensor_tensor(tmp[:, 0], r_, rb["r_k"], ALU.mult))
                    dve.wait_ge(R["lora_sum"], seen(R["lora_sum"]))
                    V.tensor_tensor(xwa.rearrange("p a d n -> p (a d n)"), pb[:, 6:8, :].rearrange("p b n -> p (b n)"), rb["wbias"], ALU.add
                                    ).then_inc(R["xwa_ready"], 1)
                    yield
                    dve.wait_ge(R["th_ready"], seen(R["th_ready"]))
                    V.tensor_scalar(xwa[:, 0], xwa[:, 0], 1.0, 0.5 * DECAY, ALU.add, ALU.mult).then_inc(R["lw_ready"], 1)
                    dve.wait_ge(R["lw_ready"], sent(R["lw_ready"]))
                    step(V.tensor_scalar(xwa[:, 1], xwa[:, 1], 1.0, 0.5, ALU.add, ALU.mult))
                    V.tensor_tensor(arr[:, 2], xwa[:, 1], over_dirs(kk), ALU.mult)
                    yield
                    step(V.scalar_tensor_tensor(arr[:, 3], xwa[:, 1], -1.0, over_dirs(rb["k_a"]), ALU.add, ALU.mult))
                    step(V.scalar_tensor_tensor(arr[:, 3], arr[:, 3], 1.0, over_dirs(k_), ALU.add, ALU.mult))
                    if i in tiles_of(l):
                        step(V.tensor_tensor(tmp[:, 1], arr[:, 3, 0, :], arr[:, 3, 1, :], ALU.add))
                        step(V.tensor_tensor(tmp[:, 0], tmp[:, 0], tmp[:, 1], ALU.mult))
                        step(V.tensor_reduce(st[:, RH:2 * RH], heads(tmp[:, 0]), AX.X, ALU.add))
                        V.tensor_tensor(heads(rb["bonus"][:, i, :]), heads(v_), over_heads(st[:, RH:2 * RH]), ALU.mult)
                    dve.wait_ge(R["cum_sum"], seen(R["cum_sum"]))
                    dve.wait_ge(R["eL_ready"], seen(R["eL_ready"]))
                    V.tensor_tensor(rb["s2"], pb[:, 6, :].rearrange("p (d n) -> p d n", d=2), xwa[:, 0], ALU.subtract).then_inc(R["Lx_ready"], 1)
                    if i in tiles_of(l):
                        V.tensor_copy(rb["g"][:, i, :], pb[:, 7, 8:8 + RW])
                    V.tensor_tensor(arr[:, 1], arr[:, 1], over_dirs(r_), ALU.mult)
                    V.tensor_tensor(arr[:, 2], arr[:, 2], rb["s1"], ALU.mult)
                    V.tensor_tensor(arr[:, 3], arr[:, 3], rb["s1"], ALU.mult)
                    dve.wait_ge(R["eLx_ready"], seen(R["eLx_ready"]))
                    V.tensor_tensor(arr[:, 0], arr[:, 0], over_dirs(kk), ALU.mult).then_inc(R["arr_ready"], 1)
                    dve.wait_ge(R["arr_ready"], sent(R["arr_ready"]))

                for _ in front(0):
                    pass
                for s in range(len(tiles_of(l)) // 2):
                    pool_out(s)
                for i in range(NT):
                    arr = rb["arr2"][:, i % 2]
                    ahead = front(i + 1) if i + 1 < NT else iter(())
                    for d in range(2):
                        lv0 = lambda dd: levels[:, dd, 0:1, :].broadcast_to([P, NPAIR, P])
                        m2 = masks[:, d].rearrange("p m t -> p (m t)").rearrange("p (a n) -> p a n", a=1).broadcast_to([P, NPAIR, 2 * P])
                        eye = ident.rearrange("p (a t) -> p a t", a=1).broadcast_to([P, NPAIR, P])
                        for r in range(2):
                            dve.wait_ge(R["mats_sum"], seen(R["mats_sum"]))
                            mine = lambda nm: rb[nm][:, d].rearrange("p (q r) t -> p r q t", r=2)[:, r]
                            mine2 = lambda nm: rb[nm][:, d].rearrange("p (q r) m t -> p r q (m t)", r=2)[:, r]
                            lg = pb[:, r, :].rearrange("p (q n) -> p q n", q=2)
                            mg = pb[:, 2 + r, :].rearrange("p (q n) -> p q n", q=2)
                            V.tensor_tensor(mine("X"), pb[:, 4 + r, 0:2 * P].rearrange("p (q t) -> p q t", q=2), lv0(d), ALU.mult)
                            V.tensor_tensor(mine("XT"), lg[:, :, 0:P], lv0(1 - d), ALU.mult)
                            V.tensor_tensor(mine2("LG"), lg, m2, ALU.mult)
                            V.tensor_tensor(mine2("MG"), mg, m2, ALU.mult).then_inc(R["mats_used"], 1)
                            dve.wait_ge(R["mats_used"], sent(R["mats_used"]))
                            V.tensor_tensor(mine("X"), mine("X"), eye, ALU.add)
                            V.tensor_tensor(mine("XT"), mine("XT"), eye, ALU.add).then_inc(R["mats_ready"], 1)
                            dve.wait_ge(R["mats_ready"], sent(R["mats_ready"]))
                    for lv in range(1, 6):
                        for d in range(2):
                            dve.wait_ge(R["t1_sum"], seen(R["t1_sum"]))
                            V.tensor_tensor(rb["T1"][:, d], pb[:, 4 + d, :].rearrange("p (h t) -> p h t", h=RH),
                                            levels[:, d, lv:lv + 1, :].broadcast_to([P, RH, P]), ALU.mult).then_inc(R["t1_ready"], 1)
                        if lv == 5:
                            for d in range(2):
                                dve.wait_ge(R["mv_sum"], seen(R["mv_sum"]))
                                V.tensor_copy(rb["KMV"][:, d, :, 0, :], heads(arr[:, 0, d, :]))
                                V.tensor_copy(rb["KMV"][:, d, :, 1, :], heads(pb[:, d, 0:RW])).then_inc(R["kmv_ready"], 1)
                        for d in range(2):
                            dve.wait_ge(R["x_sum"], seen(R["x_sum"]))
                            if lv < 5:
                                V.tensor_tensor(rb["X"][:, d], pb[:, d, :].rearrange("p (h t) -> p h t", h=RH), rb["X"][:, d], ALU.add)
                            V.tensor_tensor(rb["XT"][:, d], pb[:, 2 + d, :].rearrange("p (h t) -> p h t", h=RH), rb["XT"][:, d], ALU.add
                                            ).then_inc(R["x_ready"], 1)
                        dve.wait_ge(R["x_ready"], sent(R["x_ready"], 2))
                        if lv < 5:
                            next(ahead, None)
                    for d in range(2):
                        dve.wait_ge(R["nx_sum"], seen(R["nx_sum"]))
                        V.tensor_scalar(rb["nX"][:, d].rearrange("p m h n -> p h m n"), pb[:, 4 + d, :].rearrange("p (h m n) -> p h m n", h=RH, m=2),
                                        -1.0, None, ALU.mult).then_inc(R["nx_ready"], 1)
                    next(ahead, None)
                    dve.wait_ge(R["fin_sum"], seen(R["fin_sum"]))
                    if i in tiles_of(l):
                        V.tensor_copy(rb["YV"][:, i, :], pb[:, 0, 0:RW])
                        rq = rb["RQT"].rearrange("p d q t -> p (d q) t")[:, :, i * P:(i + 1) * P]
                        V.tensor_tensor(rq, pb[:, 1, :].rearrange("p (a t) -> p a t", a=4), rq, ALU.add)
                    eye2 = c_("eye2").rearrange("p (a k) -> p a k", a=1)
                    for c in range(2):
                        cc = 2 * i + c
                        V.tensor_tensor(rb["TT"].rearrange("p d q c k -> p (d q) c k")[:, :, cc, :], pb[:, 2 + 2 * c, 0:4 * C].rearrange("p (a k) -> p a k", a=4),
                                        eye2.broadcast_to([P, 4, C]), ALU.add)
                        last = V.tensor_tensor(rb["W"].rearrange("p d q c k -> p (d q) c k")[:, :, cc, :], pb[:, 3 + 2 * c, 0:4 * C].rearrange("p (a k) -> p a k", a=4),
                                               rb["AC"].rearrange("p d q c -> p (d q) c")[:, :, cc:cc + 1].broadcast_to([P, 4, C]), ALU.mult)
                    last.then_inc(R["fin_ready"], 1)
                    dve.wait_ge(R["fin_ready"], sent(R["fin_ready"]))
                for d in range(2):
                    c0, c1 = ORDER[d][0], ORDER[d][1]
                    V.tensor_copy(rb["Z"][:, d, :, c1, :], rb["W"][:, d, :, c0, :]).then_inc(R["chain_ready"], 1)
                    dve.wait_ge(R["chain_ready"], sent(R["chain_ready"]))
                for n in range(1, NC - 1):
                    for d in range(2):
                        dve.wait_ge(R["chain_sum"], seen(R["chain_sum"]))
                        cp, cn = ORDER[d][n], ORDER[d][n + 1]
                        for q in range(NPAIR):
                            last = V.scalar_tensor_tensor(rb["Z"][:, d, q, cn, :], pb[:, d, q * RD:(q + 1) * RD], rb["AC"][:, d, q, cp:cp + 1],
                                                          rb["W"][:, d, q, cp, :], ALU.mult, ALU.add)
                        last.then_inc(R["chain_ready"], 1)
                        dve.wait_ge(R["chain_ready"], sent(R["chain_ready"]))
                nt = len(tiles_of(l))
                nh = nt * RH
                Y = rb["zs2"].rearrange("p j n -> p (j n)")[:, 0:nt * RW]
                SQ = rb["xwa"].rearrange("p a d n -> p (a d n)")[:, 0:nt * RW]
                st = rb["st"]
                heads = lambda ap: ap.rearrange("p (h n) -> p h n", n=RD)
                over_heads = lambda ap: ap.rearrange("p (h a) -> p h a", a=1).broadcast_to([P, nh, RD])
                tiles = lambda ap: ap.rearrange("p (i n) -> p i n", n=RW)
                over_tiles = lambda ap: ap.rearrange("p (a n) -> p a n", a=1).broadcast_to([P, nt, RW])
                flat = lambda nm: rb[nm].rearrange("p i n -> p (i n)")[:, 0:nt * RW]
                dve.wait_ge(R["inter_sum"], seen(R["inter_sum"]))
                for r in range(2):
                    by_pair = lambda ap: ap.rearrange("p (u r n) -> p r u n", r=2, n=RD)[:, r]
                    last = V.tensor_tensor(by_pair(Y), pb[:, 4 + r, 0:nt * P].rearrange("p (u n) -> p u n", n=RD), by_pair(flat("YV")), ALU.add)
                step(last)
                step(V.tensor_reduce(st[:, 0:nh], heads(Y), AX.X, ALU.add))
                step(V.tensor_scalar(st[:, 0:nh], st[:, 0:nh], -1.0 / RD, None, ALU.mult))
                step(V.tensor_tensor(heads(Y), heads(Y), over_heads(st[:, 0:nh]), ALU.add))
                step(V.tensor_tensor(SQ, Y, Y, ALU.mult))
                step(V.tensor_reduce(st[:, 16:16 + nh], heads(SQ), AX.X, ALU.add))
                step(V.tensor_tensor(heads(Y), heads(Y), over_heads(inv_root(st[:, 16:16 + nh], RD, GN_EPS)), ALU.mult))
                step(V.tensor_tensor(tiles(Y), tiles(Y), over_tiles(rb["ln_w"]), ALU.mult))
                step(V.tensor_tensor(tiles(Y), tiles(Y), over_tiles(rb["ln_b"]), ALU.add))
                step(V.tensor_tensor(Y, Y, flat("bonus"), ALU.add))
                V.tensor_tensor(mix[:, 0:nt, H * VH + PW:D], tiles(Y), tiles(flat("g")), ALU.mult).then_inc(R["mix_ready"], 1)
                nt = len(tiles_of(l))
                iota = c_("iota")
                def ffn_norm(i):
                    if i >= 2:
                        dve.wait_ge(ms["h_out"], 16 * (sum(len(tiles_of(a)) for a in range(l)) + i - 1))
                        dve.wait_ge(hT_sum, seen(hT_sum))
                    s = i // NL
                    norm_tile(i, mbc[:, 2 * s, :], mbc[:, 2 * s + 1, :], mh[:, i % 2, :], mtmp).then_inc(h_ready, 1)
                    dve.wait_ge(h_ready, sent(h_ready))

                dve.wait_ge(w_out_in, seen(w_out_in, 96))
                for i in range(nt):
                    dve.wait_ge(y_sq, seen(y_sq))
                    residual(i, pb[:, Y_BANK[i % 2]:Y_BANK[i % 2] + 2, :].rearrange("p b n -> p (b n)"), gbc[:, i // NL, :], ytmp).then_inc(y_used, 1)
                    dve.wait_ge(y_used, sent(y_used))
                    if i == 0:
                        dve.wait_ge(ms["in"], seen(ms["in"], 16 * (5 + 2 * (nt // 2))))
                        step(V.memset(zero64, 0.0))
                    if i == 1 and nt > 2:
                        ffn_norm(0)
                    if i == 1 or nt == 2:
                        ffn_norm(i)
                for i in range(nt):
                    if 2 <= i + 1 < nt:
                        ffn_norm(i + 1)
                    dve.wait_ge(ms["shg_ready"], seen(ms["shg_ready"]))
                    V.tensor_tensor(sh_act.rearrange("p (k q) -> p q k", k=2), sh_sg.rearrange("p (q k) -> p q k", k=2),
                                    pb[:, 5, FF:2 * FF].rearrange("p (q k) -> p q k", k=2), ALU.mult).then_inc(ms["act_ready"], 1)
                    dve.wait_ge(ms["act_ready"], sent(ms["act_ready"]))
                    dve.wait_ge(ms["ex_ready"], seen(ms["ex_ready"]))
                    step(V.tensor_scalar(sc_, ex, 1.0, None, ALU.add))
                    step(V.reciprocal(sc_, sc_))
                    step(V.tensor_tensor(sel, sc_, rbias, ALU.add))
                    for g in range(NG):
                        last = V.max(g8[:, g, :], sel[:, g * EG:(g + 1) * EG])
                    step(last)
                    step(V.tensor_tensor(small8[:, 0, :], g8[:, :, 0], g8[:, :, 1], ALU.add))
                    step(V.max(small8[:, 1, :], small8[:, 0, :]))
                    step(V.max_index(idx8, small8[:, 1, :], small8[:, 0, :]))
                    step(V.tensor_copy(small8[:, 2, :], idx8))

                    def chosen(dst, n, count):
                        q = eq[:, 0:n * count].rearrange("p (n k) -> p n k", n=n)
                        step(V.tensor_tensor(q, iota[:, 0:n].rearrange("p (n a) -> p n a", a=1).broadcast_to([P, n, count]),
                                             small8[:, 2:3, 0:count].broadcast_to([P, n, count]), ALU.is_equal))
                        step(V.tensor_reduce(dst, q, AX.X, ALU.add))

                    chosen(small8[:, 3, :], NG, TG)
                    step(V.tensor_scalar(small8[:, 3, :], small8[:, 3, :], -1.0, 1e30, ALU.add, ALU.mult))
                    step(V.tensor_tensor(sel.rearrange("p (g n) -> p g n", g=NG), sel.rearrange("p (g n) -> p g n", g=NG),
                                         small8[:, 3, :].rearrange("p (g a) -> p g a", a=1).broadcast_to([P, NG, EG]), ALU.add))
                    step(V.max(small8[:, 1, :], sel))
                    step(V.max_index(idx8, small8[:, 1, :], sel))
                    step(V.tensor_copy(small8[:, 2, :], idx8))
                    chosen(mask[:, i, :], E, TOPK)
                    step(V.tensor_tensor(gates, sc_, mask[:, i, :], ALU.mult))
                    step(V.tensor_reduce(small8[:, 4, 0:1], gates, AX.X, ALU.add))
                    step(V.reciprocal(small8[:, 4, 0:1], small8[:, 4, 0:1]))
                    step(V.tensor_scalar(gates, gates, small8[:, 4, 0:1], ROUTED, ALU.mult, ALU.mult))
                    step(V.tensor_tensor_scan(incl, mask[:, i, :], zero64, 0.0, ALU.add, ALU.add))
                    step(V.tensor_tensor(incl, incl, mask[:, i, :], ALU.mult))
                    q = eq[:, 0:TOPK * E].rearrange("p (k n) -> p k n", k=TOPK)
                    step(V.tensor_tensor(q, incl.rearrange("p (a n) -> p a n", a=1).broadcast_to([P, TOPK, E]),
                                         iota[:, 1:TOPK + 1].rearrange("p (k a) -> p k a", a=1).broadcast_to([P, TOPK, E]), ALU.is_equal))
                    step(V.tensor_tensor(q, q, gates.rearrange("p (a n) -> p a n", a=1).broadcast_to([P, TOPK, E]), ALU.mult))
                    step(V.tensor_reduce(gk[:, i, 0:TOPK], q, AX.X, ALU.add))
                    V.tensor_copy(meta[:, i, :, 0], c_("tok").broadcast_to([P, E]))
                    V.memset(meta[:, i, :, 1], float(i))
                    V.tensor_scalar(meta[:, i, :, 2], incl, -1.0, None, ALU.add)
                    V.memset(meta[:, i, :, 3], 1.0)
                    step(V.tensor_copy(mask_bf[:, i, :], mask[:, i, :]))
                    V.tensor_copy(small8[:, 5, 0:1], small8[:, 4, 0:1]).then_inc(ms["mask_ready"], 1)
                    dve.wait_ge(ms["mask_ready"], sent(ms["mask_ready"]))
                seen(hT_sum, 2)
                dve.wait_ge(ms["pos_sum"], seen(ms["pos_sum"]))
                step(V.scalar_tensor_tensor(posm[:, 0:nt, :], pb[:, 0, 0:nt * E].rearrange("p (i e) -> p i e", i=nt), 1.0, mask[:, 0:nt, :], ALU.add, ALU.mult))
                step(V.tensor_scalar(posm[:, 0:nt, :], posm[:, 0:nt, :], -1.0, None, ALU.add))
                step(V.tensor_reduce(cntf, pb[:, 0, nt * E:(nt + 1) * E], AX.X, ALU.max))
                V.tensor_copy(cnti, cntf).then_inc(ms["count_ready"], 1)
                end_phase(dve, "dve")

                def slots(b, ready, step):
                    if b > 0:
                        step(V.tensor_copy(iota_e, iota[:, 0:CAP].rearrange("p (s a) -> p s a", a=1).broadcast_to([P, CAP, E])))
                    step(V.tensor_scalar(posb[:, 0:nt, :], posm[:, 0:nt, :], -float(b * ROWS[l]), -1.0, ALU.add, ALU.max))
                    step(V.tensor_scalar(posb_bf[:, 0:nt, :], posb[:, 0:nt, :], float(P), None, ALU.min))
                    for i in range(nt):
                        last = V.tensor_tensor(onehot[:, i], iota_e, posb_bf[:, i:i + 1, :].broadcast_to([P, CAP, E]), ALU.is_equal)
                    last.then_inc(ready, 1)

                def index_tables(step):
                    t = pb[:, 0, 0:4 * E].rearrange("p (e c) -> p e c", c=4)
                    V.tensor_scalar(tabf[:, 0, :], t[:, :, 1], float(P), None, ALU.mult)
                    step(V.tensor_scalar(tabf[:, 1, :], t[:, :, 3], -OUT_OF_RANGE, OUT_OF_RANGE, ALU.mult, ALU.add))
                    step(V.tensor_tensor(tabf[:, 0, :], t[:, :, 0], tabf[:, 0, :], ALU.add))
                    step(V.scalar_tensor_tensor(tabf[:, 2, :], tabf[:, 0, :], float(TOPK), tabf[:, 1, :], ALU.mult, ALU.add))
                    step(V.tensor_tensor(tabf[:, 2, :], t[:, :, 2], tabf[:, 2, :], ALU.add))
                    step(V.tensor_tensor(tabf[:, 0, :], tabf[:, 0, :], tabf[:, 1, :], ALU.add))
                    V.tensor_copy(gi, tabf[:, 0, :])
                    return V.tensor_copy(si, tabf[:, 2, :])

                dve.wait_ge(ms["iota_ready"], seen(ms["iota_ready"]))
                slots(0, ms["onehot_ready"], step)
                dve.wait_ge(ms["tab_sum"], seen(ms["tab_sum"]))
                V.memset(gx, 0.0)
                step(index_tables(step))
                end_phase(dve, "dve")

                def dve_walk(S, base):
                    def rows(it, j, n, waits):
                        dve.wait_ge(S.dn_sum, n + 1)
                        if waits:
                            dve.wait_ge(S.y_out[j % 4], 16 * (it + base // 4 + j // 4))
                        V.tensor_copy(yx[:, j % 4], pb[:, 5:7, :].rearrange("p b n -> p (b n)")).then_inc(S.y_ready, 1)

                    def body(it, first, last_):
                        for j in range(4):
                            n = it * 4 + j + base
                            dve.wait_ge(S.sg_ready, n + 1)
                            if not (first and j < 2):
                                dve.wait_ge(S.aT_sum, n - 1)
                            V.tensor_tensor(actx[:, j % 2].rearrange("p (k q) -> p q k", k=2), sg[:, j % 2].rearrange("p (q k) -> p q k", k=2),
                                            pb[:, 2 + j % 2, FF:2 * FF].rearrange("p (q k) -> p q k", k=2), ALU.mult).then_inc(S.act_ready, 1)
                            if not (first and j == 0):
                                rows(it, j - 1, n - 1, not first)
                            dve.wait_ge(S.aT_sum, n + 1)
                            if not (first and j < 2):
                                dve.wait_ge(S.dn_sum, n - 1)
                            V.tensor_copy(aT[:, j % 2].rearrange("p k t -> p (k t)"), pb[:, 4, 0:2 * P]).then_inc(S.aT_ready, 1)
                    walk(dve, body)
                    rows(E // 4 - 1, 3, base + E - 1, True)

                dve_walk(main, E * l)
                end_phase(dve, "dve")
                dve.wait_ge(ms["count_ready"], l + 1)
                most = dve.value_load(cnti[0:1, 0:1], min_val=0, max_val=NT * P)
                with dve.If(most > ROWS[l]):
                    xstep = lambda ins: link(dve, ins, x_step[l])
                    for b in range(1, blocks(l)):
                        if b > 1:
                            dve.wait_ge(x_chain[l], x_at(b, 0) - X_TAB)
                        slots(b, x_chain[l], xstep)
                        dve.wait_ge(x_chain[l], x_at(b, 0) - 1)
                        xstep(index_tables(xstep))
                        dve.engine_nop().then_inc(x_chain[l], 1)
                        with dve.Fori(0, E) as e:
                            dve.wait_ge(x_chain[l], x_at(b, e, X_SILU))
                            V.tensor_tensor(actx[:, 0].rearrange("p (k q) -> p q k", k=2), sg[:, 0].rearrange("p (q k) -> p q k", k=2),
                                            pb[:, 2, FF:2 * FF].rearrange("p (q k) -> p q k", k=2), ALU.mult).then_inc(x_chain[l], 1)
                            dve.wait_ge(x_chain[l], x_at(b, e, X_AT))
                            V.tensor_copy(aT[:, 0].rearrange("p k t -> p (k t)"), pb[:, 4, 0:2 * P]).then_inc(x_chain[l], 1)
                            dve.wait_ge(x_chain[l], x_at(b, e, X_DN))
                            V.tensor_copy(yx[:, 0], pb[:, 5:7, :].rearrange("p b n -> p (b n)")).then_inc(x_chain[l], 1)
                end_phase(dve, "dve")
                if l == DEPTH - 1:
                    dve.wait_ge(f_in[0], seen(f_in[0], 16))
                    for i in range(nt):
                        combine(l, i)
                    end_phase(dve, "dve")

        @block.gpsimd
        def _(pool):
            seen = Seen()

            def roots(n, cols=8):
                for _ in range(n):
                    pool.wait_ge(root_in, seen(root_in))
                    nc.gpsimd.tensor_tensor(root[:, 0:cols], root[:, 0:cols], minus_half[:, 0:cols], ALU.pow).then_inc(root_out, 1)

            for l in range(DEPTH):
                roots(NT)
                end_phase(pool, "pool")
                nc.gpsimd.memset(rb["loraW"], 0.0).then_inc(rs["zero"], 1)
                roots(NT)
                end_phase(pool, "pool")
                roots(NT)
                roots(1, 16)
                roots(len(tiles_of(l)))
                roots(len(tiles_of(l)))
                end_phase(pool, "pool")
                end_phase(pool, "pool")

                def row_walk(S, base):
                    def gather(e, n, j):
                        nc.gpsimd.tensor_copy(idx_now[:, j:j + 1], gi[:, bass.ds(e, 1)]).then_inc(S.gather_idx, 1)
                        pool.wait_ge(S.gather_idx, n + 1)
                        pool.sem_inc(wait_held, 1)
                        nc.gpsimd.indirect_dma_start(gx[0:ROWS[l], j, :], None, h_dram, bass.IndirectOffsetOnAxis(ap=idx_now[0:ROWS[l], j:j + 1], axis=0),
                                                     bounds_check=NT * P - 1, oob_is_err=False).then_inc(S.g_in[j], 16)

                    def body(it, first, last_):
                        if first:
                            for a in range(4):
                                gather(a, base + a, a)
                        for j in range(4):
                            e = it * 4 + j
                            n = e + base
                            if not last_:
                                pool.wait_ge(S.gT_sum, n + 1)
                                gather(e + 4, n + 4, j)
                            pool.wait_ge(S.y_ready, n + 1)
                            sl = idx_now[:, 4 + j:5 + j]
                            if not first:
                                pool.wait_ge(S.y_out[j], 16 * (base // 4 + it))
                            nc.gpsimd.tensor_copy(sl, si[:, bass.ds(e, 1)]).then_inc(S.scatter_idx, 1)
                            pool.wait_ge(S.scatter_idx, n + 1)
                            pool.sem_inc(wait_held, 1)
                            nc.gpsimd.indirect_dma_start(y_dram, bass.IndirectOffsetOnAxis(ap=sl[0:ROWS[l], :], axis=0), yx[0:ROWS[l], j, :], None,
                                                         bounds_check=NT * P * TOPK - 1, oob_is_err=False).then_inc(S.y_out[j], 16)
                    walk(pool, body)
                    for j in range(4):
                        pool.wait_ge(S.y_out[j], 16 * (base // 4 + E // 4))

                row_walk(main, E * l)
                end_phase(pool, "pool")
                pool.wait_ge(ms["count_ready"], l + 1)
                most = pool.value_load(cnti[0:1, 0:1], min_val=0, max_val=NT * P)
                with pool.If(most > ROWS[l]):
                    for b in range(1, blocks(l)):
                        with pool.Fori(0, E) as e:
                            pool.wait_ge(x_chain[l], x_at(b, e))
                            nc.gpsimd.tensor_copy(idx_now[:, 0:1], gi[:, bass.ds(e, 1)]).then_inc(x_chain[l], 1)
                            pool.wait_ge(x_chain[l], x_at(b, e, X_IDX))
                            pool.sem_inc(wait_held, 1)
                            nc.gpsimd.indirect_dma_start(gx[0:ROWS[l], 0, :], None, h_dram, bass.IndirectOffsetOnAxis(ap=idx_now[0:ROWS[l], 0:1], axis=0),
                                                         bounds_check=NT * P - 1, oob_is_err=False).then_inc(x_rows[l], 16)
                            pool.wait_ge(x_chain[l], x_at(b, e, X_Y))
                            nc.gpsimd.tensor_copy(idx_now[:, 1:2], si[:, bass.ds(e, 1)]).then_inc(x_chain[l], 1)
                            pool.wait_ge(x_chain[l], x_at(b, e, X_SIDX))
                            pool.sem_inc(wait_held, 1)
                            nc.gpsimd.indirect_dma_start(y_dram, bass.IndirectOffsetOnAxis(ap=idx_now[0:ROWS[l], 1:2], axis=0), yx[0:ROWS[l], 0, :], None,
                                                         bounds_check=NT * P * TOPK - 1, oob_is_err=False).then_inc(x_out[l], 16)
                            pool.wait_ge(x_out[l], 16 * ((b - 1) * E + e + 1))
                            pool.sem_inc(x_chain[l], 1)
                end_phase(pool, "pool")
                roots(len(tiles_of(l)))
                if l == DEPTH - 1:
                    end_phase(pool, "pool")



_INS = ['x', 'c', 'ctx', 'c_ctx', 'ada_w', 'ada_b', 'pre_mix_g', 'post_mix_g', 'pre_ffn_g', 'post_ffn_g', 'w_in', 'w_out',
        'mla_q_norm', 'mla_w_q_b', 'mla_kv_norm', 'mla_w_kv_b', 'pool_w', 'pool_scale', 'rwkv_mu', 'rwkv_w0', 'rwkv_w2',
        'rwkv_a0', 'rwkv_a2', 'rwkv_g2', 'rwkv_k_k', 'rwkv_k_a', 'rwkv_r_k', 'rwkv_ln_w', 'rwkv_ln_b', 'router_w',
        'router_bias', 'exp_w_gate', 'exp_w_up', 'exp_w_down', 'sh_w_gate', 'sh_w_up', 'sh_w_down']


def kernel(**inputs):
    import numpy as _np
    import concourse.bacc as _bacc
    from concourse import mybir as _mybir
    from concourse.bass_utils import run_bass_kernel_spmd as _run

    nc = _bacc.Bacc("TRN2", target_bir_lowering=False, num_devices=1)
    arrays, args = {}, {}
    const, _, pool = lay_constants()
    for name, a in [(n, inputs[n]) for n in _INS] + [("shape_consts", const), ("pool_matrix", pool)]:
        a = _np.ascontiguousarray(a)
        arrays[f"in_{name}_dram"] = a
        args[name] = nc.dram_tensor(f"in_{name}_dram", a.shape, _mybir.dt.from_np(a.dtype), kind="ExternalInput").ap()
    out = nc.dram_tensor("out_0_dram", (1, SEQ, D), _mybir.dt.float32, kind="ExternalOutput").ap()
    trunk_kernel(nc, args, out)
    r = _run(nc, [arrays], core_ids=[0])
    return r.results[0]["out_0_dram"]
```
